# Optimizing a Trainium2 kernel written in Bass

```python
import jax, jax.numpy as jnp
from jax import lax
import numpy as np

D_MODEL = 1024
BATCH = 1
SEQ = 256
DEPTH = 2
DEC_BATCH = 8
DEC_SEQ = 1
PAST_LEN = 2048
PAGE_SIZE = 128

N_A_LAYERS = DEPTH // 2
N_B_LAYERS = DEPTH - N_A_LAYERS
N_DENSE = (DEPTH + 1) // 2
N_MOE = DEPTH // 2
POOL_WINDOWS = (2, 4, 8, 16)
N_POOL_GROUPS = len(POOL_WINDOWS)
POOL_GROUP = D_MODEL // N_POOL_GROUPS
POOL_STATE = max(POOL_WINDOWS) - 1
ATTN_GROUPS = ((128, 1), (512, 4), (2048, 16))
N_ATTN_GROUPS = len(ATTN_GROUPS)
N_KV_HEADS = 16
HEAD_DIM = D_MODEL // N_KV_HEADS
N_Q_HEADS = N_ATTN_GROUPS * N_KV_HEADS
MAX_WINDOW = max(w for w, _ in ATTN_GROUPS)
BLK = 128
ROPE_THETA = 10000.0
D_FF = 2816
N_EXPERTS = 8
TOP_K = 2
D_FF_EXPERT = 3584
EPS = 1e-6

kernel_name = "yoco_pool_dilated_attn_step"

def rms_norm(x, g):
    xf = x.astype(jnp.float32)
    y = xf * lax.rsqrt(jnp.mean(xf * xf, axis=-1, keepdims=True) + EPS)
    return (y * g.astype(jnp.float32)).astype(x.dtype)

def ada_mod(c, w, b):
    m = (jax.nn.silu(c) @ w + b).astype(jnp.float32)[:, None, :]
    return jnp.split(m, 3, axis=-1)

def rope(x, pos):
    half = HEAD_DIM // 2
    inv = ROPE_THETA ** (-jnp.arange(half, dtype=jnp.float32) / half)
    ang = pos.astype(jnp.float32)[:, None] * inv[None, :]
    cos = jnp.cos(ang)[None, :, None, :]
    sin = jnp.sin(ang)[None, :, None, :]
    xf = x.astype(jnp.float32)
    x1, x2 = xf[..., :half], xf[..., half:]
    return jnp.concatenate([x1 * cos - x2 * sin, x2 * cos + x1 * sin], axis=-1).astype(x.dtype)

def multiscale_pool(u, prev, pos, w_grp, ls):
    B, T, D = u.shape
    ext = jnp.concatenate([prev.astype(u.dtype), u], axis=1)
    cs = jnp.cumsum(ext.astype(jnp.float32), axis=1)
    cs = jnp.concatenate([jnp.zeros((B, 1, D), jnp.float32), cs], axis=1)
    cs = cs.reshape(B, POOL_STATE + T + 1, N_POOL_GROUPS, POOL_GROUP)
    win = jnp.array(POOL_WINDOWS, dtype=jnp.int32)
    end = POOL_STATE + 1 + jnp.arange(T, dtype=jnp.int32)
    lo_idx = end[:, None] - win[None, :]
    hi = cs[:, end]
    lo = cs[:, lo_idx, jnp.arange(N_POOL_GROUPS)[None, :]]
    cnt = jnp.minimum(win[None, :], pos[:, None] + 1).astype(jnp.float32)
    mean = (hi - lo) / cnt[None, :, :, None]
    tok = ext[:, POOL_STATE:].astype(jnp.float32).reshape(B, T, N_POOL_GROUPS, POOL_GROUP)
    y = jnp.einsum('btgc,gcd->btgd', mean - tok, w_grp.astype(jnp.float32))
    y = y.reshape(B, T, D) * ls.astype(jnp.float32)
    return y.astype(u.dtype), ext[:, -POOL_STATE:]

def dilated_group_prompt(q, k, v, dil, span):
    B, T, H, hd = q.shape
    step = dil * BLK
    Tp = -(-T // step) * step
    nb = Tp // step
    pad = ((0, 0), (0, Tp - T), (0, 0), (0, 0))

    def split(a):
        a = jnp.pad(a, pad).reshape(B, Tp // dil, dil, H, hd).transpose(0, 2, 1, 3, 4)
        return a.reshape(B, dil, nb, BLK, H, hd)

    def with_prev(a):
        prev = jnp.pad(a, ((0, 0), (0, 0), (1, 0), (0, 0), (0, 0), (0, 0)))[:, :, :-1]
        return jnp.concatenate([prev, a], axis=3)

    qb = split(q)
    kc = with_prev(split(k))
    vc = with_prev(split(v))
    s = jnp.einsum('brnqhd,brnkhd->brnhqk', qb, kc,
                   preferred_element_type=jnp.float32) * (HEAD_DIM ** -0.5)
    i = jnp.arange(BLK)[:, None]
    j = jnp.arange(2 * BLK)[None, :]
    dist = i + BLK - j
    band = (dist >= 0) & (dist <= span)
    has_prev = (jnp.arange(nb)[:, None, None] > 0) | (j >= BLK)[None]
    mask = band[None] & has_prev
    s = jnp.where(mask[None, None, :, None], s, -jnp.inf)
    m = jnp.max(s, axis=-1, keepdims=True)
    p = jnp.exp(s - m)
    den = jnp.sum(p, axis=-1, keepdims=True)
    o = jnp.einsum('brnhqk,brnkhd->brnqhd', p, vc.astype(jnp.float32))
    o = o / jnp.swapaxes(den, 3, 4)
    lse = jnp.swapaxes((m + jnp.log(den))[..., 0], 3, 4)
    o = o.reshape(B, dil, Tp // dil, H, hd).transpose(0, 2, 1, 3, 4).reshape(B, Tp, H, hd)[:, :T]
    lse = lse.reshape(B, dil, Tp // dil, H).transpose(0, 2, 1, 3).reshape(B, Tp, H)[:, :T]
    return o, lse

def dilated_group_sample(q, k_all, v_all, n_past, dil, span):
    S = q.shape[1]
    idx = n_past + jnp.arange(S)[:, None] - dil * jnp.arange(span + 1)[None, :]
    valid = idx >= 0
    idx_c = jnp.maximum(idx, 0)
    kg = k_all[:, idx_c]
    vg = v_all[:, idx_c]
    s = jnp.einsum('bshd,bskhd->bshk', q, kg,
                   preferred_element_type=jnp.float32) * (HEAD_DIM ** -0.5)
    s = jnp.where(valid[None, :, None, :], s, -jnp.inf)
    m = jnp.max(s, axis=-1, keepdims=True)
    p = jnp.exp(s - m)
    den = jnp.sum(p, axis=-1, keepdims=True)
    o = jnp.einsum('bshk,bskhd->bshd', p, vg.astype(jnp.float32)) / den
    return o, (m + jnp.log(den))[..., 0]

def dilated_attention(h, pos, k_all, v_all, n_past, w_q, w_o, prompt):
    B, T, _ = h.shape
    q = (h @ w_q).reshape(B, T, N_Q_HEADS, HEAD_DIM)
    q = rope(q, pos).reshape(B, T, N_ATTN_GROUPS, N_KV_HEADS, HEAD_DIM)
    outs, lses = [], []
    for g, (win, dil) in enumerate(ATTN_GROUPS):
        span = win // dil
        if prompt:
            o, l = dilated_group_prompt(q[:, :, g], k_all, v_all, dil, span)
        else:
            o, l = dilated_group_sample(q[:, :, g], k_all, v_all, n_past, dil, span)
        outs.append(o)
        lses.append(l)
    alpha = jax.nn.softmax(jnp.stack(lses, axis=0), axis=0)
    o = jnp.sum(alpha[..., None] * jnp.stack(outs, axis=0), axis=0)
    return o.reshape(B, T, N_KV_HEADS * HEAD_DIM).astype(h.dtype) @ w_o

def swiglu(h, w1, w3, w2):
    return (jax.nn.silu(h @ w1) * (h @ w3)) @ w2

def moe_swiglu(h, w_router, b_router, w1, w3, w2):
    logits = (h @ w_router).astype(jnp.float32) + b_router.astype(jnp.float32)
    top_v, top_i = lax.top_k(logits, TOP_K)
    gates = jax.nn.softmax(top_v, axis=-1)
    dense_gate = jnp.sum(jax.nn.one_hot(top_i, N_EXPERTS, dtype=jnp.float32) * gates[..., None], axis=-2)
    out = jnp.zeros(h.shape, jnp.float32)
    for e in range(N_EXPERTS):
        y = swiglu(h, w1[e], w3[e], w2[e]).astype(jnp.float32)
        out = out + dense_gate[..., e:e + 1] * y
    return out.astype(h.dtype)

def run_trunk(x, c, pos0, pool_prev, k_past, v_past, prompt,
              ada_mix_w, ada_mix_b, g_pre_mix, g_post_mix, pool_w, pool_scale,
              g_kv, w_kv, w_q, w_o, ada_ffn_w, ada_ffn_b, g_pre_ffn, g_post_ffn,
              ffn_w1, ffn_w3, ffn_w2, router_w, router_b, moe_w1, moe_w3, moe_w2):
    T = x.shape[1]
    pos = pos0 + jnp.arange(T, dtype=jnp.int32)
    kv_width = N_KV_HEADS * HEAD_DIM
    new_pool = []
    k_all = v_all = k_new = v_new = None
    n_past = 0
    for layer in range(DEPTH):
        sh, sc, gt = ada_mod(c, ada_mix_w[layer], ada_mix_b[layer])
        hm = (rms_norm(x, g_pre_mix[layer]) * (1.0 + sc) + sh).astype(x.dtype)
        if layer < N_A_LAYERS:
            a = layer
            mix, st = multiscale_pool(hm, pool_prev[:, a], pos, pool_w[a], pool_scale[a])
            new_pool.append(st)
        else:
            b = layer - N_A_LAYERS
            mix = dilated_attention(hm, pos, k_all, v_all, n_past, w_q[b], w_o[b], prompt)
        x = x + (gt * rms_norm(mix, g_post_mix[layer])).astype(x.dtype)
        sh, sc, gt = ada_mod(c, ada_ffn_w[layer], ada_ffn_b[layer])
        hf = (rms_norm(x, g_pre_ffn[layer]) * (1.0 + sc) + sh).astype(x.dtype)
        if layer % 2 == 0:
            i = layer // 2
            f = swiglu(hf, ffn_w1[i], ffn_w3[i], ffn_w2[i])
        else:
            i = layer // 2
            f = moe_swiglu(hf, router_w[i], router_b[i], moe_w1[i], moe_w3[i], moe_w2[i])
        x = x + (gt * rms_norm(f, g_post_ffn[layer])).astype(x.dtype)
        if layer == N_A_LAYERS - 1:
            kv = rms_norm(x, g_kv) @ w_kv
            B = x.shape[0]
            k_new = rope(kv[..., :kv_width].reshape(B, T, N_KV_HEADS, HEAD_DIM), pos)
            v_new = kv[..., kv_width:].reshape(B, T, N_KV_HEADS, HEAD_DIM)
            if prompt:
                k_all, v_all, n_past = k_new, v_new, 0
            else:
                n_past = k_past.shape[1]
                k_all = jnp.concatenate([k_past.astype(k_new.dtype), k_new], axis=1)
                v_all = jnp.concatenate([v_past.astype(v_new.dtype), v_new], axis=1)
    pool_state = jnp.stack(new_pool, axis=1)
    if prompt:
        n_keep = min(MAX_WINDOW, T)
        k_new, v_new = k_new[:, T - n_keep:], v_new[:, T - n_keep:]
    return x, pool_state, k_new, v_new

def setup_inputs(seed: int = 0) -> dict:
    key = jax.random.key(seed)
    ks = iter(jax.random.split(key, 48))
    D = D_MODEL

    def nrm(shape, scale=1.0):
        return scale * jax.random.normal(next(ks), shape, jnp.float32)

    def gain(shape):
        return 1.0 + 0.05 * nrm(shape)

    kv_buf = min(MAX_WINDOW, PAST_LEN)
    kv_width = N_KV_HEADS * HEAD_DIM
    return {
        "x_prompt": nrm((BATCH, SEQ, D)),
        "x_sample": nrm((DEC_BATCH, DEC_SEQ, D)),
        "state_pool": nrm((DEC_BATCH, N_A_LAYERS, POOL_STATE, D)),
        "cache_k": nrm((DEC_BATCH, kv_buf, N_KV_HEADS, HEAD_DIM)),
        "cache_v": nrm((DEC_BATCH, kv_buf, N_KV_HEADS, HEAD_DIM)),
        "c_prompt": nrm((BATCH, D)),
        "c_sample": nrm((DEC_BATCH, D)),
        "ada_mix_w": nrm((DEPTH, D, 3 * D), 0.5 * D ** -0.5),
        "ada_mix_b": nrm((DEPTH, 3 * D), 0.02),
        "g_pre_mix": gain((DEPTH, D)),
        "g_post_mix": gain((DEPTH, D)),
        "pool_w": nrm((N_A_LAYERS, N_POOL_GROUPS, POOL_GROUP, POOL_GROUP), POOL_GROUP ** -0.5),
        "pool_scale": 1.0 + 0.1 * nrm((N_A_LAYERS, D)),
        "g_kv": gain((D,)),
        "w_kv": nrm((D, 2 * kv_width), D ** -0.5),
        "w_q": nrm((N_B_LAYERS, D, N_Q_HEADS * HEAD_DIM), D ** -0.5),
        "w_o": nrm((N_B_LAYERS, kv_width, D), kv_width ** -0.5),
        "ada_ffn_w": nrm((DEPTH, D, 3 * D), 0.5 * D ** -0.5),
        "ada_ffn_b": nrm((DEPTH, 3 * D), 0.02),
        "g_pre_ffn": gain((DEPTH, D)),
        "g_post_ffn": gain((DEPTH, D)),
        "ffn_w1": nrm((N_DENSE, D, D_FF), D ** -0.5),
        "ffn_w3": nrm((N_DENSE, D, D_FF), D ** -0.5),
        "ffn_w2": nrm((N_DENSE, D_FF, D), D_FF ** -0.5),
        "router_w": nrm((N_MOE, D, N_EXPERTS), D ** -0.5),
        "router_b": nrm((N_MOE, N_EXPERTS), 0.01),
        "moe_w1": nrm((N_MOE, N_EXPERTS, D, D_FF_EXPERT), D ** -0.5),
        "moe_w3": nrm((N_MOE, N_EXPERTS, D, D_FF_EXPERT), D ** -0.5),
        "moe_w2": nrm((N_MOE, N_EXPERTS, D_FF_EXPERT, D), D_FF_EXPERT ** -0.5),
    }

def reference(x_prompt, x_sample, state_pool, cache_k, cache_v, c_prompt, c_sample,
              ada_mix_w, ada_mix_b, g_pre_mix, g_post_mix, pool_w, pool_scale,
              g_kv, w_kv, w_q, w_o, ada_ffn_w, ada_ffn_b, g_pre_ffn, g_post_ffn,
              ffn_w1, ffn_w3, ffn_w2, router_w, router_b, moe_w1, moe_w3, moe_w2):
    params = (ada_mix_w, ada_mix_b, g_pre_mix, g_post_mix, pool_w, pool_scale,
              g_kv, w_kv, w_q, w_o, ada_ffn_w, ada_ffn_b, g_pre_ffn, g_post_ffn,
              ffn_w1, ffn_w3, ffn_w2, router_w, router_b, moe_w1, moe_w3, moe_w2)
    pool_zero = jnp.zeros((x_prompt.shape[0], N_A_LAYERS, POOL_STATE, D_MODEL), x_prompt.dtype)
    y_prompt, pool_prompt, k_prompt, v_prompt = run_trunk(
        x_prompt, c_prompt, 0, pool_zero, None, None, True, *params)
    y_sample, pool_sample, k_sample, v_sample = run_trunk(
        x_sample, c_sample, PAST_LEN, state_pool, cache_k, cache_v, False, *params)
    return (y_prompt, y_sample, pool_prompt, pool_sample, k_prompt, v_prompt, k_sample, v_sample)


_drawn_inputs = setup_inputs


def setup_inputs(seed=0):
    import zlib

    import numpy as np

    out = dict(_drawn_inputs(seed))
    spreads = {}
    factors = {'router_b': 3.006}
    for name, (base, spread) in spreads.items():
        noise = np.random.default_rng([zlib.crc32(name.encode()), seed]).standard_normal(out[name].shape)
        drawn = base * np.exp(spread * noise) if base else spread * noise
        out[name] = __import__('jax').numpy.asarray(drawn.astype(out[name].dtype))
    for name, factor in factors.items():
        out[name] = (out[name] * factor).astype(out[name].dtype)
    return out
```

```python
from contextlib import ExitStack

import concourse.bass as bass
from concourse import mybir

F32 = mybir.dt.float32
I32 = mybir.dt.int32
ALU = mybir.AluOpType
ACT = mybir.ActivationFunctionType
X = mybir.AxisListType.X

P = 128
D = 1024
KC = D // P
T = 256
NB = 8
NT = T + NB
PAST = 2048
GROUPS = ((128, 1), (512, 4), (2048, 16))
NG = len(GROUPS)
H, HD = 16, 64
WIN = (2, 4, 8, 16)
STATE = 15
FF = 2816
FB = FF // P
NE = 8
FE = 3584
FCH = FE // 512
EPS = 1e-6
SCALE = HD ** -0.5
RING = 7
SLAB = 4096
SLOTS = 128
PASSES = -(-NT // SLOTS)
NEG = -1e30

CONST = {}


def _lay():
    at = 0
    for name, n in (("cos", NT), ("sin", NT), ("mask", NG * 256), ("cnt", 4 * 16), ("ident", P), ("rot", P),
                    ("before", P), ("ones", P), ("iota", SLOTS * PASSES), ("tri", NE * NE), ("eps", 1)):
        CONST[name] = (at, at + n)
        at += n
    return at


NCONST = _lay()


def slab_plan():
    plan = []

    def cols(name, k, rows, ncols, step=512):
        for c in range(0, ncols, step):
            plan.append((name, k, 0, rows, c, min(step, ncols - c)))

    cols("ada", 0, KC, 3 * D)
    cols("ada", 1, KC, 3 * D)
    for c in range(0, FF, 512):
        plan.append(("w1", 0, 0, KC, c, min(512, FF - c)))
        plan.append(("w3", 0, 0, KC, c, min(512, FF - c)))
    for c in range(0, D, 512):
        for r in range(0, FB, 8):
            plan.append(("w2", 0, r, min(8, FB - r), c, 512))
    cols("ada", 2, KC, 3 * D)
    cols("wkv", 0, KC, 2 * D)
    cols("wq", 0, KC, NG * D)
    for b in range(NB):
        plan.append(("ck", b, 0, NG, 0, D))
    for b in range(NB):
        plan.append(("cv", b, 0, NG, 0, D))
    cols("wo", 0, KC, D)
    cols("ada", 3, KC, 3 * D)
    return plan


def yoco_step(nc, w, o):
    plan = slab_plan()
    first = {}
    for n, item in enumerate(plan):
        first.setdefault(item[:2], n)
    NPRE = len(plan)
    dmas = [NG if item[0] in ("ck", "cv") else 1 for item in plan]
    PER_E = 3 * FCH
    assert PER_E % RING == 0

    with ExitStack() as ctx:
        def sb(name, shape, dt=F32):
            return ctx.enter_context(nc.sbuf_tensor(name, shape, dt))

        def sem(name):
            return ctx.enter_context(nc.semaphore(name))

        bank = [ctx.enter_context(nc.psum_tensor(f"bank{i}", [P, 512], F32)) for i in range(8)]

        ring = sb("ring", [P, RING, SLAB])
        const = sb("const", [P, NCONST])

        def cst(name):
            a, b = CONST[name]
            return const[:, a:b]

        cos, sin, ident, rot, before, ones, iota = (cst(n) for n in ("cos", "sin", "ident", "rot", "before", "ones", "iota"))
        one1 = ones[:, 0:1]
        eps1 = cst("eps")
        mask = cst("mask").rearrange("p (g k) -> p g k", g=NG)
        invcnt = cst("cnt").rearrange("p (g k) -> p g k", g=4)
        tri = cst("tri").rearrange("p (a b) -> p a b", a=NE)

        xT = sb("xT", [P, KC, NT])
        hT = sb("hT", [P, KC, NT])
        mT = sb("mT", [P, KC, NT])
        tT = sb("tT", [P, KC, NT])
        ada = sb("ada", [P, 4, 24, 1 + NB])
        vec1 = sb("vec1", [P, 96])
        vec2 = sb("vec2", [P, 80])
        vrow1 = sb("vrow1", [96, P])
        vrow2 = sb("vrow2", [80, P])
        cT = sb("cT", [P, KC, 1 + NB])
        std = sb("std", [P, NT])
        rstd = sb("rstd", [P, NT])
        small = sb("small", [P, KC, NB])
        rw = sb("rw", [P, KC, NE])
        rb = sb("rb", [1, NE])
        flag = sb("flag", [P, 1], I32)
        PHASE = 11600
        phase = sb("phase", [P, PHASE])
        places = {}

        def at(offset, *shape):
            n = 1
            for s in shape:
                n *= s
            assert offset + n <= PHASE, (offset, shape)
            v = phase[:, offset:offset + n]
            if len(shape) == 2:
                v = v.rearrange("p (a b) -> p a b", a=shape[0])
            if len(shape) == 3:
                v = v.rearrange("p (a b c) -> p a b c", a=shape[0], b=shape[1])
            if len(shape) == 4:
                v = v.rearrange("p (a b c d) -> p a b c d", a=shape[0], b=shape[1], c=shape[2])
            return v

        EXT = STATE + T
        xtok = at(0, 3, D)
        crow = at(3072, D)
        strow = at(4096, D)
        ext = at(5120, KC, EXT)
        sExt = at(5120 + KC * EXT, KC, NB, STATE + 1)
        sum_a = at(0, KC, EXT)
        sum_b = at(KC * EXT, KC, EXT)
        ext = at(2 * KC * EXT, KC, EXT)
        sExt = at(3 * KC * EXT, KC, NB, STATE + 1)
        poolw = at(3 * KC * EXT + KC * NB * (STATE + 1), 4, 2, 256)
        pstate = at(0, D)
        gT = at(0, FB, NT)
        silu_up = at(FB * NT, 2, NT)
        kT = at(0, KC, NT)
        vtok = at(KC * NT, 2, D)
        vnew = at(KC * NT + 2 * D, KC, NB)
        qT = at(KC * NT + 2 * D + KC * NB, NG * KC, NT)
        ktok = qT.rearrange("p a b -> p (a b)")[:, 0:3 * D].rearrange("p (a b) -> p a b", a=3)
        vntok = qT.rearrange("p a b -> p (a b)")[0:NB, 3 * D:4 * D]
        rawT = tT
        QEND = KC * NT + 2 * D + KC * NB + NG * KC * NT
        hflat = hT[:, :, :].rearrange("p a b -> p (a b)")
        tflat = tT[:, :, :].rearrange("p a b -> p (a b)")
        qpair = hflat[:, 0:384].rearrange("p (g b j s) -> p g b j s", g=NG, b=NB, j=KC)
        kprod = hflat[:, 384:768].rearrange("p (g b j s) -> p g b j s", g=NG, b=NB, j=KC)
        s_scores = hflat[:, 768:1152].rearrange("p (g n) -> p g n", g=NG)
        s_soft = hflat[:, 1152:1152 + 387]
        s_pT = hflat[:, 1540:1924].rearrange("p (g n) -> p g n", g=NG)
        pnewb = hflat[:, 1924:1924 + P]
        s_stat = hflat[:, 2060:2064]
        kTs = tflat[:, 0:2048].rearrange("p (a b) -> p a b", a=2)
        otok = hflat[:, 0:2048].rearrange("p (c n) -> p c n", c=2)
        sm = [tflat[:, 768 * i:768 * (i + 1)].rearrange("p (g k) -> p g k", g=NG) for i in range(2)]
        rot_a, rot_b = at(QEND, NT), at(QEND + NT, NT)
        p_sum = at(QEND, 256)
        p_stat = at(QEND + 256, 4, 4)
        p_T = at(QEND + 272, 2, P)
        htok = at(0, 3, D)
        xeT = at(3072, KC, SLOTS)
        up_s = at(4096, 512)
        up = at(4608, 512)
        upT = at(5120, 4, P)
        ye = at(5632, D)
        disp = at(6656, 3, SLOTS)
        dispg = at(7040, 3, SLOTS)
        comb = at(7424, NT)
        lg = at(7688, 3, NE)
        sel = at(7712, 3, NE)
        posm = at(7736, 3, NE)
        gate = at(7760, 3, NE)
        r_a = at(7784, NE, NE)
        r_b = at(7848, NE, NE)
        r_c = at(7912, 3, NE)
        r_s = at(7936, 3, 4)
        ytok = at(0, 3, D)

        slab_in = [sem(f"slab_in{i}") for i in range(RING)]
        slab_used = sem("slab_used")
        in_const, in_vec, in_x, in_state, in_pool, in_router = (sem(n) for n in (
            "in_const", "in_vec", "in_x", "in_state", "in_pool", "in_router"))
        act_step, dve_step, pool_step = sem("act_step"), sem("dve_step"), sem("pool_step")
        vec_turned, vec_read = sem("vec_turned"), sem("vec_read")
        c_silu, c_turned, c_read = sem("c_silu"), sem("c_turned"), sem("c_read")
        x_turned, x_taken = sem("x_turned"), sem("x_taken")
        st_turned, st_taken = sem("st_turned"), sem("st_taken")
        ada_taken = sem("ada_taken")
        norm_in, sq_ready, norm_summed, std_ready = sem("norm_in"), sem("sq_ready"), sem("norm_summed"), sem("std_ready")
        h_ready = sem("h_ready")
        ext_ready, pm_ready, pool_summed, pool_taken = sem("ext_ready"), sem("pm_ready"), sem("pool_summed"), sem("pool_taken")
        ps_turned, ps_taken = sem("ps_turned"), sem("ps_taken")
        fup_summed, fup_silu, fup_done = sem("fup_summed"), sem("fup_silu"), sem("fup_done")
        fdn_summed, fdn_taken = sem("fdn_summed"), sem("fdn_taken")
        lin_summed, lin_raw, rot_summed, rot_done = sem("lin_summed"), sem("lin_raw"), sem("rot_summed"), sem("rot_done")
        kv_turned, kv_taken = sem("kv_turned"), sem("kv_taken")
        pair_ready = sem("pair_ready")
        kt_turned, kt_lo, kt_hi, s_summed, s_taken, s_turned = (sem(n) for n in (
            "kt_turned", "kt_lo", "kt_hi", "s_summed", "s_taken", "s_turned"))
        s_max, s_exp, s_prob, sp_turned, sp_taken, pn_ready, pn_spread, sv_summed, sv_done = (sem(n) for n in (
            "s_max", "s_exp", "s_prob", "sp_turned", "sp_taken", "pn_ready", "pn_spread", "sv_summed", "sv_done"))
        a_scored, a_max, a_exp, a_sum, a_turned, a_copied, a_out, a_taken = (sem(n) for n in (
            "a_scored", "a_max", "a_exp", "a_sum", "a_turned", "a_copied", "a_out", "a_taken"))
        ot_turned, ot_taken = sem("ot_turned"), sem("ot_taken")
        wo_summed, wo_taken = sem("wo_summed"), sem("wo_taken")
        lg_summed, lg_max, lg_exp, sel_ready, pos_summed = (sem(n) for n in (
            "lg_summed", "lg_max", "lg_exp", "sel_ready", "pos_summed"))
        ht_turned, ht_taken = sem("ht_turned"), sem("ht_taken")
        moe_ready, flag_ready = sem("moe_ready"), sem("flag_ready")
        route_built, gathered, xe0_copied, xe1_copied, comb_turned, comb_copied = (sem(n) for n in (
            "route_built", "gathered", "xe0_copied", "xe1_copied", "comb_turned", "comb_copied"))
        silu_done, up_ready, up_turned, upT_copied = (sem(n) for n in ("silu_done", "up_ready", "up_turned", "upT_copied"))
        y0_copied, y1_copied, c_summed, y_added = (sem(n) for n in ("y0_copied", "y1_copied", "c_summed", "y_added"))
        moe_done = sem("moe_done")
        y_turned, y_taken = sem("y_turned"), sem("y_taken")
        out_done = sem("out_done")
        kv_rows, ps_rows, y_rows = sem("kv_rows"), sem("ps_rows"), sem("y_rows")

        def slab_source(item):
            name, k, r, nr, c, ncol = item
            a = {"ada": lambda: (w["ada_mix_w"], w["ada_ffn_w"])[k % 2][k // 2], "w1": lambda: w["ffn_w1"][0],
                 "w3": lambda: w["ffn_w3"][0], "w2": lambda: w["ffn_w2"][0], "wkv": lambda: w["w_kv"],
                 "wq": lambda: w["w_q"][0], "wo": lambda: w["w_o"][0]}[name]()
            return a[r * P:(r + nr) * P, c:c + ncol].rearrange("(k p) n -> p k n", p=P)

        def slab_view(n):
            name, k, r, nr, c, ncol = plan[n]
            return ring[:, n % RING, 0:nr * ncol].rearrange("p (k n) -> p k n", k=nr)

        def slab_total(n):
            return 16 * sum(dmas[m] for m in range(n % RING, n + 1, RING))

        before_experts = [16 * sum(dmas[m] for m in range(r, NPRE, RING)) for r in range(RING)]

        eslabs = []
        for j in range(FCH):
            eslabs += [(1, j), (3, j)] + ([(2, j - 1)] if j else [])
        eslabs.append((2, FCH - 1))

        def expert_source(e, m, j):
            if m == 2:
                return w["moe_w2"][0, bass.ds(e, 1), 512 * j:512 * (j + 1), :].rearrange("a (k p) n -> p (a k) n", p=P)
            return w[f"moe_w{m}"][0, bass.ds(e, 1), :, 512 * j:512 * (j + 1)].rearrange("a (k p) n -> p (a k) n", p=P)

        def used_by(e, c, m, j):
            return e * PER_E + (NPRE + c * NE * PER_E + eslabs.index((m, j)) + 1)

        block = ctx.enter_context(nc.Block())

        @block.sync
        def _(sp):
            for n, item in enumerate(plan):
                if n >= RING:
                    sp.wait_ge(slab_used, n - RING + 1)
                if item[0] in ("ck", "cv"):
                    cache = w["cache_k" if item[0] == "ck" else "cache_v"]
                    for g, (_, dil) in enumerate(GROUPS):
                        sp.dma_start(slab_view(n)[:, g, :], cache[item[1], PAST - P * dil::dil].rearrange("t h d -> t (h d)"))\
                          .then_inc(slab_in[n % RING], 16)
                else:
                    sp.dma_start(slab_view(n), slab_source(item)).then_inc(slab_in[n % RING], 16)

            def experts(e, start):
                for k, (m, j) in enumerate(eslabs):
                    src, rows = expert_source(e, m, j), (4 if m == 2 else KC)
                    slot = (NPRE + k) % RING
                    sp.wait_ge(slab_used, e * PER_E + (start + k - RING + 1))
                    sp.dma_start(ring[:, slot, :].rearrange("p (k n) -> p k n", k=rows), src).then_inc(slab_in[slot], 16)

            with sp.Fori(0, NE) as e:
                experts(e, NPRE)
            sp.wait_ge(flag_ready, 1)
            over = sp.value_load(flag[0:1, 0:1], min_val=0, max_val=1)
            with sp.If(over > 0):
                for c in range(1, PASSES):
                    with sp.Fori(0, NE) as e:
                        experts(e, NPRE + c * NE * PER_E)

        @block.tensor
        def _(pe):
            def need_slab(n):
                pe.wait_ge(slab_in[n % RING], slab_total(n))

            pe.wait_ge(in_const, 16)
            pe.wait_ge(in_vec, 16 * 10)
            pe.transpose(bank[0][:, 0:96], vrow1[:, :], ident[0:96, 0:96])
            pe.transpose(bank[0][:, 96:176], vrow2[:, :], ident[0:80, 0:80]).then_inc(vec_turned, 1)
            pe.wait_ge(c_silu, 1)
            for k in range(KC):
                mm = pe.transpose(bank[1][:, 9 * k:9 * k + 9], crow[0:9, P * k:P * (k + 1)], ident[0:9, 0:9])
            mm.then_inc(c_turned, 1)
            pe.wait_ge(in_x, 32)
            for k in range(KC):
                if k >= 2:
                    pe.wait_ge(x_taken, k - 1)
                b = bank[2 + k % 2]
                for c, n in ((0, P), (1, P), (2, NB)):
                    mm = pe.transpose(b[:, c * P:c * P + n], xtok[0:n, c, P * k:P * (k + 1)], ident[0:n, 0:n])
                mm.then_inc(x_turned, 1)
            pe.wait_ge(in_state, 16)
            for k in range(KC):
                if k >= 2:
                    pe.wait_ge(st_taken, k - 1)
                pe.transpose(bank[4 + k % 2][:, 0:120], strow[0:120, P * k:P * (k + 1)], ident[0:120, 0:120])\
                  .then_inc(st_turned, 1)

            def ada_products(s, parts=range(6)):
                n0 = first[("ada", s)]
                for j in parts:
                    need_slab(n0 + j)
                    if s == 0 and j == 0:
                        pe.wait_ge(c_read, 1)
                    if s >= 1 and j == 0:
                        pe.wait_ge(ada_taken, s)
                    v = slab_view(n0 + j)
                    for m in range(4):
                        for k in range(KC):
                            mm = pe.matmul(bank[6][:, 9 * (4 * j + m):9 * (4 * j + m) + 9], v[:, k, P * m:P * (m + 1)],
                                           cT[:, k, :], start=(k == 0), stop=(k == KC - 1))
                    mm.then_inc(slab_used, 1)

            def norm_sum(i):
                pe.wait_ge(sq_ready, i + 1)
                for k in range(KC):
                    mm = pe.matmul(bank[7][:, 0:NT], ones, tT[:, k, :], start=(k == 0), stop=(k == KC - 1))
                mm.then_inc(norm_summed, 1)

            ada_products(0)
            norm_sum(0)
            ada_products(1)
            pe.wait_ge(in_pool, 16)
            pe.wait_ge(pm_ready, 1)
            for i in range(KC):
                g, m = i // 2, i % 2
                if i >= 2:
                    pe.wait_ge(pool_taken, i - 1)
                for k in range(2):
                    mm = pe.matmul(bank[2 + i % 2][:, 0:NT], poolw[:, g, k, P * m:P * (m + 1)], tT[:, 2 * g + k, :],
                                   start=(k == 0), stop=(k == 1))
                mm.then_inc(pool_summed, 1)
            for k in range(KC):
                mm = pe.transpose(bank[4 + k // 4][0:STATE + NB, P * (k % 4):P * (k % 4 + 1)], hT[:, k, T - STATE:NT], ident)
            mm.then_inc(ps_turned, 1)
            norm_sum(1)
            norm_sum(2)
            pe.wait_ge(h_ready, 2)
            n0 = first[("w1", 0)]
            for i in range(FB):
                for q in range(2):
                    n = n0 + 2 * (i // 4) + q
                    need_slab(n)
                    if i >= 2 and q == 0:
                        pe.wait_ge(fup_done, i - 1)
                    v = slab_view(n)
                    for k in range(KC):
                        mm = pe.matmul(bank[2 * q + i % 2][:, 0:NT], v[:, k, P * (i % 4):P * (i % 4 + 1)], hT[:, k, :],
                                       start=(k == 0), stop=(k == KC - 1))
                    mm.then_inc(fup_summed, 1)
                if i % 4 == 3 or i == FB - 1:
                    pe.matmul(bank[7][0:1, 0:1], one1, one1, start=True, stop=True).then_inc(slab_used, 2)
            n0 = first[("w2", 0)]
            for half in range(2):
                for r in range(3):
                    n = n0 + 3 * half + r
                    need_slab(n)
                    v = slab_view(n)
                    if half == 0 and r == 0:
                        pe.wait_ge(fup_done, FB)
                    for m in range(4):
                        b = (0, 1, 2, 3)[m] if half == 0 else (4, 5, 0, 1)[m]
                        if half == 1 and r == 0 and m >= 2:
                            pe.wait_ge(fdn_taken, m - 1)
                        for k in range(plan[n][3]):
                            mm = pe.matmul(bank[b][:, 0:NT], v[:, k, P * m:P * (m + 1)], gT[:, 8 * r + k, :],
                                           start=(r == 0 and k == 0), stop=(r == 2 and k == plan[n][3] - 1),
                                           skip_group_check=True)
                    mm.then_inc(slab_used, 1)
                pe.matmul(bank[7][0:1, 0:1], one1, one1, start=True, stop=True).then_inc(fdn_summed, 1)
            ada_products(2)
            norm_sum(3)
            norm_sum(4)
            lin = 0
            turned = 0

            def rotate(i):
                if i >= 2:
                    pe.wait_ge(rot_done, i - 1)
                pe.wait_ge(lin_raw, i + 1 + (KC if i >= KC else 0))
                pe.matmul(bank[2 + i % 2][:, 0:NT], rot, rawT[:, i % 2, :], start=True, stop=True).then_inc(rot_summed, 1)

            def lin_block(slab, col, rhs, i):
                need_slab(slab)
                if i >= 2:
                    pe.wait_ge(lin_raw, i - 1)
                v = slab_view(slab)
                for k in range(KC):
                    mm = pe.matmul(bank[i % 2][:, 0:NT], v[:, k, P * col:P * (col + 1)], rhs[:, k, :],
                                   start=(k == 0), stop=(k == KC - 1))
                mm.then_inc(lin_summed, 1)

            def slab_end():
                pe.matmul(bank[7][0:1, 0:1], one1, one1, start=True, stop=True).then_inc(slab_used, 1)

            pe.wait_ge(h_ready, 3)
            for i in range(2 * KC):
                lin_block(first[("wkv", 0)] + i // 4, i % 4, hT, i)
                if i % 4 == 3:
                    slab_end()
                if 1 <= i <= KC:
                    rotate(i - 1)
            for q in range(4):
                if q == 0:
                    pe.wait_ge(rot_done, KC)
                if q == 2:
                    pe.wait_ge(lin_raw, 2 * KC)
                if q >= 1:
                    pe.wait_ge(kv_taken, q)
                for m in range(4):
                    k = 4 * (q % 2) + m
                    src = (kT if q < 2 else mT)
                    for c, n in ((0, P), (1, P), (2, NB)):
                        mm = pe.transpose(bank[4 + c if c < 2 else 7][0:n, P * m:P * (m + 1)], src[:, k, c * P:c * P + n], ident)
                mm.then_inc(kv_turned, 1)
            pe.wait_ge(h_ready, 4)
            for i in range(NG * KC):
                lin_block(first[("wq", 0)] + i // 4, i % 4, hT, 2 * KC + i)
                if i % 4 == 3:
                    slab_end()
                if i >= 1:
                    rotate(KC + i - 1)
            rotate(KC + NG * KC - 1)

            pe.wait_ge(pair_ready, 1)
            for g in range(NG):
                mm = pe.matmul(bank[5][:, g:g + 1], kprod[:, g].rearrange("p b j s -> p (b j s)"), one1, start=True, stop=True)
            NTILE = NB * NG

            def key_scores(t):
                b, g = t // NG, t % NG
                pe.wait_ge(kt_lo, t + 1)
                pe.wait_ge(kt_hi, t + 1)
                for j in range(KC):
                    c = (b * KC + j) * 2
                    mm = pe.matmul(bank[4][:, P * g + c:P * g + c + 2], kTs[:, t % 2, P * j:P * (j + 1)], qpair[:, g, b, j, :],
                                   start=True, stop=True)
                mm.then_inc(s_summed, 1)

            for t in range(NTILE):
                b, g = t // NG, t % NG
                n = first[("ck", 0)] + b
                need_slab(n)
                if t >= 2:
                    pe.wait_ge(kt_lo, t - 1)
                    pe.wait_ge(kt_hi, t - 1)
                for j in range(KC):
                    mm = pe.transpose(bank[2 * (t % 2) + j // 4][:, P * (j % 4):P * (j % 4 + 1)],
                                      slab_view(n)[:, g, P * j:P * (j + 1)], ident)
                mm.then_inc(kt_turned, 1)
                if g == NG - 1:
                    slab_end()
                if t >= 1:
                    key_scores(t - 1)
            key_scores(NTILE - 1)
            pe.wait_ge(s_taken, 1)
            for g in range(NG):
                mm = pe.transpose(bank[6][:, P * g:P * (g + 1)], s_scores[:, g, :], ident)
            mm.then_inc(s_turned, 1)
            pe.wait_ge(s_prob, 1)
            for g in range(NG):
                mm = pe.transpose(bank[7][:, P * g:P * (g + 1)], s_soft[:, P * g:P * (g + 1)], ident)
            mm.then_inc(sp_turned, 1)
            pe.wait_ge(pn_ready, 1)
            pe.matmul(bank[5][:, P:2 * P], pnewb, ident, start=True, stop=True).then_inc(pn_spread, 1)
            pe.wait_ge(sp_taken, 1)
            for b in range(NB):
                n = first[("cv", 0)] + b
                need_slab(n)
                for j in range(KC):
                    c = (b * KC + j) * 2
                    for g in range(NG):
                        mm = pe.matmul(bank[4][:, c:c + 2], slab_view(n)[:, g, P * j:P * (j + 1)], s_pT[:, g, c:c + 2],
                                       start=(g == 0), stop=(g == NG - 1))
                mm.then_inc(slab_used, 1)
            pe.matmul(bank[5][0:1, 300:301], one1, one1, start=True, stop=True).then_inc(sv_summed, 1)

            units = [(h, c) for h in range(H) for c in range(2)]

            def scores(u):
                h, c = units[u]
                lo = HD * (h % 2)
                if u >= 2:
                    pe.wait_ge(a_max, u - 1)
                for g in range(NG):
                    b = bank[2 * c + g // 2]
                    n = P * (c + 1)
                    mm = pe.matmul(b[:, 256 * (g % 2):256 * (g % 2) + n], qT[lo:lo + HD, g * KC + h // 2, c * P:(c + 1) * P],
                                   kT[lo:lo + HD, h // 2, 0:n], start=True, stop=True)
                mm.then_inc(a_scored, 1)

            def weights_to_columns(u):
                h, c = units[u]
                pe.wait_ge(a_sum, u + 1)
                if u >= 1:
                    pe.wait_ge(a_copied, u)
                for k in range(c + 1):
                    mm = pe.transpose(bank[4][:, P * k:P * (k + 1)], p_sum[:, P * k:P * (k + 1)], ident)
                mm.then_inc(a_turned, 1)

            def values(u):
                h, c = units[u]
                pe.wait_ge(a_copied, u + 1)
                if u >= 2:
                    pe.wait_ge(a_taken, u - 1)
                for k in range(c + 1):
                    mm = pe.matmul(bank[6 + u % 2][:, 0:HD], p_T[:, k, :], vtok[:, k, HD * h:HD * (h + 1)],
                                   start=(k == 0), stop=(k == c))
                mm.then_inc(a_out, 1)

            pe.wait_ge(sv_done, 1)
            for u in range(len(units) + 2):
                if u < len(units):
                    scores(u)
                if 1 <= u <= len(units):
                    weights_to_columns(u - 1)
                if u >= 2:
                    values(u - 2)
            pe.wait_ge(a_taken, len(units))
            for k in range(KC):
                if k >= 2:
                    pe.wait_ge(ot_taken, k - 1)
                for c in range(2):
                    mm = pe.transpose(bank[k % 2][:, P * c:P * (c + 1)], otok[:, c, P * k:P * (k + 1)], ident)
                mm.then_inc(ot_turned, 1)
            pe.wait_ge(ot_taken, KC)
            for i in range(KC):
                n = first[("wo", 0)] + i // 4
                need_slab(n)
                if i >= 2:
                    pe.wait_ge(wo_taken, i - 1)
                for k in range(KC):
                    mm = pe.matmul(bank[2 + i % 2][:, 0:NT], slab_view(n)[:, k, P * (i % 4):P * (i % 4 + 1)], mT[:, k, :],
                                   start=(k == 0), stop=(k == KC - 1))
                mm.then_inc(wo_summed, 1)
                if i % 4 == 3:
                    slab_end()
            ada_products(3)
            norm_sum(5)
            norm_sum(6)

            pe.wait_ge(h_ready, 5)
            pe.wait_ge(in_router, 32)
            for c, n in ((0, P), (1, P), (2, NB)):
                for k in range(KC):
                    pe.matmul(bank[0][0:n, NE * c:NE * (c + 1)], hT[:, k, P * c:P * c + n], rw[:, k, :], start=(k == 0), stop=False)
                mm = pe.matmul(bank[0][0:n, NE * c:NE * (c + 1)], ones[0:1, 0:n], rb[0:1, :], start=False, stop=True)
            mm.then_inc(lg_summed, 1)
            for k in range(KC):
                if k >= 2:
                    pe.wait_ge(ht_taken, k - 1)
                for c, n in ((0, P), (1, P), (2, NB)):
                    mm = pe.transpose(bank[2 + k % 2][0:n, P * c:P * (c + 1)], hT[:, k, c * P:c * P + n], ident)
                mm.then_inc(ht_turned, 1)
            pe.wait_ge(sel_ready, 1)
            rows = (P, P, NB)
            for c in range(3):
                for k in range(c + 1):
                    n = rows[k]
                    pe.matmul(bank[1][0:rows[c], NE * c:NE * (c + 1)], (before if k == c else ones)[0:n, 0:rows[c]], sel[0:n, k, :],
                              start=(k == 0), stop=(k == c))
            for k in range(3):
                mm = pe.matmul(bank[1][:, 3 * NE:4 * NE], ones[0:rows[k], :], sel[0:rows[k], k, :], start=(k == 0), stop=(k == 2))
            mm.then_inc(pos_summed, 1)
            pe.wait_ge(ht_taken, KC)
            pe.wait_ge(moe_ready, 1)

            def expert(e, c):
                use = [[k for k in range(PER_E) if (NPRE + k) % RING == r] for r in range(RING)]

                def slab(k):
                    slot = (NPRE + k) % RING
                    pe.wait_ge(slab_in[slot], e * (16 * len(use[slot])) + (
                        before_experts[slot] + 16 * (c * NE * len(use[slot]) + use[slot].index(k) + 1)))
                    return ring[:, slot, :]

                def count(per, k):
                    return e * per + (c * NE * per + k)

                pe.wait_ge(route_built, count(1, 1))
                pe.wait_ge(y_added, count(KC, 1))
                for k in range(KC):
                    for q in range(3):
                        n = rows[q]
                        mm = pe.matmul(bank[k // 4][:, P * (k % 4):P * (k % 4) + SLOTS], htok[0:n, q, P * k:P * (k + 1)], disp[0:n, q, :],
                                       start=(q == 0), stop=(q == 2))
                    if k % 4 == 3:
                        mm.then_inc(gathered, 1)
                for q in range(3):
                    n = rows[q]
                    mm = pe.transpose(bank[2][0:SLOTS, P * q:P * q + n], dispg[0:n, q, :], ident[0:n, 0:n])
                mm.then_inc(comb_turned, 1)

                def product(m, j, bk):
                    s = slab(eslabs.index((m, j))).rearrange("p (k n) -> p k n", k=KC)
                    for i in range(KC):
                        mm = pe.matmul(bank[bk][0:SLOTS, :], xeT[:, i, :], s[:, i, :], start=(i == 0), stop=(i == KC - 1))
                    mm.then_inc(slab_used, 1)

                def turn(j):
                    pe.wait_ge(up_ready, count(FCH, j + 2))
                    pe.wait_ge(upT_copied, count(FCH, j + 1))
                    for i in range(4):
                        mm = pe.transpose(bank[5][:, SLOTS * i:SLOTS * (i + 1)], up[0:SLOTS, P * i:P * (i + 1)], ident[0:SLOTS, 0:SLOTS])
                    mm.then_inc(up_turned, 1)

                def down(j):
                    s = slab(eslabs.index((2, j))).rearrange("p (k n) -> p k n", k=4)
                    pe.wait_ge(upT_copied, count(FCH, j + 2))
                    if j == 0:
                        pe.wait_ge(y0_copied, count(1, 1))
                        pe.wait_ge(y1_copied, count(1, 1))
                    for i in range(4):
                        for half in range(2):
                            mm = pe.matmul(bank[6 + half][0:SLOTS, :], upT[:, i, 0:SLOTS], s[:, i, 512 * half:512 * (half + 1)],
                                           start=(j == 0 and i == 0), stop=(j == FCH - 1 and i == 3), skip_group_check=True)
                    mm.then_inc(slab_used, 1)

                pe.wait_ge(xe0_copied, count(1, 1))
                pe.wait_ge(xe1_copied, count(1, 1))
                for j in range(FCH):
                    pe.wait_ge(silu_done, count(FCH, j + 1))
                    product(1, j, 3)
                    if j >= 1:
                        turn(j - 1)
                    pe.wait_ge(up_ready, count(FCH, j + 1))
                    product(3, j, 4)
                    if j >= 1:
                        down(j - 1)
                turn(FCH - 1)
                down(FCH - 1)
                pe.wait_ge(comb_copied, count(1, 1))
                pe.wait_ge(y0_copied, count(1, 2))
                pe.wait_ge(y1_copied, count(1, 2))
                for k in range(KC):
                    if k >= 2:
                        pe.wait_ge(y_added, count(KC, k))
                    pe.matmul(bank[k % 2][:, 0:NT], ye[0:SLOTS, P * k:P * (k + 1)], comb[0:SLOTS, :], start=True, stop=True)\
                      .then_inc(c_summed, 1)

            with pe.Fori(0, NE) as e:
                expert(e, 0)
            over = pe.value_load(flag[0:1, 0:1], min_val=0, max_val=1)
            with pe.If(over > 0):
                for c in range(1, PASSES):
                    with pe.Fori(0, NE) as e:
                        expert(e, c)
            norm_sum(7)
            pe.wait_ge(h_ready, 6)
            for k in range(KC):
                if k >= 2:
                    pe.wait_ge(y_taken, k - 1)
                for q, n in ((0, P), (1, P), (2, NB)):
                    mm = pe.transpose(bank[2 + k % 2][0:n, P * q:P * (q + 1)], xT[:, k, q * P:q * P + n], ident)
                mm.then_inc(y_turned, 1)

        @block.scalar
        def _(act):
            steps = [0]

            def link(ins):
                steps[0] += 1
                ins.then_inc(act_step, 1)
                act.wait_ge(act_step, steps[0])

            act.dma_start(crow[0:1, :], w["c_prompt"]).then_inc(in_vec, 16)
            act.dma_start(crow[1:9, :], w["c_sample"]).then_inc(in_vec, 16)
            act.dma_start(const[:, :], w["shape_constants"]).then_inc(in_const, 16)
            act.dma_start(vrow1[0:48, :], w["ada_mix_b"].rearrange("l (m p) -> (l m) p", p=P)).then_inc(in_vec, 16)
            act.dma_start(vrow1[48:96, :], w["ada_ffn_b"].rearrange("l (m p) -> (l m) p", p=P)).then_inc(in_vec, 16)
            act.dma_start(xtok[:, 0:2, :], w["x_prompt"][0].rearrange("(c p) d -> p c d", p=P)).then_inc(in_x, 16)
            act.dma_start(xtok[0:NB, 2, :], w["x_sample"][:, 0, :]).then_inc(in_x, 16)
            for i, name in enumerate(("g_pre_mix", "g_post_mix", "g_pre_ffn", "g_post_ffn")):
                act.dma_start(vrow2[16 * i:16 * (i + 1), :], w[name].rearrange("l (m p) -> (l m) p", p=P)).then_inc(in_vec, 16)
            act.dma_start(vrow2[64:72, :], w["g_kv"].rearrange("(m p) -> m p", p=P)).then_inc(in_vec, 16)
            act.dma_start(vrow2[72:80, :], w["pool_scale"][0].rearrange("(m p) -> m p", p=P)).then_inc(in_vec, 16)
            act.dma_start(strow[0:NB * STATE, :], w["state_pool"][:, 0].rearrange("b t d -> (b t) d")).then_inc(in_state, 16)
            act.dma_start(poolw[:, :, :, :], w["pool_w"][0].rearrange("g (k p) n -> p g k n", p=P)).then_inc(in_pool, 16)
            act.dma_start(rw[:, :, :], w["router_w"][0].rearrange("(k p) n -> p k n", p=P)).then_inc(in_router, 16)
            act.dma_start(rb[:, :], w["router_b"]).then_inc(in_router, 16)
            act.dma_start(o["pool_sample"][:, 0, 0:STATE - 1, :], w["state_pool"][:, 0, 1:STATE, :]).then_inc(out_done, 16)

            act.wait_ge(in_vec, 16 * 10)
            act.activation(crow[0:9, :], crow[0:9, :], ACT.Silu).then_inc(c_silu, 1)

            def norm(i, src):
                act.wait_ge(norm_in, i + 1)
                act.activation(tT[:, :, :], src[:, :, :], ACT.Square).then_inc(sq_ready, 1)
                act.wait_ge(norm_summed, i + 1)
                act.activation(std[:, :], bank[7][:, 0:NT], ACT.Sqrt, bias=eps1, scale=1.0 / D).then_inc(std_ready, 1)

            norm(0, xT)
            for i in range(KC):
                act.wait_ge(pool_summed, i + 1)
                act.activation(mT[:, i, :], bank[2 + i % 2][:, 0:NT], ACT.Copy, scale=vec2[:, 72 + i:73 + i]).then_inc(pool_taken, 1)
            act.wait_ge(ps_turned, 1)
            for k in range(2):
                ins = act.activation(pstate[0:STATE + NB, 512 * k:512 * (k + 1)], bank[4 + k][0:STATE + NB, :], ACT.Copy)
            ins.then_inc(ps_rows, 1)
            act.wait_ge(ps_rows, 1)
            act.dma_start(o["pool_prompt"][0, 0], pstate[0:STATE, :]).then_inc(out_done, 16)
            act.dma_start(o["pool_sample"][:, 0, STATE - 1, :], pstate[STATE:STATE + NB, :]).then_inc(out_done, 16)
            act.wait_ge(pool_taken, KC)
            norm(1, mT)
            norm(2, xT)
            act.wait_ge(out_done, 48)
            for i in range(FB):
                act.wait_ge(fup_summed, 2 * i + 1)
                if i >= 2:
                    act.wait_ge(fup_done, i - 1)
                act.activation(silu_up[:, i % 2, :], bank[i % 2][:, 0:NT], ACT.Silu).then_inc(fup_silu, 1)
            norm(3, mT)
            norm(4, xT)
            for i in range(2 * KC + NG * KC):
                act.wait_ge(lin_summed, i + 1)
                if KC <= i < 2 * KC:
                    act.activation(mT[:, i - KC, :], bank[i % 2][:, 0:NT], ACT.Copy).then_inc(lin_raw, 1)
                    continue
                r = i if i < KC else i - KC
                if r >= 2:
                    act.wait_ge(rot_done, r - 1)
                if i == 2 * KC:
                    act.wait_ge(rot_done, KC)
                act.activation(rawT[:, r % 2, :], bank[i % 2][:, 0:NT], ACT.Copy).then_inc(lin_raw, 1)

            for t in range(NB * NG):
                act.wait_ge(kt_turned, t + 1)
                if t >= 2:
                    act.wait_ge(s_summed, t - 1)
                if t == 0:
                    act.wait_ge(pair_ready, 1)
                act.activation(kTs[:, t % 2, 0:512], bank[2 * (t % 2)][:, :], ACT.Copy).then_inc(kt_lo, 1)
            act.wait_ge(s_max, 1)
            act.activation(s_soft, s_soft, ACT.Exp, bias=s_stat[:, 0:1], accum_out=s_stat[:, 1:2]).then_inc(s_exp, 1)
            for u in range(2 * H):
                c = u % 2
                n = P * (c + 1)
                act.wait_ge(a_max, u + 1)
                act.activation(sm[u % 2][:, :, 0:n], sm[u % 2][:, :, 0:n], ACT.Exp, bias=p_stat[:, u % 4, 0:1],
                               accum_out=p_stat[:, u % 4, 1:2]).then_inc(a_exp, 1)
                if u >= 1:
                    v = u - 1
                    act.wait_ge(a_turned, v + 1)
                    if v >= 1:
                        act.wait_ge(a_out, v)
                    act.activation(p_T[:, 0:v % 2 + 1, :], bank[4][:, 0:P * (v % 2 + 1)].rearrange("p (k n) -> p k n", n=P),
                                   ACT.Copy).then_inc(a_copied, 1)
            v = 2 * H - 1
            act.wait_ge(a_turned, v + 1)
            act.wait_ge(a_out, v)
            act.activation(p_T[:, 0:v % 2 + 1, :], bank[4][:, 0:P * (v % 2 + 1)].rearrange("p (k n) -> p k n", n=P),
                           ACT.Copy).then_inc(a_copied, 1)
            for i in range(KC):
                act.wait_ge(wo_summed, i + 1)
                if i == 0:
                    act.wait_ge(wo_summed, 1)
                act.activation(hT[:, i, :], bank[2 + i % 2][:, 0:NT], ACT.Copy).then_inc(wo_taken, 1)
            act.wait_ge(wo_taken, KC)
            norm(5, hT)
            norm(6, xT)
            act.wait_ge(lg_max, 1)
            for q, n in ((0, P), (1, P), (2, NB)):
                ins = act.activation(r_c[0:n, q, :], lg[0:n, q, :], ACT.Exp, bias=r_s[0:n, q, 0:1])
            ins.then_inc(lg_exp, 1)
            for k in range(KC):
                act.wait_ge(ht_turned, k + 1)
                act.activation(htok[:, 0:2, P * k:P * (k + 1)], bank[2 + k % 2][:, 0:256].rearrange("p (c n) -> p c n", c=2), ACT.Copy)
                act.activation(htok[0:NB, 2, P * k:P * (k + 1)], bank[2 + k % 2][0:NB, 256:384], ACT.Copy).then_inc(ht_taken, 1)
            act.sem_inc(silu_done, 1)
            act.sem_inc(upT_copied, 1)
            act.sem_inc(y0_copied, 1)

            def expert(e, c):
                def count(per, k):
                    return e * per + (c * NE * per + k)

                act.wait_ge(gathered, count(2, 1))
                act.activation(xeT[:, 0:4, :], bank[0][:, 0:4 * P].rearrange("p (k n) -> p k n", k=4)[:, :, 0:SLOTS], ACT.Copy).then_inc(xe0_copied, 1)
                for j in range(FCH):
                    act.wait_ge(slab_used, used_by(e, c, 1, j))
                    act.wait_ge(up_ready, count(FCH, j + 1))
                    act.activation(up_s[0:SLOTS, :], bank[3][0:SLOTS, :], ACT.Silu).then_inc(silu_done, 1)
                    if j >= 1:
                        act.wait_ge(up_turned, count(FCH, j))
                        act.activation(upT[:, :, 0:SLOTS], bank[5][:, 0:4 * SLOTS].rearrange("p (k n) -> p k n", k=4), ACT.Copy)\
                           .then_inc(upT_copied, 1)
                act.wait_ge(up_turned, count(FCH, FCH))
                act.activation(upT[:, :, 0:SLOTS], bank[5][:, 0:4 * SLOTS].rearrange("p (k n) -> p k n", k=4), ACT.Copy)\
                   .then_inc(upT_copied, 1)
                act.wait_ge(slab_used, used_by(e, c, 2, FCH - 1))
                act.activation(ye[0:SLOTS, 0:512], bank[6][0:SLOTS, :], ACT.Copy).then_inc(y0_copied, 1)

            with act.Fori(0, NE) as e:
                expert(e, 0)
            over = act.value_load(flag[0:1, 0:1], min_val=0, max_val=1)
            with act.If(over > 0):
                for c in range(1, PASSES):
                    with act.Fori(0, NE) as e:
                        expert(e, c)
            norm(7, mT)
            for k in range(KC):
                act.wait_ge(y_turned, k + 1)
                act.activation(ytok[:, 0:2, P * k:P * (k + 1)], bank[2 + k % 2][:, 0:256].rearrange("p (c n) -> p c n", c=2), ACT.Copy)
                act.activation(ytok[0:NB, 2, P * k:P * (k + 1)], bank[2 + k % 2][0:NB, 256:384], ACT.Copy).then_inc(y_taken, 1)
            act.wait_ge(y_taken, KC)
            act.dma_start(o["y_prompt"][0].rearrange("(c p) d -> p c d", p=P), ytok[:, 0:2, :]).then_inc(out_done, 16)
            act.dma_start(o["y_sample"][:, 0, :], ytok[0:NB, 2, :]).then_inc(out_done, 16)
            act.wait_ge(out_done, 16 * 5)

        @block.vector
        def _(dve):
            steps = [0]

            def link(ins):
                steps[0] += 1
                ins.then_inc(dve_step, 1)
                dve.wait_ge(dve_step, steps[0])

            dve.wait_ge(vec_turned, 1)
            dve.tensor_copy(vec1[:, :], bank[0][:, 0:96])
            dve.tensor_copy(vec2[:, :], bank[0][:, 96:176]).then_inc(vec_read, 1)
            dve.wait_ge(c_turned, 1)
            dve.tensor_copy(cT[:, :, :], bank[1][:, 0:9 * KC].rearrange("p (k n) -> p k n", k=KC)).then_inc(c_read, 1)
            for k in range(KC):
                dve.wait_ge(x_turned, k + 1)
                dve.tensor_copy(xT[:, k, :], bank[2 + k % 2][:, 0:NT]).then_inc(x_taken, 1)
            dve.wait_ge(x_taken, KC)
            dve.sem_inc(norm_in, 1)
            for k in range(KC):
                dve.wait_ge(st_turned, k + 1)
                dve.tensor_copy(sExt[:, k, :, 0:STATE], bank[4 + k % 2][:, 0:120].rearrange("p (b t) -> p b t", b=NB))\
                   .then_inc(st_taken, 1)
            link(dve.memset(ext[:, :, 0:STATE], 0.0))

            def across(a, n):
                return a.unsqueeze(2).to_broadcast(list(a.shape[:2]) + [n])

            def ada_take(s, kind, layer):
                a = ada[:, s]
                dve.wait_ge(slab_used, first[("ada", s)] + 6)
                dve.wait_ge(vec_read, 1)
                col = 48 * kind + 24 * layer
                link(dve.tensor_tensor(a, bank[6][:, 0:216].rearrange("p (m n) -> p m n", m=24),
                                       across(vec1[:, col:col + 24], 9), ALU.add))
                pre, post = 32 * kind + 8 * layer, 32 * kind + 16 + 8 * layer
                dve.scalar_tensor_tensor(a[:, 8:16, :], a[:, 8:16, :], 1.0, across(vec2[:, pre:pre + 8], 9), ALU.add, ALU.mult)
                link(dve.tensor_tensor(a[:, 16:24, :], a[:, 16:24, :], across(vec2[:, post:post + 8], 9), ALU.mult))
                dve.sem_inc(ada_taken, 1)

            def wide(a):
                return a.unsqueeze(1).to_broadcast([P, KC, a.shape[-1]])

            def normalise(i, src, fresh=True):
                dve.wait_ge(std_ready, i + 1)
                if fresh:
                    link(dve.reciprocal(rstd[:, :], std[:, :]))
                link(dve.tensor_tensor(tT[:, :, :], src[:, :, :], wide(rstd[:, :]), ALU.mult))

            def modulate(s, out, done):
                for k in range(KC):
                    dve.tensor_scalar(out[:, k, 0:T], tT[:, k, 0:T], ada[:, s, 8 + k, 0:1], ada[:, s, k, 0:1], ALU.mult, ALU.add)
                link(dve.tensor_tensor(small[:, :, :], tT[:, :, T:NT], ada[:, s, 8:16, 1:9], ALU.mult))
                link(dve.tensor_tensor(out[:, :, T:NT], small[:, :, :], ada[:, s, 0:8, 1:9], ALU.add))
                if done is not None:
                    dve.sem_inc(done, 1)

            def residual(s, done):
                for k in range(KC):
                    dve.scalar_tensor_tensor(xT[:, k, 0:T], tT[:, k, 0:T], ada[:, s, 16 + k, 0:1], xT[:, k, 0:T], ALU.mult, ALU.add)
                link(dve.tensor_tensor(small[:, :, :], tT[:, :, T:NT], ada[:, s, 16:24, 1:9], ALU.mult))
                link(dve.tensor_tensor(xT[:, :, T:NT], xT[:, :, T:NT], small[:, :, :], ALU.add))
                if done is not None:
                    dve.sem_inc(done, 1)

            ada_take(0, 0, 0)
            normalise(0, xT)
            modulate(0, hT, None)
            link(dve.tensor_copy(ext[:, :, STATE:EXT], hT[:, :, 0:T]))
            link(dve.tensor_copy(sExt[:, :, :, STATE], hT[:, :, T:NT]))
            link(dve.tensor_tensor(sum_a[:, :, 1:EXT], ext[:, :, 1:EXT], ext[:, :, 0:EXT - 1], ALU.add))
            link(dve.tensor_tensor(sum_b[:, 2:KC, 3:EXT], sum_a[:, 2:KC, 3:EXT], sum_a[:, 2:KC, 1:EXT - 2], ALU.add))
            link(dve.tensor_tensor(sum_a[:, 4:KC, 7:EXT], sum_b[:, 4:KC, 7:EXT], sum_b[:, 4:KC, 3:EXT - 4], ALU.add))
            link(dve.tensor_tensor(sum_b[:, 6:KC, 15:EXT], sum_a[:, 6:KC, 15:EXT], sum_a[:, 6:KC, 7:EXT - 8], ALU.add))
            for g, n in enumerate(WIN):
                s = (sum_a, sum_b)[g % 2]
                ks = slice(2 * g, 2 * g + 2)
                link(dve.scalar_tensor_tensor(tT[:, ks, 16:T], s[:, ks, STATE + 16:EXT], 1.0 / n, ext[:, ks, STATE + 16:EXT],
                                              ALU.mult, ALU.subtract))
                link(dve.tensor_tensor(tT[:, ks, 0:16], s[:, ks, STATE:STATE + 16],
                                       invcnt[:, g, :].unsqueeze(1).to_broadcast([P, 2, 16]), ALU.mult))
                link(dve.tensor_tensor(tT[:, ks, 0:16], tT[:, ks, 0:16], ext[:, ks, STATE:STATE + 16], ALU.subtract))
                for k in range(2 * g, 2 * g + 2):
                    link(dve.tensor_reduce(small[:, k, :], sExt[:, k, :, STATE + 1 - n:STATE + 1], X, ALU.add))
                    link(dve.scalar_tensor_tensor(tT[:, k, T:NT], small[:, k, :], 1.0 / n, sExt[:, k, :, STATE], ALU.mult, ALU.subtract))
            dve.sem_inc(pm_ready, 1)
            ada_take(1, 1, 0)
            dve.wait_ge(pool_taken, KC)
            dve.sem_inc(norm_in, 1)
            normalise(1, mT)
            residual(0, norm_in)
            normalise(2, xT)
            dve.wait_ge(ps_turned, 1)
            modulate(1, hT, None)
            dve.sem_inc(h_ready, 2)
            dve.wait_ge(out_done, 48)
            for i in range(FB):
                dve.wait_ge(fup_summed, 2 * i + 2)
                dve.wait_ge(fup_silu, i + 1)
                dve.tensor_tensor(gT[:, i, :], bank[2 + i % 2][:, 0:NT], silu_up[:, i % 2, :], ALU.mult).then_inc(fup_done, 1)
            for half in range(2):
                dve.wait_ge(fdn_summed, half + 1)
                for m in range(4):
                    b = (0, 1, 2, 3)[m] if half == 0 else (4, 5, 0, 1)[m]
                    dve.tensor_copy(mT[:, 4 * half + m, :], bank[b][:, 0:NT]).then_inc(fdn_taken, 1)
            dve.wait_ge(fdn_taken, 8)
            dve.sem_inc(norm_in, 1)
            ada_take(2, 0, 1)
            normalise(3, mT)
            residual(1, norm_in)
            normalise(4, xT)
            for k in range(KC):
                ins = dve.tensor_scalar(hT[:, k, :], tT[:, k, :], vec2[:, 64 + k:65 + k], None, ALU.mult)
            link(ins)
            dve.sem_inc(h_ready, 1)

            def rope(i, out):
                dve.wait_ge(rot_summed, i + 1)
                link(dve.tensor_tensor(rot_a, bank[2 + i % 2][:, 0:NT], sin, ALU.mult))
                link(dve.tensor_tensor(rot_b, rawT[:, i % 2, :], cos, ALU.mult))
                dve.tensor_tensor(out, rot_a, rot_b, ALU.add).then_inc(rot_done, 1)
                dve.wait_ge(rot_done, i + 1)

            for i in range(KC):
                rope(i, kT[:, i, :])
            for q in range(4):
                dve.wait_ge(kv_turned, q + 1)
                cols = slice(512 * (q % 2), 512 * (q % 2) + 512)
                rows = (ktok[:, 0, cols], ktok[:, 1, cols], ktok[0:NB, 2, cols]) if q < 2 else \
                    (vtok[:, 0, cols], vtok[:, 1, cols], vntok[:, cols])
                dve.tensor_copy(rows[0], bank[4][:, :])
                dve.tensor_copy(rows[1], bank[5][:, :])
                dve.tensor_copy(rows[2], bank[7][0:NB, :]).then_inc(kv_taken, 1)
            dve.wait_ge(lin_raw, 2 * KC)
            link(dve.tensor_copy(vnew[:, :, :], mT[:, :, T:NT]))
            dve.wait_ge(lin_summed, 2 * KC)
            link(dve.tensor_tensor(tT[:, :, :], xT[:, :, :], wide(rstd[:, :]), ALU.mult))
            modulate(2, hT, h_ready)
            dve.wait_ge(kv_rows, 16 * 4)
            for i in range(NG * KC):
                rope(KC + i, qT[:, i, :])
            dve.wait_ge(rot_summed, KC + NG * KC)
            dve.memset(hflat[:, 0:384], 0.0)
            link(dve.memset(hflat[:, 384:768], 0.0))
            for g in range(NG):
                for s in range(2):
                    q = slice(HD * s, HD * (s + 1))
                    link(dve.tensor_copy(qpair[q, g, :, :, s], qT[q, g * KC:(g + 1) * KC, T:NT].rearrange("p j b -> p b j")))
                    link(dve.tensor_tensor(kprod[q, g, :, :, s], qpair[q, g, :, :, s], kT[q, :, T:NT].rearrange("p j b -> p b j"), ALU.mult))
            dve.sem_inc(pair_ready, 1)
            for t in range(NB * NG):
                dve.wait_ge(kt_turned, t + 1)
                if t >= 2:
                    dve.wait_ge(s_summed, t - 1)
                dve.tensor_copy(kTs[:, t % 2, 512:1024], bank[2 * (t % 2) + 1][:, :]).then_inc(kt_hi, 1)
            dve.wait_ge(s_summed, NB * NG)
            dve.tensor_copy(s_scores, bank[4][:, 0:384].rearrange("p (g n) -> p g n", g=NG)).then_inc(s_taken, 1)
            dve.wait_ge(s_turned, 1)
            link(dve.tensor_scalar(s_soft[:, 0:384], bank[6][:, 0:384], SCALE, None, ALU.mult))
            link(dve.tensor_scalar(s_soft[:, 384:387], bank[5][:, 0:3], SCALE, None, ALU.mult))
            dve.tensor_reduce(s_stat[:, 0:1], s_soft, X, ALU.max, negate=True).then_inc(s_max, 1)
            dve.wait_ge(s_exp, 1)
            link(dve.reciprocal(s_stat[:, 2:3], s_stat[:, 1:2]))
            dve.tensor_scalar(s_soft, s_soft, s_stat[:, 2:3], None, ALU.mult).then_inc(s_prob, 1)
            dve.wait_ge(s_prob, 1)
            link(dve.tensor_reduce(s_stat[:, 3:4], s_soft[:, 384:387], X, ALU.add))
            dve.tensor_copy(pnewb, s_stat[:, 3:4].to_broadcast([P, P])).then_inc(pn_ready, 1)
            dve.wait_ge(sp_turned, 1)
            dve.tensor_copy(s_pT, bank[7][:, 0:384].rearrange("p (g n) -> p g n", g=NG)).then_inc(sp_taken, 1)
            dve.wait_ge(pn_spread, 1)
            dve.wait_ge(sv_summed, 1)
            for s in range(2):
                q = slice(HD * s, HD * (s + 1))
                pn = bank[5][q, P:2 * P].rearrange("p (b j s) -> p j b s", b=NB, j=KC)[:, :, :, s]
                sv = bank[4][q, 0:P].rearrange("p (b j s) -> p j b s", b=NB, j=KC)[:, :, :, s]
                link(dve.tensor_tensor(small[q, :, :], pn, vnew[q, :, :], ALU.mult))
                link(dve.tensor_tensor(mT[q, :, T:NT], small[q, :, :], sv, ALU.add))
            dve.sem_inc(sv_done, 1)
            def mask_max(u):
                c = u % 2
                n = P * (c + 1)
                dve.wait_ge(a_scored, u + 1)
                if u >= 2:
                    dve.wait_ge(a_sum, u - 1)
                for q, (g0, g1) in enumerate(((0, 2), (2, 3))):
                    src = bank[2 * c + q][:, 0:256 * (g1 - g0)].rearrange("p (g k) -> p g k", k=256)[:, :, 0:n]
                    ins = dve.scalar_tensor_tensor(sm[u % 2][:, g0:g1, 0:n], src, SCALE, mask[:, g0:g1, 256 - n:256], ALU.mult, ALU.add)
                link(ins)
                dve.tensor_reduce(p_stat[:, u % 4, 0:1], sm[u % 2][:, :, 0:n], mybir.AxisListType.XY, ALU.max, negate=True).then_inc(a_max, 1)

            def head_out(u):
                h, c = u // 2, u % 2
                dve.wait_ge(a_exp, u + 1)
                link(dve.reciprocal(p_stat[:, u % 4, 2:3], p_stat[:, u % 4, 1:2]))
                dve.wait_ge(a_out, u + 1)
                dve.tensor_scalar(otok[:, c, HD * h:HD * (h + 1)], bank[6 + u % 2][:, 0:HD], p_stat[:, u % 4, 2:3], None, ALU.mult)\
                   .then_inc(a_taken, 1)

            for u in range(2 * H + 2):
                if u < 2 * H:
                    mask_max(u)
                if u >= 2:
                    head_out(u - 2)
            for k in range(KC):
                dve.wait_ge(ot_turned, k + 1)
                dve.tensor_copy(mT[:, k, 0:T], bank[k % 2][:, 0:T]).then_inc(ot_taken, 1)
            dve.wait_ge(wo_taken, KC)
            dve.sem_inc(norm_in, 1)
            ada_take(3, 1, 1)
            normalise(5, hT)
            residual(2, norm_in)
            normalise(6, xT)
            modulate(3, hT, h_ready)
            dve.wait_ge(lg_summed, 1)
            rows = (P, P, NB)
            link(dve.memset(sel[:, :, :], 0.0))
            for q, n in enumerate(rows):
                ins = dve.tensor_copy(lg[0:n, q, :], bank[0][0:n, NE * q:NE * (q + 1)])
            link(ins)
            for q, n in enumerate(rows):
                ins = dve.tensor_reduce(r_s[0:n, q, 0:1], lg[0:n, q, :], X, ALU.max, negate=True)
            ins.then_inc(lg_max, 1)
            for q, n in enumerate(rows):
                mine = lg[0:n, q, :].unsqueeze(2).to_broadcast([n, NE, NE])
                other = lg[0:n, q, :].unsqueeze(1).to_broadcast([n, NE, NE])
                link(dve.tensor_tensor(r_a[0:n], other, mine, ALU.is_gt))
                link(dve.tensor_tensor(r_b[0:n], other, mine, ALU.is_equal))
                link(dve.tensor_tensor(r_b[0:n], r_b[0:n], tri[0:n], ALU.mult))
                link(dve.tensor_tensor(r_a[0:n], r_a[0:n], r_b[0:n], ALU.add))
                link(dve.tensor_reduce(gate[0:n, q, :], r_a[0:n], X, ALU.add))
                link(dve.tensor_scalar(sel[0:n, q, :], gate[0:n, q, :], 1.5, None, ALU.is_lt))
            dve.sem_inc(sel_ready, 1)
            dve.wait_ge(lg_exp, 1)
            for q, n in enumerate(rows):
                link(dve.tensor_tensor(r_c[0:n, q, :], r_c[0:n, q, :], sel[0:n, q, :], ALU.mult))
                link(dve.tensor_reduce(r_s[0:n, q, 1:2], r_c[0:n, q, :], X, ALU.add))
                link(dve.reciprocal(r_s[0:n, q, 2:3], r_s[0:n, q, 1:2]))
                link(dve.tensor_scalar(gate[0:n, q, :], r_c[0:n, q, :], r_s[0:n, q, 2:3], None, ALU.mult))
            dve.wait_ge(pos_summed, 1)
            for q, n in enumerate(rows):
                link(dve.scalar_tensor_tensor(r_c[0:n, q, :], bank[1][0:n, NE * q:NE * (q + 1)], 1.0, sel[0:n, q, :], ALU.add, ALU.mult))
                link(dve.tensor_scalar(posm[0:n, q, :], r_c[0:n, q, :], -1.0, None, ALU.add))
            link(dve.tensor_reduce(r_s[:, 0, 3:4], bank[1][:, 3 * NE:4 * NE], X, ALU.max))
            dve.tensor_scalar(flag[:, :], r_s[:, 0, 3:4], SLOTS + 0.5, None, ALU.is_gt).then_inc(flag_ready, 1)
            dve.wait_ge(flag_ready, 1)
            link(dve.memset(mT[:, :, :], 0.0))
            dve.sem_inc(moe_ready, 1)
            dve.sem_inc(up_ready, 1)
            dve.sem_inc(y1_copied, 1)
            dve.sem_inc(y_added, 1)

            def expert(e, c):
                def count(per, k):
                    return e * per + (c * NE * per + k)

                dve.wait_ge(y_added, count(KC, 1))
                for q, n in enumerate(rows):
                    place = posm[0:n, q, :][:, bass.ds(e, 1)]
                    dve.tensor_scalar(disp[0:n, q, :], iota[0:n, c * SLOTS:(c + 1) * SLOTS], place, None, ALU.is_equal)
                    ins = dve.tensor_scalar(dispg[0:n, q, :], iota[0:n, c * SLOTS:(c + 1) * SLOTS], place,
                                            gate[0:n, q, :][:, bass.ds(e, 1)], ALU.is_equal, ALU.mult)
                ins.then_inc(route_built, 1)
                dve.wait_ge(gathered, count(2, 2))
                dve.tensor_copy(xeT[:, 4:8, :], bank[1][:, 0:4 * P].rearrange("p (k n) -> p k n", k=4)[:, :, 0:SLOTS]).then_inc(xe1_copied, 1)
                dve.wait_ge(comb_turned, count(1, 1))
                dve.tensor_copy(comb[0:SLOTS, :], bank[2][0:SLOTS, 0:NT]).then_inc(comb_copied, 1)
                for j in range(FCH):
                    dve.wait_ge(slab_used, used_by(e, c, 3, j))
                    dve.wait_ge(silu_done, count(FCH, j + 2))
                    dve.tensor_tensor(up[0:SLOTS, :], bank[4][0:SLOTS, :], up_s[0:SLOTS, :], ALU.mult).then_inc(up_ready, 1)
                dve.wait_ge(slab_used, used_by(e, c, 2, FCH - 1))
                dve.tensor_copy(ye[0:SLOTS, 512:1024], bank[7][0:SLOTS, :]).then_inc(y1_copied, 1)
                for k in range(KC):
                    dve.wait_ge(c_summed, count(KC, k + 1))
                    dve.tensor_tensor(mT[:, k, :], mT[:, k, :], bank[k % 2][:, 0:NT], ALU.add).then_inc(y_added, 1)

            with dve.Fori(0, NE) as e:
                expert(e, 0)
            over = dve.value_load(flag[0:1, 0:1], min_val=0, max_val=1)
            with dve.If(over > 0):
                for c in range(1, PASSES):
                    with dve.Fori(0, NE) as e:
                        expert(e, c)
            link(dve.tensor_copy(small[:, 0, 0:1], mT[:, 0, 0:1]))
            dve.sem_inc(norm_in, 1)
            normalise(7, mT)
            residual(3, h_ready)

        @block.gpsimd
        def _(pool):
            pool.wait_ge(kv_taken, 2)
            pool.dma_start(o["k_prompt"][0].rearrange("(c p) h d -> p c (h d)", p=P), ktok[:, 0:2, :]).then_inc(kv_rows, 16)
            pool.dma_start(o["k_sample"][:, 0].rearrange("b h d -> b (h d)"), ktok[0:NB, 2, :]).then_inc(kv_rows, 16)
            pool.wait_ge(kv_taken, 4)
            pool.dma_start(o["v_prompt"][0].rearrange("(c p) h d -> p c (h d)", p=P), vtok[:, 0:2, :]).then_inc(kv_rows, 16)
            pool.dma_start(o["v_sample"][:, 0].rearrange("b h d -> b (h d)"), vntok).then_inc(kv_rows, 16)
            pool.wait_ge(kv_rows, 64)
            for u in range(2 * H):
                n = P * (u % 2 + 1)
                pool.wait_ge(a_exp, u + 1)
                if u >= 1:
                    pool.wait_ge(a_turned, u)
                s = sm[u % 2]
                pool.tensor_tensor(p_sum[:, 0:n], s[:, 0, 0:n], s[:, 1, 0:n], ALU.add).then_inc(pool_step, 1)
                pool.wait_ge(pool_step, u + 1)
                pool.tensor_tensor(p_sum[:, 0:n], p_sum[:, 0:n], s[:, 2, 0:n], ALU.add).then_inc(a_sum, 1)


def shape_constants():
    import numpy as np
    t = np.zeros((P, NCONST), np.float32)

    def put(name, v):
        a, b = CONST[name]
        t[:, a:b] = np.asarray(v, np.float32).reshape(-1, b - a)

    p = np.arange(P)
    half = HD // 2
    inv = (10000.0 ** (-np.arange(half, dtype=np.float64) / half)).astype(np.float32)
    pos = np.concatenate([np.arange(T), np.full(NB, PAST)]).astype(np.float32)
    ang = (inv[p % half][:, None] * pos[None, :]).astype(np.float32)
    put("cos", np.cos(ang.astype(np.float64)))
    put("sin", np.sin(ang.astype(np.float64)))
    dist = (P + p)[:, None] - np.arange(T)[None, :]
    m = [np.where((dist >= 0) & (dist <= win) & (dist % dil == 0), 0.0, NEG) for win, dil in GROUPS]
    put("mask", np.stack(m, 1))
    put("cnt", np.tile(np.stack([1.0 / np.minimum(n, np.arange(16) + 1) for n in WIN])[None], (P, 1, 1)))
    put("ident", np.eye(P))
    r = np.zeros((P, P))
    for i in range(P):
        r[i + half if i % HD < half else i - half, i] = -1.0 if i % HD < half else 1.0
    put("rot", r)
    put("before", p[:, None] < p[None, :])
    put("ones", np.ones((P, P)))
    put("iota", np.tile(np.arange(SLOTS * PASSES), (P, 1)))
    e = np.arange(NE)
    put("tri", np.tile((e[None, :] < e[:, None]).reshape(1, -1), (P, 1)))
    put("eps", np.full((P, 1), EPS))
    return t


_INS = ["x_prompt", "x_sample", "state_pool", "cache_k", "cache_v", "c_prompt", "c_sample", "ada_mix_w", "ada_mix_b",
        "g_pre_mix", "g_post_mix", "pool_w", "pool_scale", "g_kv", "w_kv", "w_q", "w_o", "ada_ffn_w", "ada_ffn_b",
        "g_pre_ffn", "g_post_ffn", "ffn_w1", "ffn_w3", "ffn_w2", "router_w", "router_b", "moe_w1", "moe_w3", "moe_w2"]
_OUTS = [("y_prompt", (1, T, D)), ("y_sample", (NB, 1, D)), ("pool_prompt", (1, 1, STATE, D)), ("pool_sample", (NB, 1, STATE, D)),
         ("k_prompt", (1, T, H, HD)), ("v_prompt", (1, T, H, HD)), ("k_sample", (NB, 1, H, HD)), ("v_sample", (NB, 1, H, HD))]


def kernel(**inputs):
    import numpy as np
    import concourse.bacc as bacc
    from concourse.bass_utils import run_bass_kernel_spmd

    nc = bacc.Bacc("TRN2", target_bir_lowering=False, num_devices=1)
    arrays, w, o = {}, {}, {}
    for name in _INS:
        arrays[f"in_{name}"] = np.ascontiguousarray(inputs[name])
    arrays["in_shape_constants"] = shape_constants()
    for name, a in arrays.items():
        w[name[3:]] = nc.dram_tensor(name, a.shape, F32, kind="ExternalInput").ap()
    for name, shape in _OUTS:
        o[name] = nc.dram_tensor(f"out_{name}", shape, F32, kind="ExternalOutput").ap()
    yoco_step(nc, w, o)
    r = run_bass_kernel_spmd(nc, [arrays], core_ids=[0])
    return tuple(r.results[0][f"out_{name}"] for name, _ in _OUTS)
```

```python
from contextlib import ExitStack

import concourse.bass as bass
from concourse import mybir

F32 = mybir.dt.float32
F32R = mybir.dt.float32r
I32 = mybir.dt.int32
ALU = mybir.AluOpType
ACT = mybir.ActivationFunctionType
X = mybir.AxisListType.X

P = 128
D = 1024
KC = D // P
T = 256
NB = 8
NT = T + NB
PAST = 2048
GROUPS = ((128, 1), (512, 4), (2048, 16))
NG = len(GROUPS)
H, HD = 16, 64
WIN = (2, 4, 8, 16)
STATE = 15
FF = 2816
FB = FF // P
NE = 8
FE = 3584
FCH = FE // 512
EPS = 1e-6
SCALE = HD ** -0.5
RING = 7
PAIRS = 3
SLAB = 2048
SLOTS = 128
PASSES = -(-NT // SLOTS)
NEG = -1e30

CONST = {}


def _lay():
    at = 0
    for name, n in (("cos", NT), ("sin", NT), ("mask", NG * 256), ("cnt", 4 * 16), ("ident", P), ("rot", P),
                    ("before", P), ("ones", P), ("iota", SLOTS * PASSES), ("tri", NE * NE), ("eps", 1)):
        CONST[name] = (at, at + n)
        at += n
    return at


NCONST = _lay()


def slab_plan():
    plan = []
    ada = [[("ada", s, r, 4, c, 512) for c in range(0, 3 * D, 512) for r in (0, 4)] for s in range(4)]
    plan += ada[0] + ada[1]
    for c in range(0, FF, 256):
        plan += [("w1", 0, 0, KC, c, 256), ("w3", 0, 0, KC, c, 256)]
    for c in range(0, D, 256):
        plan += [("w2", 0, r, min(8, FB - r), c, 256) for r in range(0, FB, 8)]
    plan += ada[2]
    plan += [("wkv", 0, 0, KC, c, 256) for c in range(0, 2 * D, 256)]
    plan += [("wq", 0, 0, KC, c, 256) for c in range(0, NG * D, 256)]
    plan += [("ck", t, 0, 2, 0, D) for t in range(0, NB * NG, 2)]
    plan += [("cv", t, 0, 2, 0, D) for t in range(0, NB * NG, 2)]
    plan += [("wo", 0, 0, KC, c, 256) for c in range(0, D, 256)]
    plan += ada[3]
    return plan


def yoco_step(nc, w, o):
    plan = slab_plan()
    first = {}
    for n, item in enumerate(plan):
        first.setdefault(item[:2], n)
    NPRE = len(plan)
    dmas = [2 if item[0] in ("ck", "cv") else 1 for item in plan]
    split = [n for n, item in enumerate(plan) if item[0] not in ("ck", "cv")]
    cache = [n for n, item in enumerate(plan) if item[0] in ("ck", "cv")]
    order = {n: i for part in (split, cache) for i, n in enumerate(part)}
    firsts = {}
    for i, n in enumerate(split):
        firsts.setdefault(plan[n][:2], i)
    NSPLIT = len(split)
    eslabs = []
    for j in range(FCH):
        eslabs += [(1, j, 0), (1, j, 1), (3, j, 0), (3, j, 1)] + ([(2, j - 1, 0), (2, j - 1, 1)] if j else [])
    eslabs += [(2, FCH - 1, 0), (2, FCH - 1, 1)]
    PER_E = len(eslabs)
    assert PER_E % RING == 0 and PER_E % PAIRS == 0
    assert all(n in order and plan[n][0] not in ("ck", "cv") for n in range(NPRE - RING, NPRE))

    with ExitStack() as ctx:
        free = [-(-nc.sbuf_base // 64) * 64]
        placed = {}

        def sb(name, shape, dt=F32):
            n = 4
            for x in shape[1:]:
                n *= x
            placed[name] = free[0]
            free[0] += -(-n // 64) * 64
            return nc.alloc_sbuf_tensor_at(name, shape, dt, offset=placed[name])

        def over(name, other, skip, shape, dt):
            return nc.alloc_sbuf_tensor_at(name, shape, dt, offset=placed[other] + 4 * skip)

        def sem(name):
            return ctx.enter_context(nc.semaphore(name))

        bank = [ctx.enter_context(nc.psum_tensor(f"bank{i}", [P, 512], F32)) for i in range(8)]

        ring = sb("ring", [P, RING, SLAB])
        w_hi = sb("w_hi", [P, PAIRS, SLAB], F32R)
        w_lo = sb("w_lo", [P, PAIRS, SLAB], F32R)
        const = sb("const", [P, NCONST])

        def cst(name):
            a, b = CONST[name]
            return const[:, a:b]

        cos, sin, ident, rot, before, ones, iota = (cst(n) for n in ("cos", "sin", "ident", "rot", "before", "ones", "iota"))
        one1 = ones[:, 0:1]
        eps1 = cst("eps")
        mask = cst("mask").rearrange("p (g k) -> p g k", g=NG)
        invcnt = cst("cnt").rearrange("p (g k) -> p g k", g=4)
        tri = cst("tri").rearrange("p (a b) -> p a b", a=NE)

        xT = sb("xT", [P, KC, NT])
        hT = sb("hT", [P, KC, NT])
        mT = sb("mT", [P, KC, NT])
        tT = sb("tT", [P, KC, NT])
        ada = sb("ada", [P, 4, 24, 1 + NB])
        vec1 = sb("vec1", [P, 96])
        vec2 = sb("vec2", [P, 80])
        vrow1 = sb("vrow1", [96, P])
        vrow2 = sb("vrow2", [80, P])
        cT = sb("cT", [P, KC, 1 + NB])
        c18 = sb("c18", [P, KC, 18], F32R)
        tHi = over("tHi", "tT", 0, [P, KC, NT], F32R)
        mLo = over("mLo", "mT", 0, [P, KC, NT], F32R)
        hLo = over("hLo", "hT", 0, [P, KC, NT], F32R)
        shared = sb("shared", [P, 4 * NT])
        arow = shared[0:18, 0:1024].rearrange("p (a n) -> p a n", a=2)
        g_new = shared[:, :].rearrange("p (a n) -> p a n", a=4)
        std = sb("std", [P, NT])
        rstd = sb("rstd", [P, NT])
        small = sb("small", [P, KC, NB])
        rw = sb("rw", [P, KC, NE])
        rb = sb("rb", [1, NE])
        flag = sb("flag", [P, 1], I32)
        PHASE = 12300
        phase = sb("phase", [P, PHASE])
        places = {}

        def at(offset, *shape):
            n = 1
            for s in shape:
                n *= s
            assert offset + n <= PHASE, (offset, shape)
            v = phase[:, offset:offset + n]
            if len(shape) == 2:
                v = v.rearrange("p (a b) -> p a b", a=shape[0])
            if len(shape) == 3:
                v = v.rearrange("p (a b c) -> p a b c", a=shape[0], b=shape[1])
            if len(shape) == 4:
                v = v.rearrange("p (a b c d) -> p a b c d", a=shape[0], b=shape[1], c=shape[2])
            return v

        EXT = STATE + T
        xtok = at(0, 3, D)
        crow = at(3072, D)
        strow = at(4096, D)
        ext = at(5120, KC, EXT)
        sExt = at(5120 + KC * EXT, KC, NB, STATE + 1)
        sum_a = at(0, KC, EXT)
        sum_b = at(KC * EXT, KC, EXT)
        ext = at(2 * KC * EXT, KC, EXT)
        sExt = at(3 * KC * EXT, KC, NB, STATE + 1)
        poolw = at(3 * KC * EXT + KC * NB * (STATE + 1), 4, 2, 256)
        pstate = at(0, D)
        gHi = over("gHi", "phase", 0, [P, FB, NT], F32R)
        gLo = over("gLo", "phase", FB * NT, [P, FB, NT], F32R)
        silu_up = at(2 * FB * NT, 2, NT)
        kT = at(0, KC, NT)
        vtok = at(KC * NT, 2, D)
        vnew = at(KC * NT + 2 * D, KC, NB)
        qT = at(KC * NT + 2 * D + KC * NB, NG * KC, NT)
        ktok = qT.rearrange("p a b -> p (a b)")[:, 0:3 * D].rearrange("p (a b) -> p a b", a=3)
        vntok = qT.rearrange("p a b -> p (a b)")[0:NB, 3 * D:4 * D]
        vraw = qT.rearrange("p a b -> p (a b)")[:, 4 * D:4 * D + KC * NT].rearrange("p (a b) -> p a b", a=KC)
        QEND = KC * NT + 2 * D + KC * NB + NG * KC * NT
        woT = at(0, KC, NT)
        hflat = hT[:, :, :].rearrange("p a b -> p (a b)")
        tflat = tT[:, :, :].rearrange("p a b -> p (a b)")
        qpair = hflat[:, 0:384].rearrange("p (g b j s) -> p g b j s", g=NG, b=NB, j=KC)
        kprod = hflat[:, 384:768].rearrange("p (g b j s) -> p g b j s", g=NG, b=NB, j=KC)
        s_scores = hflat[:, 768:1152].rearrange("p (g n) -> p g n", g=NG)
        s_soft = hflat[:, 1152:1152 + 387]
        s_pT = hflat[:, 1540:1924].rearrange("p (g n) -> p g n", g=NG)
        pnewb = hflat[:, 1924:1924 + P]
        s_stat = hflat[:, 2060:2064]
        kTs = tflat[:, 0:2048].rearrange("p (a b) -> p a b", a=2)
        otok = hflat[:, 0:2048].rearrange("p (c n) -> p c n", c=2)
        sm = [tflat[:, 768 * i:768 * (i + 1)].rearrange("p (g k) -> p g k", g=NG) for i in range(2)]
        rot_a, rot_b = at(QEND, NT), at(QEND + NT, NT)
        rawT = at(QEND + 2 * NT, 4, NT)
        p_sum = at(QEND, 256)
        p_stat = at(QEND + 256, 4, 4)
        p_T = at(QEND + 272, 2, P)
        htok_hi = over("htok_hi", "phase", 0, [P, 3, D], F32R)
        htok_lo = over("htok_lo", "phase", 8192, [P, 3, D], F32R)
        xe_hi = over("xe_hi", "phase", 3072, [P, KC, SLOTS], F32R)
        xe_lo = over("xe_lo", "phase", 11264, [P, KC, SLOTS], F32R)
        upT_hi = over("upT_hi", "tT", 0, [P, 4, P], F32R)
        upT_lo = over("upT_lo", "tT", 512, [P, 4, P], F32R)
        up_s = at(4096, 512)
        up = at(4608, 512)
        ye = at(5632, D)
        disp = over("disp", "phase", 6656, [P, 3, SLOTS], F32R)
        dispg = at(7040, 3, SLOTS)
        comb = at(7424, NT)
        lg = at(7688, 3, NE)
        sel = at(7712, 3, NE)
        posm = at(7736, 3, NE)
        gate = at(7760, 3, NE)
        r_a = at(7784, NE, NE)
        r_b = at(7848, NE, NE)
        r_c = at(7912, 3, NE)
        r_s = at(7936, 3, 4)
        ytok = at(0, 3, D)

        slab_in = [sem(f"slab_in{i}") for i in range(RING)]
        hi_done, lo_done, lo_done_pool = sem("hi_done"), sem("lo_done"), sem("lo_done_pool")
        pair_used = sem("pair_used")
        cache_used = sem("cache_used")
        arow_ready, ada_turned, c_split = sem("arow_ready"), sem("ada_turned"), sem("c_split")
        act_hi, act_lo = sem("act_hi"), sem("act_lo")
        g_hi, g_lo = sem("g_hi"), sem("g_lo")
        xe_hi_ready, xe_ready, upT_hi_ready, upT_ready = (sem(n) for n in ("xe_hi_ready", "xe_ready", "upT_hi_ready", "upT_ready"))
        in_const, in_vec, in_x, in_state, in_pool, in_router = (sem(n) for n in (
            "in_const", "in_vec", "in_x", "in_state", "in_pool", "in_router"))
        act_step, dve_step, pool_step = sem("act_step"), sem("dve_step"), sem("pool_step")
        vec_turned, vec_read = sem("vec_turned"), sem("vec_read")
        c_silu, c_turned, c_read = sem("c_silu"), sem("c_turned"), sem("c_read")
        x_turned, x_taken = sem("x_turned"), sem("x_taken")
        st_turned, st_taken = sem("st_turned"), sem("st_taken")
        ada_taken = sem("ada_taken")
        norm_in, sq_ready, norm_summed, std_ready = sem("norm_in"), sem("sq_ready"), sem("norm_summed"), sem("std_ready")
        h_ready = sem("h_ready")
        ext_ready, pm_ready, pool_summed, pool_taken = sem("ext_ready"), sem("pm_ready"), sem("pool_summed"), sem("pool_taken")
        ps_turned, ps_taken = sem("ps_turned"), sem("ps_taken")
        fup_silu, fup_done = sem("fup_silu"), sem("fup_done")
        fdn_taken = sem("fdn_taken")
        lin_raw, rot_summed, rot_done = sem("lin_raw"), sem("rot_summed"), sem("rot_done")
        kv_turned, kv_taken = sem("kv_turned"), sem("kv_taken")
        pair_ready = sem("pair_ready")
        kt_turned, kt_lo, kt_hi, s_summed, s_taken, s_turned = (sem(n) for n in (
            "kt_turned", "kt_lo", "kt_hi", "s_summed", "s_taken", "s_turned"))
        s_max, s_exp, s_prob, sp_turned, sp_taken, pn_ready, pn_spread, sv_summed, sv_done = (sem(n) for n in (
            "s_max", "s_exp", "s_prob", "sp_turned", "sp_taken", "pn_ready", "pn_spread", "sv_summed", "sv_done"))
        a_scored, a_max, a_exp, a_sum, a_turned, a_copied, a_out, a_taken = (sem(n) for n in (
            "a_scored", "a_max", "a_exp", "a_sum", "a_turned", "a_copied", "a_out", "a_taken"))
        ot_turned, ot_taken = sem("ot_turned"), sem("ot_taken")
        wo_taken = sem("wo_taken")
        lg_summed, lg_max, lg_exp, sel_ready, pos_summed = (sem(n) for n in (
            "lg_summed", "lg_max", "lg_exp", "sel_ready", "pos_summed"))
        ht_turned, ht_hi, ht_taken = sem("ht_turned"), sem("ht_hi"), sem("ht_taken")
        moe_ready, flag_ready = sem("moe_ready"), sem("flag_ready")
        route_built, gathered, comb_turned, comb_copied = (sem(n) for n in (
            "route_built", "gathered", "comb_turned", "comb_copied"))
        silu_done, up_ready, up_turned = (sem(n) for n in ("silu_done", "up_ready", "up_turned"))
        y0_copied, y1_copied, c_summed, y_added = (sem(n) for n in ("y0_copied", "y1_copied", "c_summed", "y_added"))
        moe_done = sem("moe_done")
        y_turned, y_taken = sem("y_turned"), sem("y_taken")
        out_done, moved_up = sem("out_done"), sem("moved_up")
        kv_rows, ps_rows, y_rows = sem("kv_rows"), sem("ps_rows"), sem("y_rows")

        def slab_source(item):
            name, k, r, nr, c, ncol = item
            a = {"ada": lambda: (w["ada_mix_w"], w["ada_ffn_w"])[k % 2][k // 2], "w1": lambda: w["ffn_w1"][0],
                 "w3": lambda: w["ffn_w3"][0], "w2": lambda: w["ffn_w2"][0], "wkv": lambda: w["w_kv"],
                 "wq": lambda: w["w_q"][0], "wo": lambda: w["w_o"][0]}[name]()
            return a[r * P:(r + nr) * P, c:c + ncol].rearrange("(k p) n -> p k n", p=P)

        def slab_view(n):
            name, k, r, nr, c, ncol = plan[n]
            return ring[:, n % RING, 0:nr * ncol].rearrange("p (k n) -> p k n", k=nr)

        def slab_total(n):
            return 16 * sum(dmas[m] for m in range(n % RING, n + 1, RING))

        before_experts = [16 * sum(dmas[m] for m in range(r, NPRE, RING)) for r in range(RING)]

        def expert_source(e, m, j, half):
            if m == 2:
                rows = slice(512 * j + 256 * half, 512 * j + 256 * (half + 1))
                return w["moe_w2"][0, bass.ds(e, 1), rows, :].rearrange("a (k p) n -> p (a k) n", p=P)
            return w[f"moe_w{m}"][0, bass.ds(e, 1), 512 * half:512 * (half + 1), 512 * j:512 * (j + 1)].rearrange("a (k p) n -> p (a k) n", p=P)

        def used_by(e, c, m, j, half=1):
            return e * PER_E + (NSPLIT + c * NE * PER_E + eslabs.index((m, j, half)) + 1)

        def owner(i):
            return "vector"

        def lows(i, who):
            return sum(owner(m) == who for m in range(i + 1))

        LO_PRE = lows(NSPLIT - 1, "vector")
        assert all(owner(i) == "vector" for i in range(NSPLIT - RING, NSPLIT))

        def need_split(eng, i):
            if owner(i) == "vector":
                eng.wait_ge(lo_done, lows(i, "vector"))
            else:
                eng.wait_ge(lo_done_pool, lows(i, "pool"))

        def parts(i):
            name, k, r, nr, c, ncol = plan[split[i]]
            return [t[:, i % PAIRS, 0:nr * ncol].rearrange("p (k n) -> p k n", k=nr) for t in (w_hi, w_lo)]

        def remainder(eng, i, done):
            n = split[i]
            size = plan[n][3] * plan[n][5]
            eng.wait_ge(hi_done, i + 1)
            eng.tensor_tensor(w_lo[:, i % PAIRS, 0:size], ring[:, n % RING, 0:size], w_hi[:, i % PAIRS, 0:size].bitcast(F32),
                              ALU.subtract).then_inc(done, 1)

        block = ctx.enter_context(nc.Block())

        @block.sync
        def _(sp):
            sp.dma_start(const[:, :], w["shape_constants"]).then_inc(in_const, 16)
            sp.dma_start(crow[0:1, :], w["c_prompt"]).then_inc(in_vec, 16)
            sp.dma_start(crow[1:9, :], w["c_sample"]).then_inc(in_vec, 16)
            sp.dma_start(vrow1[0:48, :], w["ada_mix_b"].rearrange("l (m p) -> (l m) p", p=P)).then_inc(in_vec, 16)
            sp.dma_start(vrow1[48:96, :], w["ada_ffn_b"].rearrange("l (m p) -> (l m) p", p=P)).then_inc(in_vec, 16)
            for i, name in enumerate(("g_pre_mix", "g_post_mix", "g_pre_ffn", "g_post_ffn")):
                sp.dma_start(vrow2[16 * i:16 * (i + 1), :], w[name].rearrange("l (m p) -> (l m) p", p=P)).then_inc(in_vec, 16)
            sp.dma_start(vrow2[64:72, :], w["g_kv"].rearrange("(m p) -> m p", p=P)).then_inc(in_vec, 16)
            sp.dma_start(vrow2[72:80, :], w["pool_scale"][0].rearrange("(m p) -> m p", p=P)).then_inc(in_vec, 16)
            sp.dma_start(xtok[:, 0:2, :], w["x_prompt"][0].rearrange("(c p) d -> p c d", p=P)).then_inc(in_x, 16)
            sp.dma_start(xtok[0:NB, 2, :], w["x_sample"][:, 0, :]).then_inc(in_x, 16)
            for n, item in enumerate(plan):
                if n >= RING:
                    m = n - RING
                    if m in cache:
                        sp.wait_ge(cache_used, order[m] + 1)
                    else:
                        need_split(sp, order[m])
                if item[0] in ("ck", "cv"):
                    rows = w["cache_k" if item[0] == "ck" else "cache_v"]
                    for q in range(2):
                        b, dil = (item[1] + q) // NG, GROUPS[(item[1] + q) % NG][1]
                        sp.dma_start(slab_view(n)[:, q, :], rows[b, PAST - P * dil::dil].rearrange("t h d -> t (h d)"))\
                          .then_inc(slab_in[n % RING], 16)
                else:
                    sp.dma_start(slab_view(n), slab_source(item)).then_inc(slab_in[n % RING], 16)
                if n == RING - 1:
                    sp.dma_start(strow[0:NB * STATE, :], w["state_pool"][:, 0].rearrange("b t d -> (b t) d")).then_inc(in_state, 16)
                    sp.dma_start(poolw[:, :, :, :], w["pool_w"][0].rearrange("g (k p) n -> p g k n", p=P)).then_inc(in_pool, 16)
                    sp.dma_start(rw[:, :, :], w["router_w"][0].rearrange("(k p) n -> p k n", p=P)).then_inc(in_router, 16)
                    sp.dma_start(rb[:, :], w["router_b"]).then_inc(in_router, 16)

            def experts(e, c):
                for k, (m, j, half) in enumerate(eslabs):
                    slot = (NPRE + k) % RING
                    sp.wait_ge(lo_done, e * PER_E + (LO_PRE + c * NE * PER_E + k - RING + 1))
                    sp.dma_start(ring[:, slot, :].rearrange("p (k n) -> p k n", k=(2 if m == 2 else 4)), expert_source(e, m, j, half))\
                      .then_inc(slab_in[slot], 16)

            with sp.Fori(0, NE) as e:
                experts(e, 0)
            sp.wait_ge(flag_ready, 1)
            over = sp.value_load(flag[0:1, 0:1], min_val=0, max_val=1)
            with sp.If(over > 0):
                for c in range(1, PASSES):
                    with sp.Fori(0, NE) as e:
                        experts(e, c)

        @block.tensor
        def _(pe):
            def need_slab(n):
                pe.wait_ge(slab_in[n % RING], slab_total(n))

            def three(out, a, b, start, stop):
                pe.matmul(out, a[0], b[0], start=start, stop=False, skip_group_check=True)
                pe.matmul(out, a[0], b[1], start=False, stop=False, skip_group_check=True)
                return pe.matmul(out, a[1], b[0], start=False, stop=stop, skip_group_check=True)

            pe.wait_ge(in_const, 16)
            pe.wait_ge(in_vec, 16 * 10)
            pe.transpose(bank[0][:, 0:96], vrow1[:, :], ident[0:96, 0:96])
            pe.transpose(bank[0][:, 96:176], vrow2[:, :], ident[0:80, 0:80]).then_inc(vec_turned, 1)
            pe.wait_ge(c_silu, 1)
            for k in range(KC):
                mm = pe.transpose(bank[1][:, 9 * k:9 * k + 9], crow[0:9, P * k:P * (k + 1)], ident[0:9, 0:9])
            mm.then_inc(c_turned, 1)
            pe.wait_ge(in_x, 32)
            for k in range(KC):
                if k >= 2:
                    pe.wait_ge(x_taken, k - 1)
                b = bank[2 + k % 2]
                for c, n in ((0, P), (1, P), (2, NB)):
                    mm = pe.transpose(b[:, c * P:c * P + n], xtok[0:n, c, P * k:P * (k + 1)], ident[0:n, 0:n])
                mm.then_inc(x_turned, 1)
            pe.wait_ge(in_state, 16)
            for k in range(KC):
                if k >= 2:
                    pe.wait_ge(st_taken, k - 1)
                pe.transpose(bank[4 + k % 2][:, 0:120], strow[0:120, P * k:P * (k + 1)], ident[0:120, 0:120])\
                  .then_inc(st_turned, 1)

            def ada_products(s):
                i0 = firsts[("ada", s)]

                def columns(j):
                    pe.wait_ge(arow_ready, 6 * s + j + 1)
                    if s >= 1 and j == 0:
                        pe.wait_ge(ada_taken, s)
                    for m in range(4):
                        mm = pe.transpose(bank[6][:, 18 * (4 * j + m):18 * (4 * j + m + 1)], arow[:, j % 2, P * m:P * (m + 1)], ident[0:18, 0:18])
                    mm.then_inc(ada_turned, 1)

                if s == 0:
                    pe.wait_ge(c_split, 1)
                    pe.wait_ge(x_taken, KC)
                for j in range(6):
                    if 6 * s + j >= 2:
                        pe.wait_ge(arow_ready, 6 * s + j - 1)
                    out = bank[2 + j % 2]
                    for half in range(2):
                        i = i0 + 2 * j + half
                        need_split(pe, i)
                        hi, lo = parts(i)
                        for k in range(4):
                            pe.matmul(out[0:18, :], c18[:, 4 * half + k, :], hi[:, k, :], start=(half == 0 and k == 0), stop=False, skip_group_check=True)
                            mm = pe.matmul(out[0:9, :], c18[:, 4 * half + k, 0:9], lo[:, k, :], start=False, stop=(half == 1 and k == 3), skip_group_check=True)
                        mm.then_inc(pair_used, 1)
                    if j >= 1:
                        columns(j - 1)
                columns(5)

            def norm_sum(i):
                pe.wait_ge(sq_ready, i + 1)
                for k in range(KC):
                    mm = pe.matmul(bank[7][:, 0:NT], ones, tT[:, k, :], start=(k == 0), stop=(k == KC - 1))
                mm.then_inc(norm_summed, 1)

            ada_products(0)
            norm_sum(0)
            ada_products(1)
            pe.wait_ge(in_pool, 16)
            pe.wait_ge(pm_ready, 1)
            for i in range(KC):
                g, m = i // 2, i % 2
                if i >= 2:
                    pe.wait_ge(pool_taken, i - 1)
                for k in range(2):
                    mm = pe.matmul(bank[i % 2][:, 0:NT], poolw[:, g, k, P * m:P * (m + 1)], tT[:, 2 * g + k, :],
                                   start=(k == 0), stop=(k == 1))
                mm.then_inc(pool_summed, 1)
            for k in range(KC):
                mm = pe.transpose(bank[4 + k // 4][0:STATE + NB, P * (k % 4):P * (k % 4 + 1)], hT[:, k, T - STATE:NT], ident)
            mm.then_inc(ps_turned, 1)
            norm_sum(1)
            norm_sum(2)
            def block_pair(i, a, banks, k0=0, first_k=True, last_k=True):
                need_split(pe, i)
                hi, lo = parts(i)
                nr = plan[split[i]][3]
                for m in range(2):
                    for k in range(nr):
                        mm = three(bank[banks[m]][:, 0:NT], (hi[:, k, P * m:P * (m + 1)], lo[:, k, P * m:P * (m + 1)]),
                                   (a[0][:, k0 + k, :], a[1][:, k0 + k, :]), first_k and k == 0, last_k and k == nr - 1)
                mm.then_inc(pair_used, 1)

            pe.wait_ge(act_lo, 1)
            i0 = firsts[("w1", 0)]
            for c in range(FB // 2):
                if c >= 2:
                    pe.wait_ge(fup_done, 2 * (c - 1))
                b = 4 * (c % 2)
                block_pair(i0 + 2 * c, (tHi, mLo), (b, b + 1))
                block_pair(i0 + 2 * c + 1, (tHi, mLo), (b + 2, b + 3))
            i0 = firsts[("w2", 0)]
            pe.wait_ge(fup_done, FB)
            pe.wait_ge(g_lo, FB)
            for c in range(4):
                if c >= 2:
                    pe.wait_ge(fdn_taken, 2 * (c - 1))
                for r in range(3):
                    block_pair(i0 + 3 * c + r, (gHi, gLo), ((0, 1), (4, 5))[c % 2], 8 * r, r == 0, r == 2)
            ada_products(2)
            norm_sum(3)
            norm_sum(4)

            def rotate(i):
                if i >= 2:
                    pe.wait_ge(rot_done, i - 1)
                pe.wait_ge(lin_raw, i + 1 + (KC if i >= KC else 0))
                pe.matmul(bank[4 + i % 2][:, 0:NT], rot, rawT[:, i % 4, :], start=True, stop=True).then_inc(rot_summed, 1)

            def lin_pair(i, c):
                if c >= 2:
                    pe.wait_ge(lin_raw, 2 * (c - 1))
                b = 2 * (c % 2)
                block_pair(i, (tHi, mLo), (b, b + 1))

            pe.wait_ge(act_lo, 2)
            for c in range(8):
                lin_pair(firsts[("wkv", 0)] + c, c)
                if 1 <= c <= 4:
                    rotate(2 * c - 2)
                    rotate(2 * c - 1)
            for q in range(4):
                if q == 0:
                    pe.wait_ge(rot_done, KC)
                if q == 2:
                    pe.wait_ge(lin_raw, 2 * KC)
                if q >= 1:
                    pe.wait_ge(kv_taken, q)
                for m in range(4):
                    k = 4 * (q % 2) + m
                    src = (kT if q < 2 else vraw)
                    for c, n in ((0, P), (1, P), (2, NB)):
                        mm = pe.transpose(bank[(4, 5, 7)[c]][0:n, P * m:P * (m + 1)], src[:, k, c * P:c * P + n], ident)
                mm.then_inc(kv_turned, 1)
            pe.wait_ge(kv_taken, 4)
            pe.wait_ge(act_lo, 3)
            for c in range(12):
                lin_pair(firsts[("wq", 0)] + c, 8 + c)
                if c >= 1:
                    rotate(KC + 2 * c - 2)
                    rotate(KC + 2 * c - 1)
            rotate(KC + 22)
            rotate(KC + 23)

            pe.wait_ge(pair_ready, 1)
            for g in range(NG):
                mm = pe.matmul(bank[5][:, g:g + 1], kprod[:, g].rearrange("p b j s -> p (b j s)"), one1, start=True, stop=True)
            NTILE = NB * NG

            def key_scores(t):
                b, g = t // NG, t % NG
                pe.wait_ge(kt_lo, t + 1)
                pe.wait_ge(kt_hi, t + 1)
                for j in range(KC):
                    c = (b * KC + j) * 2
                    mm = pe.matmul(bank[4][:, P * g + c:P * g + c + 2], kTs[:, t % 2, P * j:P * (j + 1)], qpair[:, g, b, j, :],
                                   start=True, stop=True)
                mm.then_inc(s_summed, 1)

            for t in range(NTILE):
                b, g = t // NG, t % NG
                n = first[("ck", 0)] + t // 2
                need_slab(n)
                if t >= 2:
                    pe.wait_ge(kt_lo, t - 1)
                    pe.wait_ge(kt_hi, t - 1)
                for j in range(KC):
                    mm = pe.transpose(bank[2 * (t % 2) + j // 4][:, P * (j % 4):P * (j % 4 + 1)],
                                      slab_view(n)[:, t % 2, P * j:P * (j + 1)], ident)
                mm.then_inc(kt_turned, 1)
                if t % 2 == 1:
                    pe.matmul(bank[7][0:1, 0:1], one1, one1, start=True, stop=True).then_inc(cache_used, 1)
                if t >= 1:
                    key_scores(t - 1)
            key_scores(NTILE - 1)
            pe.wait_ge(s_taken, 1)
            for g in range(NG):
                mm = pe.transpose(bank[6][:, P * g:P * (g + 1)], s_scores[:, g, :], ident)
            mm.then_inc(s_turned, 1)
            pe.wait_ge(s_prob, 1)
            for g in range(NG):
                mm = pe.transpose(bank[7][:, P * g:P * (g + 1)], s_soft[:, P * g:P * (g + 1)], ident)
            mm.then_inc(sp_turned, 1)
            pe.wait_ge(pn_ready, 1)
            pe.matmul(bank[5][:, P:2 * P], pnewb, ident, start=True, stop=True).then_inc(pn_spread, 1)
            pe.wait_ge(sp_taken, 1)
            for b in range(NB):
                for g in range(NG):
                    need_slab(first[("cv", 0)] + (NG * b + g) // 2)
                for j in range(KC):
                    c = (b * KC + j) * 2
                    for g in range(NG):
                        t = NG * b + g
                        mm = pe.matmul(bank[4][:, c:c + 2], slab_view(first[("cv", 0)] + t // 2)[:, t % 2, P * j:P * (j + 1)],
                                       s_pT[:, g, c:c + 2], start=(g == 0), stop=(g == NG - 1))
                if b % 2 == 0:
                    mm.then_inc(cache_used, 1)
                else:
                    mm.then_inc(cache_used, 2)
            pe.matmul(bank[5][0:1, 300:301], one1, one1, start=True, stop=True).then_inc(sv_summed, 1)

            units = [(h, c) for h in range(H) for c in range(2)]

            def scores(u):
                h, c = units[u]
                lo = HD * (h % 2)
                if u >= 2:
                    pe.wait_ge(a_max, u - 1)
                for g in range(NG):
                    b = bank[2 * c + g // 2]
                    n = P * (c + 1)
                    mm = pe.matmul(b[:, 256 * (g % 2):256 * (g % 2) + n], qT[lo:lo + HD, g * KC + h // 2, c * P:(c + 1) * P],
                                   kT[lo:lo + HD, h // 2, 0:n], start=True, stop=True)
                mm.then_inc(a_scored, 1)

            def weights_to_columns(u):
                h, c = units[u]
                pe.wait_ge(a_sum, u + 1)
                if u >= 1:
                    pe.wait_ge(a_copied, u)
                for k in range(c + 1):
                    mm = pe.transpose(bank[4][:, P * k:P * (k + 1)], p_sum[:, P * k:P * (k + 1)], ident)
                mm.then_inc(a_turned, 1)

            def values(u):
                h, c = units[u]
                pe.wait_ge(a_copied, u + 1)
                if u >= 2:
                    pe.wait_ge(a_taken, u - 1)
                for k in range(c + 1):
                    mm = pe.matmul(bank[6 + u % 2][:, 0:HD], p_T[:, k, :], vtok[:, k, HD * h:HD * (h + 1)],
                                   start=(k == 0), stop=(k == c))
                mm.then_inc(a_out, 1)

            pe.wait_ge(sv_done, 1)
            for u in range(len(units) + 2):
                if u < len(units):
                    scores(u)
                if 1 <= u <= len(units):
                    weights_to_columns(u - 1)
                if u >= 2:
                    values(u - 2)
            pe.wait_ge(a_taken, len(units))
            for k in range(KC):
                if k >= 2:
                    pe.wait_ge(ot_taken, k - 1)
                for c in range(2):
                    mm = pe.transpose(bank[k % 2][:, P * c:P * (c + 1)], otok[:, c, P * k:P * (k + 1)], ident)
                mm.then_inc(ot_turned, 1)
            pe.wait_ge(act_lo, 4)
            for c in range(4):
                if c >= 2:
                    pe.wait_ge(wo_taken, 2 * (c - 1))
                block_pair(firsts[("wo", 0)] + c, (tHi, hLo), ((2, 3), (4, 5))[c % 2])
            pe.wait_ge(wo_taken, KC)
            ada_products(3)
            norm_sum(5)
            norm_sum(6)

            pe.wait_ge(h_ready, 4)
            pe.wait_ge(in_router, 32)
            for c, n in ((0, P), (1, P), (2, NB)):
                for k in range(KC):
                    pe.matmul(bank[0][0:n, NE * c:NE * (c + 1)], hT[:, k, P * c:P * c + n], rw[:, k, :], start=(k == 0), stop=False)
                mm = pe.matmul(bank[0][0:n, NE * c:NE * (c + 1)], ones[0:1, 0:n], rb[0:1, :], start=False, stop=True)
            mm.then_inc(lg_summed, 1)
            for k in range(KC):
                if k >= 2:
                    pe.wait_ge(ht_taken, k - 1)
                for c, n in ((0, P), (1, P), (2, NB)):
                    mm = pe.transpose(bank[2 + k % 2][0:n, P * c:P * (c + 1)], hT[:, k, c * P:c * P + n], ident)
                mm.then_inc(ht_turned, 1)
            pe.wait_ge(sel_ready, 1)
            rows = (P, P, NB)
            for c in range(3):
                for k in range(c + 1):
                    n = rows[k]
                    pe.matmul(bank[1][0:rows[c], NE * c:NE * (c + 1)], (before if k == c else ones)[0:n, 0:rows[c]], sel[0:n, k, :],
                              start=(k == 0), stop=(k == c))
            for k in range(3):
                mm = pe.matmul(bank[1][:, 3 * NE:4 * NE], ones[0:rows[k], :], sel[0:rows[k], k, :], start=(k == 0), stop=(k == 2))
            mm.then_inc(pos_summed, 1)
            pe.wait_ge(ht_taken, KC)
            pe.wait_ge(moe_ready, 1)

            def expert(e, c):
                def weights(m, j, half, rows):
                    k = eslabs.index((m, j, half))
                    pe.wait_ge(lo_done, e * PER_E + (LO_PRE + c * NE * PER_E + k + 1))
                    return [t[:, (NSPLIT + k) % PAIRS, :].rearrange("p (k n) -> p k n", k=rows) for t in (w_hi, w_lo)]

                def count(per, k):
                    return e * per + (c * NE * per + k)

                pe.wait_ge(route_built, count(1, 1))
                pe.wait_ge(y_added, count(KC, 1))
                for k in range(KC):
                    for q in range(3):
                        n = rows[q]
                        for part, last in ((htok_hi, False), (htok_lo, q == 2)):
                            mm = pe.matmul(bank[k // 4][:, P * (k % 4):P * (k % 4) + SLOTS], part[0:n, q, P * k:P * (k + 1)], disp[0:n, q, :],
                                           start=(q == 0 and part is htok_hi), stop=last)
                    if k % 4 == 3:
                        mm.then_inc(gathered, 1)
                for q in range(3):
                    n = rows[q]
                    mm = pe.transpose(bank[2][0:SLOTS, P * q:P * q + n], dispg[0:n, q, :], ident[0:n, 0:n])
                mm.then_inc(comb_turned, 1)

                def product(m, j, bk):
                    for half in range(2):
                        hi, lo = weights(m, j, half, 4)
                        for i in range(4):
                            k = 4 * half + i
                            mm = three(bank[bk][0:SLOTS, :], (xe_hi[:, k, :], xe_lo[:, k, :]), (hi[:, i, :], lo[:, i, :]), k == 0, k == KC - 1)
                        mm.then_inc(pair_used, 1)

                def turn(j):
                    pe.wait_ge(up_ready, count(FCH, j + 2))
                    pe.wait_ge(upT_ready, count(FCH, j + 1))
                    for i in range(4):
                        mm = pe.transpose(bank[5][:, SLOTS * i:SLOTS * (i + 1)], up[0:SLOTS, P * i:P * (i + 1)], ident[0:SLOTS, 0:SLOTS])
                    mm.then_inc(up_turned, 1)

                def down(j):
                    pe.wait_ge(upT_ready, count(FCH, j + 2))
                    if j == 0:
                        pe.wait_ge(y0_copied, count(1, 1))
                        pe.wait_ge(y1_copied, count(1, 1))
                    for half in range(2):
                        hi, lo = weights(2, j, half, 2)
                        for i in range(2):
                            for q in range(2):
                                cols = slice(512 * q, 512 * (q + 1))
                                mm = three(bank[6 + q][0:SLOTS, :], (upT_hi[:, 2 * half + i, :], upT_lo[:, 2 * half + i, :]),
                                           (hi[:, i, cols], lo[:, i, cols]), j == 0 and half == 0 and i == 0, j == FCH - 1 and half == 1 and i == 1)
                        mm.then_inc(pair_used, 1)

                pe.wait_ge(xe_ready, count(1, 1))
                for j in range(FCH):
                    pe.wait_ge(silu_done, count(FCH, j + 1))
                    product(1, j, 3)
                    if j >= 1:
                        turn(j - 1)
                    pe.wait_ge(up_ready, count(FCH, j + 1))
                    product(3, j, 4)
                    if j >= 1:
                        down(j - 1)
                turn(FCH - 1)
                down(FCH - 1)
                pe.wait_ge(comb_copied, count(1, 1))
                pe.wait_ge(y0_copied, count(1, 2))
                pe.wait_ge(y1_copied, count(1, 2))
                for k in range(KC):
                    if k >= 2:
                        pe.wait_ge(y_added, count(KC, k))
                    pe.matmul(bank[k % 2][:, 0:NT], ye[0:SLOTS, P * k:P * (k + 1)], comb[0:SLOTS, :], start=True, stop=True)\
                      .then_inc(c_summed, 1)

            with pe.Fori(0, NE) as e:
                expert(e, 0)
            over = pe.value_load(flag[0:1, 0:1], min_val=0, max_val=1)
            with pe.If(over > 0):
                for c in range(1, PASSES):
                    with pe.Fori(0, NE) as e:
                        expert(e, c)
            norm_sum(7)
            pe.wait_ge(h_ready, 5)
            for k in range(KC):
                if k >= 2:
                    pe.wait_ge(y_taken, k - 1)
                for q, n in ((0, P), (1, P), (2, NB)):
                    mm = pe.transpose(bank[2 + k % 2][0:n, P * q:P * (q + 1)], xT[:, k, q * P:q * P + n], ident)
                mm.then_inc(y_turned, 1)

        @block.scalar
        def _(act):
            steps = [0]

            def link(ins):
                steps[0] += 1
                ins.then_inc(act_step, 1)
                act.wait_ge(act_step, steps[0])

            split_to = [0]

            def high(i):
                n = split[i]
                size = plan[n][3] * plan[n][5]
                if i >= PAIRS:
                    act.wait_ge(pair_used, i - PAIRS + 1)
                act.wait_ge(slab_in[n % RING], slab_total(n))
                act.activation(w_hi[:, i % PAIRS, 0:size], ring[:, n % RING, 0:size], ACT.Copy).then_inc(hi_done, 1)

            def highs(end):
                while split_to[0] < min(end, NSPLIT):
                    high(split_to[0])
                    split_to[0] += 1

            def ada_rows(s):
                i0 = firsts[("ada", s)]
                for j in range(6):
                    highs(i0 + 2 * j + 1 + PAIRS)
                    act.wait_ge(pair_used, i0 + 2 * j + 2)
                    if 6 * s + j >= 2:
                        act.wait_ge(ada_turned, 6 * s + j - 1)
                    act.activation(arow[:, j % 2, :], bank[2 + j % 2][0:18, :], ACT.Copy).then_inc(arow_ready, 1)
                    highs(i0 + 2 * j + 2 + PAIRS)

            act.wait_ge(in_vec, 16 * 10)
            act.activation(crow[0:9, :], crow[0:9, :], ACT.Silu).then_inc(c_silu, 1)

            def norm(i, src):
                act.wait_ge(norm_in, i + 1)
                act.activation(tT[:, :, :], src[:, :, :], ACT.Square).then_inc(sq_ready, 1)
                act.wait_ge(norm_summed, i + 1)
                act.activation(std[:, :], bank[7][:, 0:NT], ACT.Sqrt, bias=eps1, scale=1.0 / D).then_inc(std_ready, 1)

            highs(PAIRS)
            ada_rows(0)
            norm(0, xT)
            ada_rows(1)
            for i in range(KC):
                act.wait_ge(pool_summed, i + 1)
                act.activation(mT[:, i, :], bank[i % 2][:, 0:NT], ACT.Copy, scale=vec2[:, 72 + i:73 + i]).then_inc(pool_taken, 1)
            act.wait_ge(ps_turned, 1)
            for k in range(2):
                ins = act.activation(pstate[0:STATE + NB, 512 * k:512 * (k + 1)], bank[4 + k][0:STATE + NB, :], ACT.Copy)
            ins.then_inc(ps_rows, 1)
            act.wait_ge(ps_rows, 1)
            act.dma_start(o["pool_prompt"][0, 0], pstate[0:STATE, :]).then_inc(out_done, 16)
            act.dma_start(o["pool_sample"][:, 0, STATE - 1, :], pstate[STATE:STATE + NB, :]).then_inc(out_done, 16)
            act.wait_ge(pool_taken, KC)
            norm(1, mT)
            norm(2, xT)
            act.wait_ge(out_done, 32)
            def operand_high(n, out, src):
                act.wait_ge(h_ready, n)
                act.activation(out[:, :, :], src[:, :, :], ACT.Copy).then_inc(act_hi, 1)

            operand_high(1, tHi, hT)
            i0 = firsts[("w1", 0)]

            def g_high(c):
                for i in (2 * c, 2 * c + 1):
                    act.wait_ge(fup_done, i + 1)
                    act.activation(gHi[:, i, :], g_new[:, i % 4, :], ACT.Copy).then_inc(g_hi, 1)

            for c in range(FB // 2):
                highs(i0 + 2 * c + PAIRS)
                act.wait_ge(pair_used, i0 + 2 * c + 1)
                for m in range(2):
                    i = 2 * c + m
                    if i >= 2:
                        act.wait_ge(fup_done, i - 1)
                    act.activation(silu_up[:, i % 2, :], bank[4 * (c % 2) + m][:, 0:NT], ACT.Silu).then_inc(fup_silu, 1)
                highs(i0 + 2 * c + 1 + PAIRS)
                if c >= 1:
                    g_high(c - 1)
            g_high(FB // 2 - 1)
            highs(firsts[("ada", 2)] + PAIRS)
            ada_rows(2)
            norm(3, mT)
            norm(4, xT)
            operand_high(2, tHi, hT)
            for c in range(8 + 12):
                i0 = firsts[("wkv", 0)] + c
                highs(min(i0 + PAIRS, firsts[("wo", 0)]))
                if c == 8:
                    operand_high(3, tHi, hT)
                act.wait_ge(pair_used, i0 + 1)
                for m in range(2):
                    src = bank[2 * (c % 2) + m][:, 0:NT]
                    if 4 <= c < 8:
                        act.activation(vraw[:, 2 * (c - 4) + m, :], src, ACT.Copy).then_inc(lin_raw, 1)
                        continue
                    r = 2 * (c if c < 4 else c - 4) + m
                    if r >= 4:
                        act.wait_ge(rot_done, r - 3)
                    act.activation(rawT[:, r % 4, :], src, ACT.Copy).then_inc(lin_raw, 1)

            for t in range(NB * NG):
                act.wait_ge(kt_turned, t + 1)
                if t >= 2:
                    act.wait_ge(s_summed, t - 1)
                if t == 0:
                    act.wait_ge(pair_ready, 1)
                act.activation(kTs[:, t % 2, 0:512], bank[2 * (t % 2)][:, :], ACT.Copy).then_inc(kt_lo, 1)
            act.wait_ge(s_max, 1)
            act.activation(s_soft, s_soft, ACT.Exp, bias=s_stat[:, 0:1], accum_out=s_stat[:, 1:2]).then_inc(s_exp, 1)
            highs(firsts[("wo", 0)] + PAIRS)
            for u in range(2 * H):
                c = u % 2
                n = P * (c + 1)
                act.wait_ge(a_max, u + 1)
                act.activation(sm[u % 2][:, :, 0:n], sm[u % 2][:, :, 0:n], ACT.Exp, bias=p_stat[:, u % 4, 0:1],
                               accum_out=p_stat[:, u % 4, 1:2]).then_inc(a_exp, 1)
                if u >= 1:
                    v = u - 1
                    act.wait_ge(a_turned, v + 1)
                    if v >= 1:
                        act.wait_ge(a_out, v)
                    act.activation(p_T[:, 0:v % 2 + 1, :], bank[4][:, 0:P * (v % 2 + 1)].rearrange("p (k n) -> p k n", n=P),
                                   ACT.Copy).then_inc(a_copied, 1)
            v = 2 * H - 1
            act.wait_ge(a_turned, v + 1)
            act.wait_ge(a_out, v)
            act.activation(p_T[:, 0:v % 2 + 1, :], bank[4][:, 0:P * (v % 2 + 1)].rearrange("p (k n) -> p k n", n=P),
                           ACT.Copy).then_inc(a_copied, 1)
            act.wait_ge(ot_taken, KC)
            act.activation(tHi[:, :, :], mT[:, :, :], ACT.Copy).then_inc(act_hi, 1)
            i0 = firsts[("wo", 0)]
            for c in range(4):
                highs(i0 + c + PAIRS)
                act.wait_ge(pair_used, i0 + c + 1)
                for m in range(2):
                    act.activation(woT[:, 2 * c + m, :], bank[((2, 3), (4, 5))[c % 2][m]][:, 0:NT], ACT.Copy).then_inc(wo_taken, 1)
            ada_rows(3)
            norm(5, woT)
            norm(6, xT)
            act.wait_ge(lg_max, 1)
            for q, n in ((0, P), (1, P), (2, NB)):
                ins = act.activation(r_c[0:n, q, :], lg[0:n, q, :], ACT.Exp, bias=r_s[0:n, q, 0:1])
            ins.then_inc(lg_exp, 1)
            for k in range(KC):
                act.wait_ge(ht_turned, k + 1)
                act.activation(htok_hi[:, 0:2, P * k:P * (k + 1)], bank[2 + k % 2][:, 0:256].rearrange("p (c n) -> p c n", c=2), ACT.Copy)
                act.activation(htok_hi[0:NB, 2, P * k:P * (k + 1)], bank[2 + k % 2][0:NB, 256:384], ACT.Copy).then_inc(ht_hi, 1)
            act.sem_inc(silu_done, 1)
            act.sem_inc(y0_copied, 1)

            def expert(e, c):
                def count(per, k):
                    return e * per + (c * NE * per + k)

                use = [[k for k in range(PER_E) if (NPRE + k) % RING == r] for r in range(RING)]

                def high(k):
                    slot = (NPRE + k) % RING
                    act.wait_ge(pair_used, e * PER_E + (NSPLIT + c * NE * PER_E + k - PAIRS + 1))
                    act.wait_ge(slab_in[slot], e * (16 * len(use[slot])) + (
                        before_experts[slot] + 16 * (c * NE * len(use[slot]) + use[slot].index(k) + 1)))
                    act.activation(w_hi[:, (NSPLIT + k) % PAIRS, :], ring[:, slot, :], ACT.Copy).then_inc(hi_done, 1)

                for k in range(PAIRS):
                    high(k)
                act.wait_ge(gathered, count(2, 2))
                for q in range(2):
                    ins = act.activation(xe_hi[:, 4 * q:4 * q + 4, :], bank[q][:, :].rearrange("p (k n) -> p k n", k=4), ACT.Copy)
                ins.then_inc(xe_hi_ready, 1)

                def turned_high(j):
                    act.wait_ge(up_turned, count(FCH, j + 1))
                    act.activation(upT_hi[:, :, :], bank[5][:, :].rearrange("p (k n) -> p k n", k=4), ACT.Copy).then_inc(upT_hi_ready, 1)

                for k, (m, j, half) in enumerate(eslabs):
                    if k + PAIRS < PER_E:
                        high(k + PAIRS)
                    if (m, half) == (1, 1):
                        act.wait_ge(pair_used, used_by(e, c, 1, j))
                        act.wait_ge(up_ready, count(FCH, j + 1))
                        act.activation(up_s[0:SLOTS, :], bank[3][0:SLOTS, :], ACT.Silu).then_inc(silu_done, 1)
                        if j >= 1:
                            turned_high(j - 1)
                    if (m, j, half) == (3, FCH - 1, 1):
                        turned_high(FCH - 1)
                act.wait_ge(pair_used, used_by(e, c, 2, FCH - 1))
                act.activation(ye[0:SLOTS, 0:512], bank[6][0:SLOTS, :], ACT.Copy).then_inc(y0_copied, 1)

            with act.Fori(0, NE) as e:
                expert(e, 0)
            over = act.value_load(flag[0:1, 0:1], min_val=0, max_val=1)
            with act.If(over > 0):
                for c in range(1, PASSES):
                    with act.Fori(0, NE) as e:
                        expert(e, c)
            norm(7, mT)
            for k in range(KC):
                act.wait_ge(y_turned, k + 1)
                act.activation(ytok[:, 0:2, P * k:P * (k + 1)], bank[2 + k % 2][:, 0:256].rearrange("p (c n) -> p c n", c=2), ACT.Copy)
                act.activation(ytok[0:NB, 2, P * k:P * (k + 1)], bank[2 + k % 2][0:NB, 256:384], ACT.Copy).then_inc(y_taken, 1)
            act.wait_ge(y_taken, KC)
            act.dma_start(o["y_prompt"][0].rearrange("(c p) d -> p c d", p=P), ytok[:, 0:2, :]).then_inc(out_done, 16)
            act.dma_start(o["y_sample"][:, 0, :], ytok[0:NB, 2, :]).then_inc(out_done, 16)
            act.wait_ge(out_done, 16 * 4)

        @block.vector
        def _(dve):
            steps = [0]

            def link(ins):
                steps[0] += 1
                ins.then_inc(dve_step, 1)
                dve.wait_ge(dve_step, steps[0])

            dve.wait_ge(vec_turned, 1)
            dve.tensor_copy(vec1[:, :], bank[0][:, 0:96])
            dve.tensor_copy(vec2[:, :], bank[0][:, 96:176]).then_inc(vec_read, 1)
            dve.wait_ge(c_turned, 1)
            dve.tensor_copy(cT[:, :, :], bank[1][:, 0:9 * KC].rearrange("p (k n) -> p k n", k=KC)).then_inc(c_read, 1)
            dve.wait_ge(c_read, 1)
            link(dve.tensor_copy(c18[:, :, 0:9], cT[:, :, :]))
            dve.tensor_tensor(c18[:, :, 9:18], cT[:, :, :], c18[:, :, 0:9].bitcast(F32), ALU.subtract).then_inc(c_split, 1)
            split_to = [0]

            def lows_to(end):
                while split_to[0] < min(end, NSPLIT):
                    if owner(split_to[0]) == "vector":
                        remainder(dve, split_to[0], lo_done)
                    split_to[0] += 1

            for k in range(KC):
                dve.wait_ge(x_turned, k + 1)
                dve.tensor_copy(xT[:, k, :], bank[2 + k % 2][:, 0:NT]).then_inc(x_taken, 1)
            dve.wait_ge(x_taken, KC)
            dve.sem_inc(norm_in, 1)
            for k in range(KC):
                dve.wait_ge(st_turned, k + 1)
                dve.tensor_copy(sExt[:, k, :, 0:STATE], bank[4 + k % 2][:, 0:120].rearrange("p (b t) -> p b t", b=NB))\
                   .then_inc(st_taken, 1)
            link(dve.memset(ext[:, :, 0:STATE], 0.0))

            def across(a, n):
                return a.unsqueeze(2).to_broadcast(list(a.shape[:2]) + [n])

            def ada_take(s, kind, layer):
                a = ada[:, s]
                dve.wait_ge(ada_turned, 6 * (s + 1))
                dve.wait_ge(vec_read, 1)
                col = 48 * kind + 24 * layer
                sums = bank[6][:, 0:432].rearrange("p (m n) -> p m n", m=24)
                link(dve.tensor_tensor(a, sums[:, :, 0:9], across(vec1[:, col:col + 24], 9), ALU.add))
                link(dve.tensor_tensor(a, a, sums[:, :, 9:18], ALU.add))
                pre, post = 32 * kind + 8 * layer, 32 * kind + 16 + 8 * layer
                dve.scalar_tensor_tensor(a[:, 8:16, :], a[:, 8:16, :], 1.0, across(vec2[:, pre:pre + 8], 9), ALU.add, ALU.mult)
                link(dve.tensor_tensor(a[:, 16:24, :], a[:, 16:24, :], across(vec2[:, post:post + 8], 9), ALU.mult))
                dve.sem_inc(ada_taken, 1)

            def wide(a):
                return a.unsqueeze(1).to_broadcast([P, KC, a.shape[-1]])

            def normalise(i, src, fresh=True):
                dve.wait_ge(std_ready, i + 1)
                if fresh:
                    link(dve.reciprocal(rstd[:, :], std[:, :]))
                link(dve.tensor_tensor(tT[:, :, :], src[:, :, :], wide(rstd[:, :]), ALU.mult))

            def modulate(s, out, done):
                for k in range(KC):
                    dve.tensor_scalar(out[:, k, 0:T], tT[:, k, 0:T], ada[:, s, 8 + k, 0:1], ada[:, s, k, 0:1], ALU.mult, ALU.add)
                link(dve.tensor_tensor(small[:, :, :], tT[:, :, T:NT], ada[:, s, 8:16, 1:9], ALU.mult))
                link(dve.tensor_tensor(out[:, :, T:NT], small[:, :, :], ada[:, s, 0:8, 1:9], ALU.add))
                if done is not None:
                    dve.sem_inc(done, 1)

            def residual(s, done):
                for k in range(KC):
                    dve.scalar_tensor_tensor(xT[:, k, 0:T], tT[:, k, 0:T], ada[:, s, 16 + k, 0:1], xT[:, k, 0:T], ALU.mult, ALU.add)
                link(dve.tensor_tensor(small[:, :, :], tT[:, :, T:NT], ada[:, s, 16:24, 1:9], ALU.mult))
                link(dve.tensor_tensor(xT[:, :, T:NT], xT[:, :, T:NT], small[:, :, :], ALU.add))
                if done is not None:
                    dve.sem_inc(done, 1)

            lows_to(firsts[("ada", 1)])
            ada_take(0, 0, 0)
            normalise(0, xT)
            modulate(0, hT, None)
            lows_to(firsts[("ada", 1)] + 3)
            link(dve.tensor_copy(ext[:, :, STATE:EXT], hT[:, :, 0:T]))
            link(dve.tensor_copy(sExt[:, :, :, STATE], hT[:, :, T:NT]))
            link(dve.tensor_tensor(sum_a[:, :, 1:EXT], ext[:, :, 1:EXT], ext[:, :, 0:EXT - 1], ALU.add))
            link(dve.tensor_tensor(sum_b[:, 2:KC, 3:EXT], sum_a[:, 2:KC, 3:EXT], sum_a[:, 2:KC, 1:EXT - 2], ALU.add))
            link(dve.tensor_tensor(sum_a[:, 4:KC, 7:EXT], sum_b[:, 4:KC, 7:EXT], sum_b[:, 4:KC, 3:EXT - 4], ALU.add))
            link(dve.tensor_tensor(sum_b[:, 6:KC, 15:EXT], sum_a[:, 6:KC, 15:EXT], sum_a[:, 6:KC, 7:EXT - 8], ALU.add))
            lows_to(firsts[("ada", 1)] + 6)
            for g, n in enumerate(WIN):
                s = (sum_a, sum_b)[g % 2]
                ks = slice(2 * g, 2 * g + 2)
                link(dve.scalar_tensor_tensor(tT[:, ks, 16:T], s[:, ks, STATE + 16:EXT], 1.0 / n, ext[:, ks, STATE + 16:EXT],
                                              ALU.mult, ALU.subtract))
                link(dve.tensor_tensor(tT[:, ks, 0:16], s[:, ks, STATE:STATE + 16],
                                       invcnt[:, g, :].unsqueeze(1).to_broadcast([P, 2, 16]), ALU.mult))
                link(dve.tensor_tensor(tT[:, ks, 0:16], tT[:, ks, 0:16], ext[:, ks, STATE:STATE + 16], ALU.subtract))
                for k in range(2 * g, 2 * g + 2):
                    link(dve.tensor_reduce(small[:, k, :], sExt[:, k, :, STATE + 1 - n:STATE + 1], X, ALU.add))
                    link(dve.scalar_tensor_tensor(tT[:, k, T:NT], small[:, k, :], 1.0 / n, sExt[:, k, :, STATE], ALU.mult, ALU.subtract))
            dve.sem_inc(pm_ready, 1)
            lows_to(firsts[("w1", 0)])
            ada_take(1, 1, 0)
            dve.wait_ge(pool_taken, KC)
            dve.sem_inc(norm_in, 1)
            normalise(1, mT)
            residual(0, norm_in)
            normalise(2, xT)
            dve.wait_ge(ps_turned, 1)
            modulate(1, hT, None)
            def operand_low(n, out, src, hi):
                dve.wait_ge(act_hi, n)
                dve.tensor_tensor(out[:, :, :], src[:, :, :], hi[:, :, :].bitcast(F32), ALU.subtract).then_inc(act_lo, 1)

            dve.sem_inc(h_ready, 1)
            dve.wait_ge(out_done, 32)
            operand_low(1, mLo, hT, tHi)
            i0 = firsts[("w1", 0)]

            def g_low(c):
                for i in (2 * c, 2 * c + 1):
                    dve.wait_ge(g_hi, i + 1)
                    dve.tensor_tensor(gLo[:, i, :], g_new[:, i % 4, :], gHi[:, i, :].bitcast(F32), ALU.subtract).then_inc(g_lo, 1)

            for c in range(FB // 2):
                lows_to(i0 + 2 * c + PAIRS)
                lows_to(i0 + 2 * c + 1 + PAIRS)
                dve.wait_ge(pair_used, i0 + 2 * c + 2)
                for m in range(2):
                    i = 2 * c + m
                    dve.wait_ge(fup_silu, i + 1)
                    if i >= 4:
                        dve.wait_ge(g_lo, i - 3)
                    dve.tensor_tensor(g_new[:, i % 4, :], bank[4 * (c % 2) + 2 + m][:, 0:NT], silu_up[:, i % 2, :], ALU.mult).then_inc(fup_done, 1)
                if c >= 1:
                    g_low(c - 1)
            g_low(FB // 2 - 1)
            i0 = firsts[("w2", 0)]
            for c in range(4):
                lows_to(i0 + 3 * c + 3 + PAIRS)
                dve.wait_ge(pair_used, i0 + 3 * c + 3)
                for m in range(2):
                    dve.tensor_copy(mT[:, 2 * c + m, :], bank[((0, 1), (4, 5))[c % 2][m]][:, 0:NT]).then_inc(fdn_taken, 1)
            dve.wait_ge(fdn_taken, 8)
            dve.sem_inc(norm_in, 1)
            lows_to(firsts[("wkv", 0)])
            ada_take(2, 0, 1)
            normalise(3, mT)
            residual(1, norm_in)
            normalise(4, xT)
            for k in range(KC):
                ins = dve.tensor_scalar(hT[:, k, :], tT[:, k, :], vec2[:, 64 + k:65 + k], None, ALU.mult)
            link(ins)
            dve.sem_inc(h_ready, 1)
            operand_low(2, mLo, hT, tHi)

            def rope(i, out):
                dve.wait_ge(rot_summed, i + 1)
                link(dve.tensor_tensor(rot_a, bank[4 + i % 2][:, 0:NT], sin, ALU.mult))
                link(dve.tensor_tensor(rot_b, rawT[:, i % 4, :], cos, ALU.mult))
                dve.tensor_tensor(out, rot_a, rot_b, ALU.add).then_inc(rot_done, 1)
                dve.wait_ge(rot_done, i + 1)

            i0 = firsts[("wkv", 0)]
            for c in range(8):
                lows_to(i0 + c + PAIRS)
                if 1 <= c <= 4:
                    rope(2 * c - 2, kT[:, 2 * c - 2, :])
                    rope(2 * c - 1, kT[:, 2 * c - 1, :])
            for q in range(4):
                dve.wait_ge(kv_turned, q + 1)
                cols = slice(512 * (q % 2), 512 * (q % 2) + 512)
                rows = (ktok[:, 0, cols], ktok[:, 1, cols], ktok[0:NB, 2, cols]) if q < 2 else \
                    (vtok[:, 0, cols], vtok[:, 1, cols], vntok[:, cols])
                dve.tensor_copy(rows[0], bank[4][:, :])
                dve.tensor_copy(rows[1], bank[5][:, :])
                dve.tensor_copy(rows[2], bank[7][0:NB, :]).then_inc(kv_taken, 1)
            dve.wait_ge(lin_raw, 2 * KC)
            link(dve.tensor_copy(vnew[:, :, :], vraw[:, :, T:NT]))
            dve.wait_ge(pair_used, firsts[("wq", 0)])
            link(dve.tensor_tensor(tT[:, :, :], xT[:, :, :], wide(rstd[:, :]), ALU.mult))
            modulate(2, hT, h_ready)
            operand_low(3, mLo, hT, tHi)
            dve.wait_ge(kv_rows, 16 * 4)
            i0 = firsts[("wq", 0)]
            for c in range(13):
                if c < 12:
                    lows_to(min(i0 + c + PAIRS, firsts[("wo", 0)]))
                if c >= 1:
                    for i in (2 * c - 2, 2 * c - 1):
                        rope(KC + i, qT[:, i, :])
            dve.wait_ge(rot_summed, KC + NG * KC)
            dve.memset(hflat[:, 0:384], 0.0)
            link(dve.memset(hflat[:, 384:768], 0.0))
            for g in range(NG):
                for s in range(2):
                    q = slice(HD * s, HD * (s + 1))
                    link(dve.tensor_copy(qpair[q, g, :, :, s], qT[q, g * KC:(g + 1) * KC, T:NT].rearrange("p j b -> p b j")))
                    link(dve.tensor_tensor(kprod[q, g, :, :, s], qpair[q, g, :, :, s], kT[q, :, T:NT].rearrange("p j b -> p b j"), ALU.mult))
            dve.sem_inc(pair_ready, 1)
            for t in range(NB * NG):
                dve.wait_ge(kt_turned, t + 1)
                if t >= 2:
                    dve.wait_ge(s_summed, t - 1)
                dve.tensor_copy(kTs[:, t % 2, 512:1024], bank[2 * (t % 2) + 1][:, :]).then_inc(kt_hi, 1)
            dve.wait_ge(s_summed, NB * NG)
            dve.tensor_copy(s_scores, bank[4][:, 0:384].rearrange("p (g n) -> p g n", g=NG)).then_inc(s_taken, 1)
            dve.wait_ge(s_turned, 1)
            link(dve.tensor_scalar(s_soft[:, 0:384], bank[6][:, 0:384], SCALE, None, ALU.mult))
            link(dve.tensor_scalar(s_soft[:, 384:387], bank[5][:, 0:3], SCALE, None, ALU.mult))
            dve.tensor_reduce(s_stat[:, 0:1], s_soft, X, ALU.max, negate=True).then_inc(s_max, 1)
            dve.wait_ge(s_exp, 1)
            link(dve.reciprocal(s_stat[:, 2:3], s_stat[:, 1:2]))
            dve.tensor_scalar(s_soft, s_soft, s_stat[:, 2:3], None, ALU.mult).then_inc(s_prob, 1)
            dve.wait_ge(s_prob, 1)
            link(dve.tensor_reduce(s_stat[:, 3:4], s_soft[:, 384:387], X, ALU.add))
            dve.tensor_copy(pnewb, s_stat[:, 3:4].to_broadcast([P, P])).then_inc(pn_ready, 1)
            dve.wait_ge(sp_turned, 1)
            dve.tensor_copy(s_pT, bank[7][:, 0:384].rearrange("p (g n) -> p g n", g=NG)).then_inc(sp_taken, 1)
            lows_to(firsts[("wo", 0)] + PAIRS)
            dve.wait_ge(pn_spread, 1)
            dve.wait_ge(sv_summed, 1)
            for s in range(2):
                q = slice(HD * s, HD * (s + 1))
                pn = bank[5][q, P:2 * P].rearrange("p (b j s) -> p j b s", b=NB, j=KC)[:, :, :, s]
                sv = bank[4][q, 0:P].rearrange("p (b j s) -> p j b s", b=NB, j=KC)[:, :, :, s]
                link(dve.tensor_tensor(small[q, :, :], pn, vnew[q, :, :], ALU.mult))
                link(dve.tensor_tensor(mT[q, :, T:NT], small[q, :, :], sv, ALU.add))
            dve.sem_inc(sv_done, 1)
            def mask_max(u):
                c = u % 2
                n = P * (c + 1)
                dve.wait_ge(a_scored, u + 1)
                if u >= 2:
                    dve.wait_ge(a_sum, u - 1)
                for q, (g0, g1) in enumerate(((0, 2), (2, 3))):
                    src = bank[2 * c + q][:, 0:256 * (g1 - g0)].rearrange("p (g k) -> p g k", k=256)[:, :, 0:n]
                    ins = dve.scalar_tensor_tensor(sm[u % 2][:, g0:g1, 0:n], src, SCALE, mask[:, g0:g1, 256 - n:256], ALU.mult, ALU.add)
                link(ins)
                dve.tensor_reduce(p_stat[:, u % 4, 0:1], sm[u % 2][:, :, 0:n], mybir.AxisListType.XY, ALU.max, negate=True).then_inc(a_max, 1)

            def head_out(u):
                h, c = u // 2, u % 2
                dve.wait_ge(a_exp, u + 1)
                link(dve.reciprocal(p_stat[:, u % 4, 2:3], p_stat[:, u % 4, 1:2]))
                dve.wait_ge(a_out, u + 1)
                dve.tensor_scalar(otok[:, c, HD * h:HD * (h + 1)], bank[6 + u % 2][:, 0:HD], p_stat[:, u % 4, 2:3], None, ALU.mult)\
                   .then_inc(a_taken, 1)

            for u in range(2 * H + 2):
                if u < 2 * H:
                    mask_max(u)
                if u >= 2:
                    head_out(u - 2)
            for k in range(KC):
                dve.wait_ge(ot_turned, k + 1)
                dve.tensor_copy(mT[:, k, 0:T], bank[k % 2][:, 0:T]).then_inc(ot_taken, 1)
            dve.wait_ge(ot_taken, KC)
            operand_low(4, hLo, mT, tHi)
            lows_to(firsts[("ada", 3)] + PAIRS)
            dve.wait_ge(wo_taken, KC)
            dve.sem_inc(norm_in, 1)
            lows_to(NSPLIT)
            ada_take(3, 1, 1)
            normalise(5, woT)
            residual(2, norm_in)
            normalise(6, xT)
            modulate(3, hT, h_ready)
            dve.wait_ge(lg_summed, 1)
            rows = (P, P, NB)
            link(dve.memset(sel[:, :, :], 0.0))
            for q, n in enumerate(rows):
                ins = dve.tensor_copy(lg[0:n, q, :], bank[0][0:n, NE * q:NE * (q + 1)])
            link(ins)
            for q, n in enumerate(rows):
                ins = dve.tensor_reduce(r_s[0:n, q, 0:1], lg[0:n, q, :], X, ALU.max, negate=True)
            ins.then_inc(lg_max, 1)
            for q, n in enumerate(rows):
                mine = lg[0:n, q, :].unsqueeze(2).to_broadcast([n, NE, NE])
                other = lg[0:n, q, :].unsqueeze(1).to_broadcast([n, NE, NE])
                link(dve.tensor_tensor(r_a[0:n], other, mine, ALU.is_gt))
                link(dve.tensor_tensor(r_b[0:n], other, mine, ALU.is_equal))
                link(dve.tensor_tensor(r_b[0:n], r_b[0:n], tri[0:n], ALU.mult))
                link(dve.tensor_tensor(r_a[0:n], r_a[0:n], r_b[0:n], ALU.add))
                link(dve.tensor_reduce(gate[0:n, q, :], r_a[0:n], X, ALU.add))
                link(dve.tensor_scalar(sel[0:n, q, :], gate[0:n, q, :], 1.5, None, ALU.is_lt))
            dve.sem_inc(sel_ready, 1)
            for k in range(KC):
                dve.wait_ge(ht_hi, k + 1)
                dve.tensor_tensor(htok_lo[:, 0:2, P * k:P * (k + 1)], bank[2 + k % 2][:, 0:256].rearrange("p (c n) -> p c n", c=2),
                                  htok_hi[:, 0:2, P * k:P * (k + 1)].bitcast(F32), ALU.subtract)
                dve.tensor_tensor(htok_lo[0:NB, 2, P * k:P * (k + 1)], bank[2 + k % 2][0:NB, 256:384],
                                  htok_hi[0:NB, 2, P * k:P * (k + 1)].bitcast(F32), ALU.subtract).then_inc(ht_taken, 1)
            dve.wait_ge(lg_exp, 1)
            for q, n in enumerate(rows):
                link(dve.tensor_tensor(r_c[0:n, q, :], r_c[0:n, q, :], sel[0:n, q, :], ALU.mult))
                link(dve.tensor_reduce(r_s[0:n, q, 1:2], r_c[0:n, q, :], X, ALU.add))
                link(dve.reciprocal(r_s[0:n, q, 2:3], r_s[0:n, q, 1:2]))
                link(dve.tensor_scalar(gate[0:n, q, :], r_c[0:n, q, :], r_s[0:n, q, 2:3], None, ALU.mult))
            dve.wait_ge(pos_summed, 1)
            for q, n in enumerate(rows):
                link(dve.scalar_tensor_tensor(r_c[0:n, q, :], bank[1][0:n, NE * q:NE * (q + 1)], 1.0, sel[0:n, q, :], ALU.add, ALU.mult))
                link(dve.tensor_scalar(posm[0:n, q, :], r_c[0:n, q, :], -1.0, None, ALU.add))
            link(dve.tensor_reduce(r_s[:, 0, 3:4], bank[1][:, 3 * NE:4 * NE], X, ALU.max))
            dve.tensor_scalar(flag[:, :], r_s[:, 0, 3:4], SLOTS + 0.5, None, ALU.is_gt).then_inc(flag_ready, 1)
            dve.wait_ge(flag_ready, 1)
            link(dve.memset(mT[:, :, :], 0.0))
            dve.sem_inc(moe_ready, 1)
            dve.sem_inc(up_ready, 1)
            dve.sem_inc(y1_copied, 1)
            dve.sem_inc(y_added, 1)
            dve.sem_inc(upT_ready, 1)

            def expert(e, c):
                def count(per, k):
                    return e * per + (c * NE * per + k)

                dve.wait_ge(y_added, count(KC, 1))
                for q, n in enumerate(rows):
                    place = posm[0:n, q, :][:, bass.ds(e, 1)]
                    dve.tensor_scalar(disp[0:n, q, :], iota[0:n, c * SLOTS:(c + 1) * SLOTS], place, None, ALU.is_equal)
                    ins = dve.tensor_scalar(dispg[0:n, q, :], iota[0:n, c * SLOTS:(c + 1) * SLOTS], place,
                                            gate[0:n, q, :][:, bass.ds(e, 1)], ALU.is_equal, ALU.mult)
                ins.then_inc(route_built, 1)
                def low(k):
                    i, slot = (NSPLIT + k) % PAIRS, (NPRE + k) % RING
                    dve.wait_ge(hi_done, e * PER_E + (NSPLIT + c * NE * PER_E + k + 1))
                    dve.tensor_tensor(w_lo[:, i, :], ring[:, slot, :], w_hi[:, i, :].bitcast(F32), ALU.subtract).then_inc(lo_done, 1)

                for k in range(PAIRS):
                    low(k)
                dve.wait_ge(xe_hi_ready, count(1, 1))
                for q in range(2):
                    ins = dve.tensor_tensor(xe_lo[:, 4 * q:4 * q + 4, :], bank[q][:, :].rearrange("p (k n) -> p k n", k=4),
                                            xe_hi[:, 4 * q:4 * q + 4, :].bitcast(F32), ALU.subtract)
                ins.then_inc(xe_ready, 1)
                dve.wait_ge(comb_turned, count(1, 1))
                dve.tensor_copy(comb[0:SLOTS, :], bank[2][0:SLOTS, 0:NT]).then_inc(comb_copied, 1)

                def turned_low(j):
                    dve.wait_ge(upT_hi_ready, count(FCH, j + 1))
                    dve.tensor_tensor(upT_lo[:, :, :], bank[5][:, :].rearrange("p (k n) -> p k n", k=4),
                                      upT_hi[:, :, :].bitcast(F32), ALU.subtract).then_inc(upT_ready, 1)

                for k, (m, j, half) in enumerate(eslabs):
                    if k + PAIRS < PER_E:
                        low(k + PAIRS)
                    if (m, half) == (1, 1) and j >= 1:
                        turned_low(j - 1)
                    if (m, half) == (3, 1):
                        dve.wait_ge(pair_used, used_by(e, c, 3, j))
                        dve.wait_ge(silu_done, count(FCH, j + 2))
                        dve.tensor_tensor(up[0:SLOTS, :], bank[4][0:SLOTS, :], up_s[0:SLOTS, :], ALU.mult).then_inc(up_ready, 1)
                        if j == FCH - 1:
                            turned_low(j)
                dve.wait_ge(pair_used, used_by(e, c, 2, FCH - 1))
                dve.tensor_copy(ye[0:SLOTS, 512:1024], bank[7][0:SLOTS, :]).then_inc(y1_copied, 1)
                for k in range(KC):
                    dve.wait_ge(c_summed, count(KC, k + 1))
                    dve.tensor_tensor(mT[:, k, :], mT[:, k, :], bank[k % 2][:, 0:NT], ALU.add).then_inc(y_added, 1)

            with dve.Fori(0, NE) as e:
                expert(e, 0)
            over = dve.value_load(flag[0:1, 0:1], min_val=0, max_val=1)
            with dve.If(over > 0):
                for c in range(1, PASSES):
                    with dve.Fori(0, NE) as e:
                        expert(e, c)
            link(dve.tensor_copy(small[:, 0, 0:1], mT[:, 0, 0:1]))
            dve.sem_inc(norm_in, 1)
            normalise(7, mT)
            residual(3, h_ready)

        @block.gpsimd
        def _(pool):
            pool.dma_start(o["pool_sample"][:, 0, 0:STATE - 1, :], w["state_pool"][:, 0, 1:STATE, :]).then_inc(moved_up, 16)
            pool.wait_ge(kv_taken, 2)
            pool.dma_start(o["k_prompt"][0].rearrange("(c p) h d -> p c (h d)", p=P), ktok[:, 0:2, :]).then_inc(kv_rows, 16)
            pool.dma_start(o["k_sample"][:, 0].rearrange("b h d -> b (h d)"), ktok[0:NB, 2, :]).then_inc(kv_rows, 16)
            pool.wait_ge(kv_taken, 4)
            pool.dma_start(o["v_prompt"][0].rearrange("(c p) h d -> p c (h d)", p=P), vtok[:, 0:2, :]).then_inc(kv_rows, 16)
            pool.dma_start(o["v_sample"][:, 0].rearrange("b h d -> b (h d)"), vntok).then_inc(kv_rows, 16)
            pool.wait_ge(kv_rows, 64)
            pool.wait_ge(moved_up, 16)
            for u in range(2 * H):
                n = P * (u % 2 + 1)
                pool.wait_ge(a_exp, u + 1)
                if u >= 1:
                    pool.wait_ge(a_turned, u)
                s = sm[u % 2]
                pool.tensor_tensor(p_sum[:, 0:n], s[:, 0, 0:n], s[:, 1, 0:n], ALU.add).then_inc(pool_step, 1)
                pool.wait_ge(pool_step, u + 1)
                pool.tensor_tensor(p_sum[:, 0:n], p_sum[:, 0:n], s[:, 2, 0:n], ALU.add).then_inc(a_sum, 1)


def shape_constants():
    import numpy as np
    t = np.zeros((P, NCONST), np.float32)

    def put(name, v):
        a, b = CONST[name]
        t[:, a:b] = np.asarray(v, np.float32).reshape(-1, b - a)

    p = np.arange(P)
    half = HD // 2
    inv = (10000.0 ** (-np.arange(half, dtype=np.float64) / half)).astype(np.float32)
    pos = np.concatenate([np.arange(T), np.full(NB, PAST)]).astype(np.float32)
    ang = (inv[p % half][:, None] * pos[None, :]).astype(np.float32)
    put("cos", np.cos(ang.astype(np.float64)))
    put("sin", np.sin(ang.astype(np.float64)))
    dist = (P + p)[:, None] - np.arange(T)[None, :]
    m = [np.where((dist >= 0) & (dist <= win) & (dist % dil == 0), 0.0, NEG) for win, dil in GROUPS]
    put("mask", np.stack(m, 1))
    put("cnt", np.tile(np.stack([1.0 / np.minimum(n, np.arange(16) + 1) for n in WIN])[None], (P, 1, 1)))
    put("ident", np.eye(P))
    r = np.zeros((P, P))
    for i in range(P):
        r[i + half if i % HD < half else i - half, i] = -1.0 if i % HD < half else 1.0
    put("rot", r)
    put("before", p[:, None] < p[None, :])
    put("ones", np.ones((P, P)))
    put("iota", np.tile(np.arange(SLOTS * PASSES), (P, 1)))
    e = np.arange(NE)
    put("tri", np.tile((e[None, :] < e[:, None]).reshape(1, -1), (P, 1)))
    put("eps", np.full((P, 1), EPS))
    return t


_INS = ["x_prompt", "x_sample", "state_pool", "cache_k", "cache_v", "c_prompt", "c_sample", "ada_mix_w", "ada_mix_b",
        "g_pre_mix", "g_post_mix", "pool_w", "pool_scale", "g_kv", "w_kv", "w_q", "w_o", "ada_ffn_w", "ada_ffn_b",
        "g_pre_ffn", "g_post_ffn", "ffn_w1", "ffn_w3", "ffn_w2", "router_w", "router_b", "moe_w1", "moe_w3", "moe_w2"]
_OUTS = [("y_prompt", (1, T, D)), ("y_sample", (NB, 1, D)), ("pool_prompt", (1, 1, STATE, D)), ("pool_sample", (NB, 1, STATE, D)),
         ("k_prompt", (1, T, H, HD)), ("v_prompt", (1, T, H, HD)), ("k_sample", (NB, 1, H, HD)), ("v_sample", (NB, 1, H, HD))]


def kernel(**inputs):
    import numpy as np
    import concourse.bacc as bacc
    from concourse.bass_utils import run_bass_kernel_spmd

    nc = bacc.Bacc("TRN2", target_bir_lowering=False, num_devices=1)
    arrays, w, o = {}, {}, {}
    for name in _INS:
        arrays[f"in_{name}"] = np.ascontiguousarray(inputs[name])
    arrays["in_shape_constants"] = shape_constants()
    for name, a in arrays.items():
        w[name[3:]] = nc.dram_tensor(name, a.shape, F32, kind="ExternalInput").ap()
    for name, shape in _OUTS:
        o[name] = nc.dram_tensor(f"out_{name}", shape, F32, kind="ExternalOutput").ap()
    yoco_step(nc, w, o)
    r = run_bass_kernel_spmd(nc, [arrays], core_ids=[0])
    return tuple(r.results[0][f"out_{name}"] for name, _ in _OUTS)
```

```python
from contextlib import ExitStack

import concourse.bass as bass
from concourse import mybir

F32 = mybir.dt.float32
F32R = mybir.dt.float32r
I32 = mybir.dt.int32
ALU = mybir.AluOpType
ACT = mybir.ActivationFunctionType
X = mybir.AxisListType.X

P = 128
D = 1024
KC = D // P
T = 256
NB = 8
HALVES = (slice(0, KC // 2), slice(KC // 2, KC))
NT = T + NB
PAST = 2048
GROUPS = ((128, 1), (512, 4), (2048, 16))
NG = len(GROUPS)
H, HD = 16, 64
WIN = (2, 4, 8, 16)
STATE = 15
FF = 2816
FB = FF // P
NE = 8
FE = 3584
FCH = FE // 512
EPS = 1e-6
SCALE = HD ** -0.5
RING = 7
PAIRS = 3
SLAB = 2048
SLOTS = 128
PASSES = -(-NT // SLOTS)
NEG = -1e30

CONST = {}


def _lay():
    at = 0
    for name, n in (("cos", NT), ("sin", NT), ("mask", NG * 256), ("cnt", 4 * 16), ("ident", P), ("rot", P),
                    ("before", P), ("ones", P), ("iota", SLOTS * PASSES), ("tri", NE * NE), ("eps", 1), ("slot", 4), ("head", H)):
        CONST[name] = (at, at + n)
        at += n
    return at


NCONST = _lay()


def slab_plan():
    plan = []
    ada = [[("ada", s, r, 4, c, 512) for c in range(0, 3 * D, 512) for r in (0, 4)] for s in range(4)]
    plan += ada[0] + ada[1]
    for c in range(0, FF, 256):
        plan += [("w1", 0, 0, KC, c, 256), ("w3", 0, 0, KC, c, 256)]
    for c in range(0, D, 256):
        plan += [("w2", 0, r, min(8, FB - r), c, 256) for r in range(0, FB, 8)]
    plan += ada[2]
    plan += [("wkv", 0, 0, KC, c, 256) for c in range(0, 2 * D, 256)]
    plan += [("wq", 0, 0, KC, c, 256) for c in range(0, NG * D, 256)]
    plan += [("ck", t, 0, 2, 0, D) for t in range(0, NB * NG, 2)]
    plan += [("cv", t, 0, 2, 0, D) for t in range(0, NB * NG, 2)]
    plan += [("wo", 0, 0, KC, c, 256) for c in range(0, D, 256)]
    plan += ada[3]
    return plan


def yoco_step(nc, w, o):
    plan = slab_plan()
    first = {}
    for n, item in enumerate(plan):
        first.setdefault(item[:2], n)
    NPRE = len(plan)
    dmas = [2 if item[0] in ("ck", "cv") else 1 for item in plan]
    split = [n for n, item in enumerate(plan) if item[0] not in ("ck", "cv")]
    order = {n: i for i, n in enumerate(split)}
    firsts = {}
    for i, n in enumerate(split):
        firsts.setdefault(plan[n][:2], i)
    NSPLIT = len(split)
    eslabs = []
    for j in range(FCH):
        eslabs += [(1, j, 0), (1, j, 1), (3, j, 0), (3, j, 1)] + ([(2, j - 1, 0), (2, j - 1, 1)] if j else [])
    eslabs += [(2, FCH - 1, 0), (2, FCH - 1, 1)]
    PER_E = len(eslabs)
    assert PER_E % RING == 0 and PER_E % PAIRS == 0
    assert all(n in order and plan[n][0] not in ("ck", "cv") for n in range(NPRE - RING, NPRE))

    with ExitStack() as ctx:
        free = [-(-nc.sbuf_base // 64) * 64]
        placed = {}

        def sb(name, shape, dt=F32):
            n = 4
            for x in shape[1:]:
                n *= x
            placed[name] = free[0]
            free[0] += -(-n // 64) * 64
            return nc.alloc_sbuf_tensor_at(name, shape, dt, offset=placed[name])

        def over(name, other, skip, shape, dt):
            return nc.alloc_sbuf_tensor_at(name, shape, dt, offset=placed[other] + 4 * skip)

        def sem(name):
            return ctx.enter_context(nc.semaphore(name))

        bank = [ctx.enter_context(nc.psum_tensor(f"bank{i}", [P, 512], F32)) for i in range(8)]

        ring = sb("ring", [P, RING, SLAB])
        w_hi = sb("w_hi", [P, PAIRS, SLAB], F32R)
        w_lo = sb("w_lo", [P, PAIRS, SLAB], F32R)
        const = sb("const", [P, NCONST])

        def cst(name):
            a, b = CONST[name]
            return const[:, a:b]

        cos, sin, ident, rot, before, ones, iota = (cst(n) for n in ("cos", "sin", "ident", "rot", "before", "ones", "iota"))
        one1 = ones[:, 0:1]
        eps1 = cst("eps")
        mask = cst("mask").rearrange("p (g k) -> p g k", g=NG)
        invcnt = cst("cnt").rearrange("p (g k) -> p g k", g=4)
        tri = cst("tri").rearrange("p (a b) -> p a b", a=NE)

        xT = sb("xT", [P, KC, NT])
        hT = sb("hT", [P, KC, NT])
        mT = sb("mT", [P, KC, NT])
        tT = sb("tT", [P, KC, NT])
        ada = sb("ada", [P, 4, 24, 1 + NB])
        vec1 = sb("vec1", [P, 96])
        vec2 = sb("vec2", [P, 80])
        vrow1 = sb("vrow1", [96, P])
        vrow2 = sb("vrow2", [80, P])
        cT = sb("cT", [P, KC, 1 + NB])
        c18 = sb("c18", [P, KC, 18], F32R)
        tHi = over("tHi", "tT", 0, [P, KC, NT], F32R)
        mLo = over("mLo", "mT", 0, [P, KC, NT], F32R)
        hLo = over("hLo", "hT", 0, [P, KC, NT], F32R)
        shared = sb("shared", [P, 4 * NT])
        arow = shared[0:18, 0:1024].rearrange("p (a n) -> p a n", a=2)
        g_new = shared[:, :].rearrange("p (a n) -> p a n", a=4)
        std = sb("std", [P, NT])
        rstd = sb("rstd", [P, NT])
        small = sb("small", [P, KC, NB])
        rw = sb("rw", [P, KC, NE])
        rb = sb("rb", [1, NE])
        flag = sb("flag", [P, 1], I32)
        PHASE = 12300
        phase = sb("phase", [P, PHASE])

        def at(offset, *shape):
            n = 1
            for s in shape:
                n *= s
            assert offset + n <= PHASE, (offset, shape)
            v = phase[:, offset:offset + n]
            if len(shape) == 2:
                v = v.rearrange("p (a b) -> p a b", a=shape[0])
            if len(shape) == 3:
                v = v.rearrange("p (a b c) -> p a b c", a=shape[0], b=shape[1])
            if len(shape) == 4:
                v = v.rearrange("p (a b c d) -> p a b c d", a=shape[0], b=shape[1], c=shape[2])
            return v

        EXT = STATE + T
        xtok = at(0, 3, D)
        crow = at(3072, D)
        strow = at(4096, D)
        ext = at(5120, KC, EXT)
        sExt = at(5120 + KC * EXT, KC, NB, STATE + 1)
        sum_a = at(0, KC, EXT)
        sum_b = at(KC * EXT, KC, EXT)
        ext = at(2 * KC * EXT, KC, EXT)
        sExt = at(3 * KC * EXT, KC, NB, STATE + 1)
        poolw = at(3 * KC * EXT + KC * NB * (STATE + 1), 4, 2, 256)
        pstate = at(0, D)
        gHi = over("gHi", "phase", 0, [P, FB, NT], F32R)
        gLo = over("gLo", "phase", FB * NT, [P, FB, NT], F32R)
        silu_up = at(2 * FB * NT, 2, NT)
        kT = at(0, KC, NT)
        vtok = at(KC * NT, 2, D)
        vnew = at(KC * NT + 2 * D, KC, NB)
        qT = at(KC * NT + 2 * D + KC * NB, NG * KC, NT)
        ktok = qT.rearrange("p a b -> p (a b)")[:, 0:3 * D].rearrange("p (a b) -> p a b", a=3)
        vntok = qT.rearrange("p a b -> p (a b)")[0:NB, 3 * D:4 * D]
        vraw = qT.rearrange("p a b -> p (a b)")[:, 4 * D:4 * D + KC * NT].rearrange("p (a b) -> p a b", a=KC)
        QEND = KC * NT + 2 * D + KC * NB + NG * KC * NT
        woT = at(0, KC, NT)
        hflat = hT[:, :, :].rearrange("p a b -> p (a b)")
        tflat = tT[:, :, :].rearrange("p a b -> p (a b)")
        kprod = hflat[:, 0:384].rearrange("p (g b j s) -> p g b j s", g=NG, b=NB, j=KC)
        s_scores = hflat[:, 384:768].rearrange("p (g n) -> p g n", g=NG)
        s_soft = hflat[:, 768:768 + 387]
        s_pT = hflat[:, 1156:1156 + 768].rearrange("p (g b n) -> p g b n", g=NG, b=NB)
        pnewb = hflat[:, 1924:1924 + P]
        s_stat = hflat[:, 2060:2064]
        q_hi = tHi[:, :, :].rearrange("p a b -> p (a b)")[:, 0:D]
        q_lo = mLo[:, :, :].rearrange("p a b -> p (a b)")[:, D:2 * D]
        k_prod = [tflat[:, D:2 * D], mT[:, :, :].rearrange("p a b -> p (a b)")[:, 0:D]]
        q_pick = over("q_pick", "phase", QEND, [P, 2, P], F32R)
        sv_own = [tflat[:, D * i:D * (i + 1)] for i in range(2)]
        otok = hflat[:, 0:2048].rearrange("p (c n) -> p c n", c=2)
        sm = [a[:, 3 * i:3 * i + 3, 0:256] for a in (tT, mT) for i in range(2)]
        rot_a, rot_b = at(QEND, NT), at(QEND + NT, NT)
        rawT = at(QEND + 2 * NT, 4, NT)
        p_sum = at(QEND, 2, 256)
        p_stat = at(QEND + 512, 8, 4)
        p_T = at(QEND + 544, 2, 2, P)
        htok_hi = over("htok_hi", "phase", 0, [P, 3, D], F32R)
        htok_lo = over("htok_lo", "phase", 8192, [P, 3, D], F32R)
        xe_hi = over("xe_hi", "phase", 3072, [P, KC, SLOTS], F32R)
        xe_lo = over("xe_lo", "phase", 11264, [P, KC, SLOTS], F32R)
        upT_hi = over("upT_hi", "tT", 0, [P, 4, P], F32R)
        upT_lo = over("upT_lo", "tT", 512, [P, 4, P], F32R)
        up_s = at(4096, 512)
        up = at(4608, 512)
        ye = at(5632, D)
        disp = over("disp", "phase", 6656, [P, 3, SLOTS], F32R)
        dispg = at(7040, 3, SLOTS)
        comb = at(7424, NT)
        lg = at(7688, 3, NE)
        sel = at(7712, 3, NE)
        posm = at(7736, 3, NE)
        gate = at(7760, 3, NE)
        r_a = at(4096, 3, NE, NE)
        r_b = at(4096 + 3 * NE * NE, 3, NE, NE)
        r_c = at(7912, 3, NE)
        r_s = at(7936, 3, 4)
        ytok = at(0, 3, D)

        slab_in = [sem(f"slab_in{i}") for i in range(RING)]
        hi_done, lo_done, lo_done_pool = sem("hi_done"), sem("lo_done"), sem("lo_done_pool")
        pair_used = sem("pair_used")
        cache_used = sem("cache_used")
        arow_ready, ada_turned, c_split = sem("arow_ready"), sem("ada_turned"), sem("c_split")
        act_hi, act_lo = sem("act_hi"), sem("act_lo")
        g_hi, g_lo = sem("g_hi"), sem("g_lo")
        xe_hi_ready, xe_ready, upT_hi_ready, upT_ready = (sem(n) for n in ("xe_hi_ready", "xe_ready", "upT_hi_ready", "upT_ready"))
        in_const, in_vec, in_x, in_state, in_pool, in_router = (sem(n) for n in (
            "in_const", "in_vec", "in_x", "in_state", "in_pool", "in_router"))
        act_step, dve_step, pool_step = sem("act_step"), sem("dve_step"), sem("pool_step")
        vec_turned, vec_read = sem("vec_turned"), sem("vec_read")
        c_silu, c_turned, c_read = sem("c_silu"), sem("c_turned"), sem("c_read")
        x_turned, x_taken = sem("x_turned"), sem("x_taken")
        st_turned, st_taken = sem("st_turned"), sem("st_taken")
        ada_taken = sem("ada_taken")
        norm_in, sq_ready, norm_summed, std_ready = sem("norm_in"), sem("sq_ready"), sem("norm_summed"), sem("std_ready")
        h_ready = sem("h_ready")
        pm_ready, pool_summed, pool_taken = sem("pm_ready"), sem("pool_summed"), sem("pool_taken")
        ps_turned = sem("ps_turned")
        fup_silu, fup_done = sem("fup_silu"), sem("fup_done")
        fdn_taken = sem("fdn_taken")
        lin_raw, rot_summed, rot_done = sem("lin_raw"), sem("rot_summed"), sem("rot_done")
        kv_turned, kv_taken = sem("kv_turned"), sem("kv_taken")
        pair_ready = sem("pair_ready")
        qr_turned, qr_hi, qr_taken, picked, q_spread, k_used, k_halved, k_summed, s_turned = (sem(n) for n in (
            "qr_turned", "qr_hi", "qr_taken", "picked", "q_spread", "k_used", "k_halved", "k_summed", "s_turned"))
        s_max, s_exp, s_prob, sp_turned, sp_taken, pn_ready, pn_spread, sv_done = (sem(n) for n in (
            "s_max", "s_exp", "s_prob", "sp_turned", "sp_taken", "pn_ready", "pn_spread", "sv_done"))
        sv_picked, sv_turned = sem("sv_picked"), sem("sv_turned")
        a_scored, a_max, a_exp, a_sum, a_turned, a_copied, a_out, a_taken = (sem(n) for n in (
            "a_scored", "a_max", "a_exp", "a_sum", "a_turned", "a_copied", "a_out", "a_taken"))
        ot_turned, ot_taken = sem("ot_turned"), sem("ot_taken")
        wo_taken = sem("wo_taken")
        lg_summed, lg_max, lg_exp, sel_ready, pos_summed = (sem(n) for n in (
            "lg_summed", "lg_max", "lg_exp", "sel_ready", "pos_summed"))
        ht_turned, ht_hi, ht_taken = sem("ht_turned"), sem("ht_hi"), sem("ht_taken")
        moe_ready, flag_ready = sem("moe_ready"), sem("flag_ready")
        route_built, gathered, comb_turned, comb_copied = (sem(n) for n in (
            "route_built", "gathered", "comb_turned", "comb_copied"))
        silu_done, up_ready, up_turned = (sem(n) for n in ("silu_done", "up_ready", "up_turned"))
        y0_copied, y1_copied, c_summed, y_added = (sem(n) for n in ("y0_copied", "y1_copied", "c_summed", "y_added"))
        y_turned, y_taken = sem("y_turned"), sem("y_taken")
        out_done, moved_up = sem("out_done"), sem("moved_up")
        k_rows, v_rows, ps_rows = sem("k_rows"), sem("v_rows"), sem("ps_rows")

        def slab_source(item):
            name, k, r, nr, c, ncol = item
            a = {"ada": lambda: (w["ada_mix_w"], w["ada_ffn_w"])[k % 2][k // 2], "w1": lambda: w["ffn_w1"][0],
                 "w3": lambda: w["ffn_w3"][0], "w2": lambda: w["ffn_w2"][0], "wkv": lambda: w["w_kv"],
                 "wq": lambda: w["w_q"][0], "wo": lambda: w["w_o"][0]}[name]()
            return a[r * P:(r + nr) * P, c:c + ncol].rearrange("(k p) n -> p k n", p=P)

        def item_is(n, name):
            return plan[n][0] == name

        def slab_view(n):
            name, k, r, nr, c, ncol = plan[n]
            return ring[:, n % RING, 0:nr * ncol].rearrange("p (k n) -> p k n", k=nr)

        def slab_total(n):
            return 16 * sum(dmas[m] for m in range(n % RING, n + 1, RING))

        before_experts = [16 * sum(dmas[m] for m in range(r, NPRE, RING)) for r in range(RING)]

        def expert_source(e, m, j, half):
            if m == 2:
                rows = slice(512 * j + 256 * half, 512 * j + 256 * (half + 1))
                return w["moe_w2"][0, bass.ds(e, 1), rows, :].rearrange("a (k p) n -> p (a k) n", p=P)
            return w[f"moe_w{m}"][0, bass.ds(e, 1), 512 * half:512 * (half + 1), 512 * j:512 * (j + 1)].rearrange("a (k p) n -> p (a k) n", p=P)

        def used_by(e, c, m, j, half=1):
            return e * PER_E + (NSPLIT + c * NE * PER_E + eslabs.index((m, j, half)) + 1)

        def owner(i):
            name, k = plan[split[i]][:2]
            j = i - firsts[(name, k)]
            return "pool" if name == "ada" and (j % 3 != 0 if k == 1 else j % 3 == 2 if k >= 2 else False) else "vector"

        def lows(i, who):
            return sum(owner(m) == who for m in range(i + 1))

        LO_PRE = lows(NSPLIT - 1, "vector")

        def need_split(eng, i):
            if owner(i) == "vector":
                eng.wait_ge(lo_done, lows(i, "vector"))
            else:
                eng.wait_ge(lo_done_pool, lows(i, "pool"))

        def parts(i):
            name, k, r, nr, c, ncol = plan[split[i]]
            return [t[:, i % PAIRS, 0:nr * ncol].rearrange("p (k n) -> p k n", k=nr) for t in (w_hi, w_lo)]

        def remainder(eng, i, done):
            n = split[i]
            size = plan[n][3] * plan[n][5]
            eng.wait_ge(hi_done, i + 1)
            eng.tensor_tensor(w_lo[:, i % PAIRS, 0:size], ring[:, n % RING, 0:size], w_hi[:, i % PAIRS, 0:size].bitcast(F32),
                              ALU.subtract).then_inc(done, 1)

        block = ctx.enter_context(nc.Block())

        @block.sync
        def _(sp):
            sp.dma_start(const[:, :], w["shape_constants"]).then_inc(in_const, 16)
            sp.dma_start(crow[0:1, :], w["c_prompt"]).then_inc(in_vec, 16)
            sp.dma_start(crow[1:9, :], w["c_sample"]).then_inc(in_vec, 16)
            sp.dma_start(vrow1[0:48, :], w["ada_mix_b"].rearrange("l (m p) -> (l m) p", p=P)).then_inc(in_vec, 16)
            sp.dma_start(vrow1[48:96, :], w["ada_ffn_b"].rearrange("l (m p) -> (l m) p", p=P)).then_inc(in_vec, 16)
            for i, name in enumerate(("g_pre_mix", "g_post_mix", "g_pre_ffn", "g_post_ffn")):
                sp.dma_start(vrow2[16 * i:16 * (i + 1), :], w[name].rearrange("l (m p) -> (l m) p", p=P)).then_inc(in_vec, 16)
            sp.dma_start(vrow2[64:72, :], w["g_kv"].rearrange("(m p) -> m p", p=P)).then_inc(in_vec, 16)
            sp.dma_start(vrow2[72:80, :], w["pool_scale"][0].rearrange("(m p) -> m p", p=P)).then_inc(in_vec, 16)
            sp.dma_start(xtok[:, 0:2, :], w["x_prompt"][0].rearrange("(c p) d -> p c d", p=P)).then_inc(in_x, 16)
            sp.dma_start(xtok[0:NB, 2, :], w["x_sample"][:, 0, :]).then_inc(in_x, 16)
            sp.dma_start(strow[0:NB * STATE, :], w["state_pool"][:, 0].rearrange("b t d -> (b t) d")).then_inc(in_state, 16)
            for n, item in enumerate(plan):
                if n >= RING:
                    m = n - RING
                    if item_is(m, "ck"):
                        sp.wait_ge(k_used, 2 * (m - first[("ck", 0)]) + 2)
                    elif item_is(m, "cv"):
                        sp.wait_ge(cache_used, m - first[("cv", 0)] + 1)
                    else:
                        need_split(sp, order[m])
                if item[0] in ("ck", "cv"):
                    rows = w["cache_k" if item[0] == "ck" else "cache_v"]
                    for q in range(2):
                        b, dil = (item[1] + q) // NG, GROUPS[(item[1] + q) % NG][1]
                        sp.dma_start(slab_view(n)[:, q, :], rows[b, PAST - P * dil::dil].rearrange("t h d -> t (h d)"))\
                          .then_inc(slab_in[n % RING], 16)
                else:
                    sp.dma_start(slab_view(n), slab_source(item)).then_inc(slab_in[n % RING], 16)
                if n == RING - 1:
                    sp.dma_start(poolw[:, :, :, :], w["pool_w"][0].rearrange("g (k p) n -> p g k n", p=P)).then_inc(in_pool, 16)
                    sp.dma_start(rw[:, :, :], w["router_w"][0].rearrange("(k p) n -> p k n", p=P)).then_inc(in_router, 16)
                    sp.dma_start(rb[:, :], w["router_b"]).then_inc(in_router, 16)

            def experts(e, c, first=False):
                for k, (m, j, half) in enumerate(eslabs):
                    slot = (NPRE + k) % RING
                    if first and k < RING:
                        need_split(sp, NSPLIT - RING + k)
                    else:
                        sp.wait_ge(lo_done, e * PER_E + (LO_PRE + c * NE * PER_E + k - RING + 1))
                    sp.dma_start(ring[:, slot, :].rearrange("p (k n) -> p k n", k=(2 if m == 2 else 4)), expert_source(e, m, j, half))\
                      .then_inc(slab_in[slot], 16)

            experts(0, 0, first=True)
            with sp.Fori(1, NE) as e:
                experts(e, 0)
            sp.wait_ge(flag_ready, 1)
            overflow = sp.value_load(flag[0:1, 0:1], min_val=0, max_val=1)
            with sp.If(overflow > 0):
                for c in range(1, PASSES):
                    with sp.Fori(0, NE) as e:
                        experts(e, c)

        @block.tensor
        def _(pe):
            def need_slab(n):
                pe.wait_ge(slab_in[n % RING], slab_total(n))

            def three(out, a, b, start, stop):
                pe.matmul(out, a[0], b[0], start=start, stop=False, skip_group_check=True)
                pe.matmul(out, a[0], b[1], start=False, stop=False, skip_group_check=True)
                return pe.matmul(out, a[1], b[0], start=False, stop=stop, skip_group_check=True)

            pe.wait_ge(in_const, 16)
            pe.wait_ge(in_vec, 16 * 10)
            pe.transpose(bank[0][:, 0:96], vrow1[:, :], ident[0:96, 0:96])
            pe.transpose(bank[0][:, 96:176], vrow2[:, :], ident[0:80, 0:80]).then_inc(vec_turned, 1)
            pe.wait_ge(c_silu, 1)
            for k in range(KC):
                mm = pe.transpose(bank[1][:, 9 * k:9 * k + 9], crow[0:9, P * k:P * (k + 1)], ident[0:9, 0:9])
            mm.then_inc(c_turned, 1)
            pe.wait_ge(in_x, 32)
            for k in range(KC):
                if k >= 2:
                    pe.wait_ge(x_taken, k - 1)
                b = bank[2 + k % 2]
                for c, n in ((0, P), (1, P), (2, NB)):
                    mm = pe.transpose(b[:, c * P:c * P + n], xtok[0:n, c, P * k:P * (k + 1)], ident[0:n, 0:n])
                mm.then_inc(x_turned, 1)
            pe.wait_ge(in_state, 16)
            for k in range(KC):
                if k >= 2:
                    pe.wait_ge(st_taken, k - 1)
                pe.transpose(bank[4 + k % 2][:, 0:120], strow[0:120, P * k:P * (k + 1)], ident[0:120, 0:120])\
                  .then_inc(st_turned, 1)

            def ada_columns(s, j):
                pe.wait_ge(arow_ready, 6 * s + j + 1)
                if s >= 1 and j == 0:
                    pe.wait_ge(ada_taken, s)
                for m in range(4):
                    mm = pe.transpose(bank[6][:, 18 * (4 * j + m):18 * (4 * j + m + 1)], arow[:, j % 2, P * m:P * (m + 1)],
                                      ident[0:18, 0:18])
                mm.then_inc(ada_turned, 1)

            def ada_product(s, j):
                if 6 * s + j >= 2:
                    pe.wait_ge(arow_ready, 6 * s + j - 1)
                out = bank[2 + j % 2]
                for half in range(2):
                    i = firsts[("ada", s)] + 2 * j + half
                    need_split(pe, i)
                    hi, lo = parts(i)
                    for k in range(4):
                        pe.matmul(out[0:18, :], c18[:, 4 * half + k, :], hi[:, k, :], start=(half == 0 and k == 0), stop=False,
                                  skip_group_check=True)
                        mm = pe.matmul(out[0:9, :], c18[:, 4 * half + k, 0:9], lo[:, k, :], start=False, stop=(half == 1 and k == 3),
                                       skip_group_check=True)
                    mm.then_inc(pair_used, 1)
                if j >= 1:
                    ada_columns(s, j - 1)

            def norm_sum(i):
                for k in range(KC):
                    if k % (KC // 2) == 0:
                        pe.wait_ge(sq_ready, 2 * i + 2 * k // KC + 1)
                    mm = pe.matmul(bank[7][:, 0:NT], ones, tT[:, k, :], start=(k == 0), stop=(k == KC - 1))
                mm.then_inc(norm_summed, 1)

            def pool_mixer():
                pe.wait_ge(in_pool, 16)
                pe.wait_ge(pm_ready, 1)
                for i in range(KC):
                    g, m = i // 2, i % 2
                    if i >= 2:
                        pe.wait_ge(pool_taken, i - 1)
                    for k in range(2):
                        mm = pe.matmul(bank[i % 2][:, 0:NT], poolw[:, g, k, P * m:P * (m + 1)], tT[:, 2 * g + k, :],
                                       start=(k == 0), stop=(k == 1))
                    mm.then_inc(pool_summed, 1)
                for k in range(KC):
                    mm = pe.transpose(bank[4 + k // 4][0:STATE + NB, P * (k % 4):P * (k % 4 + 1)], hT[:, k, T - STATE:NT], ident)
                mm.then_inc(ps_turned, 1)

            pe.wait_ge(c_split, 1)
            pe.wait_ge(x_taken, KC)
            for j in range(6):
                ada_product(0, j)
                if j == 0:
                    norm_sum(0)
            ada_columns(0, 5)
            for j in range(6):
                ada_product(1, j)
                if j == 2:
                    pool_mixer()
                    norm_sum(1)
                if j == 4:
                    norm_sum(2)
            ada_columns(1, 5)
            def block_pair(i, a, banks, k0=0, first_k=True, last_k=True, operand=0):
                need_split(pe, i)
                hi, lo = parts(i)
                nr = plan[split[i]][3]
                for m in range(2):
                    for k in range(nr):
                        if operand and m == 0 and k % (KC // 2) == 0:
                            pe.wait_ge(act_lo, 2 * operand - 1 + 2 * k // KC)
                        mm = three(bank[banks[m]][:, 0:NT], (hi[:, k, P * m:P * (m + 1)], lo[:, k, P * m:P * (m + 1)]),
                                   (a[0][:, k0 + k, :], a[1][:, k0 + k, :]), first_k and k == 0, last_k and k == nr - 1)
                mm.then_inc(pair_used, 1)

            i0 = firsts[("w1", 0)]
            for c in range(FB // 2):
                if c >= 2:
                    pe.wait_ge(fup_done, 2 * (c - 1))
                b = 4 * (c % 2)
                block_pair(i0 + 2 * c, (tHi, mLo), (b, b + 1), operand=int(c == 0))
                block_pair(i0 + 2 * c + 1, (tHi, mLo), (b + 2, b + 3))
            i0 = firsts[("w2", 0)]
            pe.wait_ge(fup_done, FB)
            pe.wait_ge(g_lo, FB)
            for c in range(4):
                if c >= 2:
                    pe.wait_ge(fdn_taken, 2 * (c - 1))
                for r in range(3):
                    block_pair(i0 + 3 * c + r, (gHi, gLo), ((0, 1), (4, 5))[c % 2], 8 * r, r == 0, r == 2)
            for j in range(6):
                ada_product(2, j)
                if j == 0:
                    norm_sum(3)
                if j == 2:
                    norm_sum(4)
            ada_columns(2, 5)

            def rotate(i):
                if i >= 2:
                    pe.wait_ge(rot_done, i - 1)
                pe.wait_ge(lin_raw, i + 1 + (KC if i >= KC else 0))
                pe.matmul(bank[4 + i % 2][:, 0:NT], rot, rawT[:, i % 4, :], start=True, stop=True).then_inc(rot_summed, 1)

            def lin_pair(i, c):
                if c >= 2:
                    pe.wait_ge(lin_raw, 2 * (c - 1))
                b = 2 * (c % 2)
                block_pair(i, (tHi, mLo), (b, b + 1), operand={0: 2, 8: 3}.get(c, 0))

            def token_rows(q):
                if q == 0:
                    pe.wait_ge(rot_done, KC)
                if q == 2:
                    pe.wait_ge(lin_raw, 2 * KC)
                if q >= 1:
                    pe.wait_ge(kv_taken, q)
                for m in range(4):
                    k = 4 * (q % 2) + m
                    src = (kT if q < 2 else vraw)
                    for c, n in ((0, P), (1, P), (2, NB)):
                        mm = pe.transpose(bank[(4, 5, 7)[c]][0:n, P * m:P * (m + 1)], src[:, k, c * P:c * P + n], ident)
                mm.then_inc(kv_turned, 1)

            for c in range(8):
                lin_pair(firsts[("wkv", 0)] + c, c)
                if 1 <= c <= 4:
                    rotate(2 * c - 2)
                    rotate(2 * c - 1)
                if c >= 6:
                    token_rows(c - 6)
            for c in range(12):
                lin_pair(firsts[("wq", 0)] + c, 8 + c)
                if c < 2:
                    token_rows(c + 2)
                if c == 1:
                    pe.wait_ge(kv_taken, 4)
                if c >= 1:
                    rotate(KC + 2 * c - 2)
                    rotate(KC + 2 * c - 1)
            rotate(KC + 22)
            rotate(KC + 23)

            pe.wait_ge(pair_ready, 1)
            for g in range(NG):
                mm = pe.matmul(bank[5][:, g:g + 1], kprod[:, g].rearrange("p b j s -> p (b j s)"), one1, start=True, stop=True)
            for g in range(NG):
                for j in range(KC):
                    mm = pe.matmul(bank[6 + j // 4][32 * g:32 * (g + 1), P * (j % 4):P * (j % 4 + 1)], qT[:, g * KC + j, NT - 32:NT], ident,
                                   start=True, stop=True)
            mm.then_inc(qr_turned, 1)
            pe.wait_ge(qr_taken, 1)
            NTILE = NB * NG
            for t in range(NTILE):
                b, g = t // NG, t % NG
                pe.wait_ge(picked, t + 1)
                if t >= 2:
                    pe.wait_ge(k_used, t - 1)
                rows = slice(32 * g, 32 * (g + 1))
                for q in range(2):
                    for part in (q_hi, q_lo):
                        mm = pe.matmul(bank[2 * (t % 2) + q][:, :], q_pick[rows, t % 2, :], part[rows, 512 * q:512 * (q + 1)],
                                       start=(part is q_hi), stop=(part is q_lo))
                mm.then_inc(q_spread, 1)
            pe.wait_ge(k_summed, NTILE)
            for g in range(NG):
                mm = pe.transpose(bank[6][:, P * g:P * (g + 1)], s_scores[:, g, :], ident)
            mm.then_inc(s_turned, 1)
            pe.wait_ge(s_prob, 1)
            for g in range(NG):
                mm = pe.transpose(bank[7][:, P * g:P * (g + 1)], s_soft[:, P * g:P * (g + 1)], ident)
            mm.then_inc(sp_turned, 1)
            pe.wait_ge(pn_ready, 1)
            pe.matmul(bank[5][:, P:2 * P], pnewb, ident, start=True, stop=True).then_inc(pn_spread, 1)
            pe.wait_ge(sp_taken, 1)
            for t in range(NTILE):
                b, g = t // NG, t % NG
                n = first[("cv", 0)] + t // 2
                need_slab(n)
                for q in range(2):
                    mm = pe.matmul(bank[2 * (b // 4) + q][32 * (b % 4):32 * (b % 4 + 1), :], s_pT[:, g, b, :],
                                   slab_view(n)[:, t % 2, 512 * q:512 * (q + 1)], start=(g == 0), stop=(g == NG - 1))
                if t % 2 == 1:
                    mm.then_inc(cache_used, 1)
            for f in range(2):
                pe.wait_ge(sv_picked, f + 1)
                for k in range(KC):
                    mm = pe.matmul(bank[4][:, 8 * k + 4 * f:8 * k + 4 * f + 4], sv_own[f][:, P * k:P * (k + 1)], cst("slot"), start=True, stop=True)
            mm.then_inc(sv_turned, 1)

            units = [(h, c) for h in range(H) for c in range(2)]

            def scores(u):
                h, c = units[u]
                lo = HD * (h % 2)
                if u >= 2:
                    pe.wait_ge(a_max, u - 1)
                for g in range(NG):
                    b = bank[2 * c + g // 2]
                    n = P * (c + 1)
                    mm = pe.matmul(b[:, 256 * (g % 2):256 * (g % 2) + n], qT[lo:lo + HD, g * KC + h // 2, c * P:(c + 1) * P],
                                   kT[lo:lo + HD, h // 2, 0:n], start=True, stop=True)
                mm.then_inc(a_scored, 1)

            def weights_to_columns(u):
                h, c = units[u]
                pe.wait_ge(a_sum, u + 1)
                if u >= 2:
                    pe.wait_ge(a_copied, u - 1)
                for k in range(c + 1):
                    mm = pe.transpose(bank[4 + u % 2][:, P * k:P * (k + 1)], p_sum[:, u % 2, P * k:P * (k + 1)], ident)
                mm.then_inc(a_turned, 1)

            def values(u):
                h, c = units[u]
                pe.wait_ge(a_copied, u + 1)
                if u >= 2:
                    pe.wait_ge(a_taken, u - 1)
                for k in range(c + 1):
                    mm = pe.matmul(bank[6 + u % 2][:, 0:HD], p_T[:, u % 2, k, :], vtok[:, k, HD * h:HD * (h + 1)],
                                   start=(k == 0), stop=(k == c))
                mm.then_inc(a_out, 1)

            pe.wait_ge(sv_done, 1)
            for u in range(len(units) + 4):
                if u < len(units):
                    scores(u)
                if 3 <= u < len(units) + 3:
                    weights_to_columns(u - 3)
                if u >= 4:
                    values(u - 4)
            pe.wait_ge(a_taken, len(units))
            for k in range(KC):
                if k >= 2:
                    pe.wait_ge(ot_taken, k - 1)
                for c in range(2):
                    mm = pe.transpose(bank[k % 2][:, P * c:P * (c + 1)], otok[:, c, P * k:P * (k + 1)], ident)
                mm.then_inc(ot_turned, 1)
            for c in range(4):
                if c >= 2:
                    pe.wait_ge(wo_taken, 2 * (c - 1))
                block_pair(firsts[("wo", 0)] + c, (tHi, hLo), ((2, 3), (4, 5))[c % 2], operand=4 * (c == 0))
            pe.wait_ge(wo_taken, KC)
            for j in range(6):
                ada_product(3, j)
                if j == 0:
                    norm_sum(5)
                if j == 2:
                    norm_sum(6)
            ada_columns(3, 5)

            pe.wait_ge(h_ready, 8)
            pe.wait_ge(in_router, 32)
            for c, n in ((0, P), (1, P), (2, NB)):
                for k in range(KC):
                    pe.matmul(bank[0][0:n, NE * c:NE * (c + 1)], hT[:, k, P * c:P * c + n], rw[:, k, :], start=(k == 0), stop=False)
                mm = pe.matmul(bank[0][0:n, NE * c:NE * (c + 1)], ones[0:1, 0:n], rb[0:1, :], start=False, stop=True)
            mm.then_inc(lg_summed, 1)
            for k in range(KC):
                if k >= 2:
                    pe.wait_ge(ht_taken, k - 1)
                for c, n in ((0, P), (1, P), (2, NB)):
                    mm = pe.transpose(bank[2 + k % 2][0:n, P * c:P * (c + 1)], hT[:, k, c * P:c * P + n], ident)
                mm.then_inc(ht_turned, 1)
            pe.wait_ge(sel_ready, 1)
            rows = (P, P, NB)
            for c in range(3):
                for k in range(c + 1):
                    n = rows[k]
                    pe.matmul(bank[1][0:rows[c], NE * c:NE * (c + 1)], (before if k == c else ones)[0:n, 0:rows[c]], sel[0:n, k, :],
                              start=(k == 0), stop=(k == c))
            for k in range(3):
                mm = pe.matmul(bank[1][:, 3 * NE:4 * NE], ones[0:rows[k], :], sel[0:rows[k], k, :], start=(k == 0), stop=(k == 2))
            mm.then_inc(pos_summed, 1)
            pe.wait_ge(ht_taken, KC)
            pe.wait_ge(moe_ready, 1)

            def gather(e, c, ahead):
                pe.wait_ge(route_built, e + (c * NE + ahead + 1))
                if ahead:
                    pe.wait_ge(y_added, e * KC + KC * (c * (NE + 1) + 1))
                elif c:
                    pe.wait_ge(y_added, KC * c * (NE + 1))
                pe.wait_ge(comb_copied, e + (c * (NE + 1) + ahead + 1))
                for k in range(KC):
                    for q in range(3):
                        n = rows[q]
                        for part, last in ((htok_hi, False), (htok_lo, q == 2)):
                            mm = pe.matmul(bank[k // 4][:, P * (k % 4):P * (k % 4) + SLOTS], part[0:n, q, P * k:P * (k + 1)], disp[0:n, q, :],
                                           start=(q == 0 and part is htok_hi), stop=last)
                    if k % 4 == 3:
                        mm.then_inc(gathered, 1)
                for q in range(3):
                    n = rows[q]
                    mm = pe.transpose(bank[2][0:SLOTS, P * q:P * q + n], dispg[0:n, q, :], ident[0:n, 0:n])
                mm.then_inc(comb_turned, 1)

            def combine(e, c, blocks=range(KC)):
                if 0 in blocks:
                    pe.wait_ge(comb_copied, e + (c * (NE + 1) + 1))
                    pe.wait_ge(y0_copied, e + (c * NE + 1))
                    pe.wait_ge(y1_copied, e + (c * NE + 1))
                for k in blocks:
                    if k >= 2:
                        pe.wait_ge(y_added, e * KC + (KC * c * (NE + 1) + k - 1))
                    pe.matmul(bank[k % 2][:, 0:NT], ye[0:SLOTS, P * k:P * (k + 1)], comb[0:SLOTS, :], start=True, stop=True)\
                      .then_inc(c_summed, 1)

            def expert(e, c, last):
                def weights(m, j, half, rows):
                    k = eslabs.index((m, j, half))
                    pe.wait_ge(lo_done, e * PER_E + (LO_PRE + c * NE * PER_E + k + 1))
                    return [t[:, (NSPLIT + k) % PAIRS, :].rearrange("p (k n) -> p k n", k=rows) for t in (w_hi, w_lo)]

                def count(per, k):
                    return e * per + (c * NE * per + k)

                def product(m, j, bk):
                    for half in range(2):
                        hi, lo = weights(m, j, half, 4)
                        for i in range(4):
                            k = 4 * half + i
                            mm = three(bank[bk][0:SLOTS, :], (xe_hi[:, k, :], xe_lo[:, k, :]), (hi[:, i, :], lo[:, i, :]), k == 0, k == KC - 1)
                        mm.then_inc(pair_used, 1)

                def turn(j):
                    pe.wait_ge(up_ready, count(FCH, j + 2))
                    pe.wait_ge(upT_ready, count(FCH, j + 1))
                    for i in range(4):
                        mm = pe.transpose(bank[5][:, SLOTS * i:SLOTS * (i + 1)], up[0:SLOTS, P * i:P * (i + 1)], ident[0:SLOTS, 0:SLOTS])
                    mm.then_inc(up_turned, 1)

                def down(j):
                    pe.wait_ge(upT_ready, count(FCH, j + 2))
                    if j == 0:
                        pe.wait_ge(y0_copied, count(1, 1))
                        pe.wait_ge(y1_copied, count(1, 1))
                    for half in range(2):
                        hi, lo = weights(2, j, half, 2)
                        for i in range(2):
                            for q in range(2):
                                cols = slice(512 * q, 512 * (q + 1))
                                mm = three(bank[6 + q][0:SLOTS, :], (upT_hi[:, 2 * half + i, :], upT_lo[:, 2 * half + i, :]),
                                           (hi[:, i, cols], lo[:, i, cols]), j == 0 and half == 0 and i == 0, j == FCH - 1 and half == 1 and i == 1)
                        mm.then_inc(pair_used, 1)

                pe.wait_ge(xe_ready, count(1, 1))
                for j in range(FCH):
                    pe.wait_ge(silu_done, count(FCH, j + 1))
                    product(1, j, 3)
                    if j < 2:
                        combine(e, c, (4 * j, 4 * j + 1))
                    if j >= 1:
                        turn(j - 1)
                    pe.wait_ge(up_ready, count(FCH, j + 1))
                    product(3, j, 4)
                    if j < 2:
                        combine(e, c, (4 * j + 2, 4 * j + 3))
                    if j >= 1:
                        down(j - 1)
                turn(FCH - 1)
                if not last:
                    gather(e, c, 1)
                down(FCH - 1)

            def experts(c):
                gather(0, c, 0)
                with pe.Fori(0, NE - 1) as e:
                    expert(e, c, False)
                expert(NE - 1, c, True)
                combine(NE, c)

            experts(0)
            overflow = pe.value_load(flag[0:1, 0:1], min_val=0, max_val=1)
            with pe.If(overflow > 0):
                for c in range(1, PASSES):
                    experts(c)
            norm_sum(7)
            pe.wait_ge(h_ready, 9)
            for k in range(KC):
                if k >= 2:
                    pe.wait_ge(y_taken, k - 1)
                for q, n in ((0, P), (1, P), (2, NB)):
                    mm = pe.transpose(bank[2 + k % 2][0:n, P * q:P * (q + 1)], xT[:, k, q * P:q * P + n], ident)
                mm.then_inc(y_turned, 1)

        @block.scalar
        def _(act):
            steps = [0]

            def link(ins):
                steps[0] += 1
                ins.then_inc(act_step, 1)
                act.wait_ge(act_step, steps[0])

            split_to = [0]

            def high(i):
                n = split[i]
                size = plan[n][3] * plan[n][5]
                if i >= PAIRS:
                    act.wait_ge(pair_used, i - PAIRS + 1)
                act.wait_ge(slab_in[n % RING], slab_total(n))
                act.activation(w_hi[:, i % PAIRS, 0:size], ring[:, n % RING, 0:size], ACT.Copy).then_inc(hi_done, 1)

            def highs(end):
                while split_to[0] < min(end, NSPLIT):
                    high(split_to[0])
                    split_to[0] += 1

            def ada_rows(s, j):
                i0 = firsts[("ada", s)]
                highs(i0 + 2 * j + 1 + PAIRS)
                act.wait_ge(pair_used, i0 + 2 * j + 2)
                if 6 * s + j >= 2:
                    act.wait_ge(ada_turned, 6 * s + j - 1)
                act.activation(arow[:, j % 2, :], bank[2 + j % 2][0:18, :], ACT.Copy).then_inc(arow_ready, 1)
                highs(i0 + 2 * j + 2 + PAIRS)

            act.wait_ge(in_vec, 16 * 10)
            act.activation(crow[0:9, :], crow[0:9, :], ACT.Silu).then_inc(c_silu, 1)

            def norm(i, src):
                for hf, ks in enumerate(HALVES):
                    act.wait_ge(norm_in, 2 * i + hf + 1)
                    act.activation(tT[:, ks, :], src[:, ks, :], ACT.Square).then_inc(sq_ready, 1)
                act.wait_ge(norm_summed, i + 1)
                act.activation(std[:, :], bank[7][:, 0:NT], ACT.Sqrt, bias=eps1, scale=1.0 / D).then_inc(std_ready, 1)

            highs(PAIRS)

            def pool_out():
                for i in range(KC):
                    act.wait_ge(pool_summed, i + 1)
                    act.activation(mT[:, i, :], bank[i % 2][:, 0:NT], ACT.Copy, scale=vec2[:, 72 + i:73 + i]).then_inc(pool_taken, 1)

            def pool_state_out():
                act.wait_ge(ps_turned, 1)
                for k in range(2):
                    ins = act.activation(pstate[0:STATE + NB, 512 * k:512 * (k + 1)], bank[4 + k][0:STATE + NB, :], ACT.Copy)
                ins.then_inc(ps_rows, 1)
                act.wait_ge(ps_rows, 1)
                act.dma_start(o["pool_prompt"][0, 0], pstate[0:STATE, :]).then_inc(out_done, 16)
                act.dma_start(o["pool_sample"][:, 0, STATE - 1, :], pstate[STATE:STATE + NB, :]).then_inc(out_done, 16)

            for j in range(6):
                ada_rows(0, j)
                if j == 0:
                    norm(0, xT)
            for j in range(6):
                ada_rows(1, j)
                if j == 2:
                    pool_out()
                    norm(1, mT)
                    pool_state_out()
                if j == 4:
                    norm(2, xT)
            act.wait_ge(out_done, 32)
            def operand_high(n, out, src):
                for hf, ks in enumerate(HALVES):
                    act.wait_ge(h_ready, 2 * n - 1 + hf)
                    act.activation(out[:, ks, :], src[:, ks, :], ACT.Copy).then_inc(act_hi, 1)

            operand_high(1, tHi, hT)
            i0 = firsts[("w1", 0)]

            def g_high(c):
                for i in (2 * c, 2 * c + 1):
                    act.wait_ge(fup_done, i + 1)
                    act.activation(gHi[:, i, :], g_new[:, i % 4, :], ACT.Copy).then_inc(g_hi, 1)

            for c in range(FB // 2):
                highs(i0 + 2 * c + PAIRS)
                act.wait_ge(pair_used, i0 + 2 * c + 1)
                for m in range(2):
                    i = 2 * c + m
                    if i >= 2:
                        act.wait_ge(fup_done, i - 1)
                    act.activation(silu_up[:, i % 2, :], bank[4 * (c % 2) + m][:, 0:NT], ACT.Silu).then_inc(fup_silu, 1)
                highs(i0 + 2 * c + 1 + PAIRS)
                if c >= 1:
                    g_high(c - 1)
            g_high(FB // 2 - 1)
            highs(firsts[("ada", 2)] + PAIRS)
            for j in range(6):
                ada_rows(2, j)
                if j == 0:
                    norm(3, mT)
                if j == 2:
                    norm(4, xT)
            operand_high(2, tHi, hT)
            for c in range(8 + 12):
                i0 = firsts[("wkv", 0)] + c
                highs(min(i0 + PAIRS, firsts[("wo", 0)]))
                if c == 8:
                    operand_high(3, tHi, hT)
                act.wait_ge(pair_used, i0 + 1)
                for m in range(2):
                    src = bank[2 * (c % 2) + m][:, 0:NT]
                    if 4 <= c < 8:
                        act.activation(vraw[:, 2 * (c - 4) + m, :], src, ACT.Copy).then_inc(lin_raw, 1)
                        continue
                    r = 2 * (c if c < 4 else c - 4) + m
                    if r >= 4:
                        act.wait_ge(rot_done, r - 3)
                    act.activation(rawT[:, r % 4, :], src, ACT.Copy).then_inc(lin_raw, 1)

            act.wait_ge(qr_turned, 1)
            rows = slice(0, 32 * NG)
            for q in range(2):
                ins = act.activation(q_hi[rows, 512 * q:512 * (q + 1)], bank[6 + q][rows, :], ACT.Copy)
            ins.then_inc(qr_hi, 1)
            for t in range(NB * NG):
                b, g = t // NG, t % NG
                rows = slice(32 * g, 32 * (g + 1))
                col = 32 * (g + 1) - NB + b
                if t >= 2:
                    act.wait_ge(q_spread, t - 1)
                act.activation(q_pick[rows, t % 2, :], ident[rows, col:col + 1].to_broadcast([32, P]), ACT.Copy).then_inc(picked, 1)
            act.wait_ge(s_max, 1)
            act.activation(s_soft, s_soft, ACT.Exp, bias=s_stat[:, 0:1], accum_out=s_stat[:, 1:2]).then_inc(s_exp, 1)
            highs(firsts[("wo", 0)] + PAIRS)
            def columns_out(v):
                act.wait_ge(a_turned, v + 1)
                if v >= 2:
                    act.wait_ge(a_out, v - 1)
                act.activation(p_T[:, v % 2, 0:v % 2 + 1, :], bank[4 + v % 2][:, 0:P * (v % 2 + 1)].rearrange("p (k n) -> p k n", n=P),
                               ACT.Copy).then_inc(a_copied, 1)

            for u in range(2 * H):
                c = u % 2
                n = P * (c + 1)
                act.wait_ge(a_max, u + 1)
                act.activation(sm[u % 4][:, :, 0:n], sm[u % 4][:, :, 0:n], ACT.Exp, bias=p_stat[:, u % 8, 0:1],
                               accum_out=p_stat[:, u % 8, 1:2]).then_inc(a_exp, 1)
                if u >= 3:
                    columns_out(u - 3)
            for u in range(2 * H - 3, 2 * H):
                columns_out(u)
            for hf, ks in enumerate(HALVES):
                act.wait_ge(ot_taken, KC // 2 * (hf + 1))
                act.activation(tHi[:, ks, :], mT[:, ks, :], ACT.Copy).then_inc(act_hi, 1)
            i0 = firsts[("wo", 0)]
            for c in range(4):
                highs(i0 + c + PAIRS)
                act.wait_ge(pair_used, i0 + c + 1)
                for m in range(2):
                    act.activation(woT[:, 2 * c + m, :], bank[((2, 3), (4, 5))[c % 2][m]][:, 0:NT], ACT.Copy).then_inc(wo_taken, 1)
            for j in range(6):
                ada_rows(3, j)
                if j == 0:
                    norm(5, woT)
                if j == 2:
                    norm(6, xT)
            act.wait_ge(lg_max, 1)
            for q in range(3):
                ins = act.activation(r_c[:, q, :], lg[:, q, :], ACT.Exp, bias=r_s[:, q, 0:1])
            ins.then_inc(lg_exp, 1)
            for k in range(KC):
                act.wait_ge(ht_turned, k + 1)
                act.activation(htok_hi[:, 0:2, P * k:P * (k + 1)], bank[2 + k % 2][:, 0:256].rearrange("p (c n) -> p c n", c=2), ACT.Copy)
                act.activation(htok_hi[0:NB, 2, P * k:P * (k + 1)], bank[2 + k % 2][0:NB, 256:384], ACT.Copy).then_inc(ht_hi, 1)
            act.sem_inc(silu_done, 1)
            act.sem_inc(y0_copied, 1)

            use = [[k for k in range(PER_E) if (NPRE + k) % RING == r] for r in range(RING)]

            def high(e, c, k):
                slot, ahead = (NPRE + k) % RING, k // PER_E
                act.wait_ge(pair_used, e * PER_E + (NSPLIT + c * NE * PER_E + k - PAIRS + 1))
                act.wait_ge(slab_in[slot], e * (16 * len(use[slot])) + (
                    before_experts[slot] + 16 * ((c * NE + ahead) * len(use[slot]) + use[slot].index(k % PER_E) + 1)))
                act.activation(w_hi[:, (NSPLIT + k) % PAIRS, :], ring[:, slot, :], ACT.Copy).then_inc(hi_done, 1)

            def gathered_high(e, c, ahead):
                act.wait_ge(gathered, e * 2 + (2 * (c * NE + ahead) + 2))
                for q in range(2):
                    ins = act.activation(xe_hi[:, 4 * q:4 * q + 4, :], bank[q][:, :].rearrange("p (k n) -> p k n", k=4), ACT.Copy)
                ins.then_inc(xe_hi_ready, 1)

            def expert(e, c, last):
                def count(per, k):
                    return e * per + (c * NE * per + k)

                def turned_high(j):
                    act.wait_ge(up_turned, count(FCH, j + 1))
                    act.activation(upT_hi[:, :, :], bank[5][:, :].rearrange("p (k n) -> p k n", k=4), ACT.Copy).then_inc(upT_hi_ready, 1)

                for k, (m, j, half) in enumerate(eslabs):
                    if k + PAIRS < PER_E or not last:
                        high(e, c, k + PAIRS)
                    if (m, half) == (1, 1):
                        act.wait_ge(pair_used, used_by(e, c, 1, j))
                        act.wait_ge(up_ready, count(FCH, j + 1))
                        act.activation(up_s[0:SLOTS, :], bank[3][0:SLOTS, :], ACT.Silu).then_inc(silu_done, 1)
                        if j >= 1:
                            turned_high(j - 1)
                    if (m, j, half) == (2, FCH - 2, 1):
                        turned_high(FCH - 1)
                        if not last:
                            gathered_high(e, c, 1)
                act.wait_ge(pair_used, used_by(e, c, 2, FCH - 1))
                act.activation(ye[0:SLOTS, 0:512], bank[6][0:SLOTS, :], ACT.Copy).then_inc(y0_copied, 1)

            def experts(c):
                for k in range(PAIRS):
                    high(0, c, k)
                gathered_high(0, c, 0)
                with act.Fori(0, NE - 1) as e:
                    expert(e, c, False)
                expert(NE - 1, c, True)

            experts(0)
            overflow = act.value_load(flag[0:1, 0:1], min_val=0, max_val=1)
            with act.If(overflow > 0):
                for c in range(1, PASSES):
                    experts(c)
            norm(7, mT)
            for k in range(KC):
                act.wait_ge(y_turned, k + 1)
                act.activation(ytok[:, 0:2, P * k:P * (k + 1)], bank[2 + k % 2][:, 0:256].rearrange("p (c n) -> p c n", c=2), ACT.Copy)
                act.activation(ytok[0:NB, 2, P * k:P * (k + 1)], bank[2 + k % 2][0:NB, 256:384], ACT.Copy).then_inc(y_taken, 1)
            act.wait_ge(y_taken, KC)
            act.dma_start(o["y_prompt"][0].rearrange("(c p) d -> p c d", p=P), ytok[:, 0:2, :]).then_inc(out_done, 16)
            act.dma_start(o["y_sample"][:, 0, :], ytok[0:NB, 2, :]).then_inc(out_done, 16)
            act.wait_ge(out_done, 16 * 4)

        @block.vector
        def _(dve):
            steps = [0]

            def link(ins):
                steps[0] += 1
                ins.then_inc(dve_step, 1)
                dve.wait_ge(dve_step, steps[0])

            dve.wait_ge(vec_turned, 1)
            dve.tensor_copy(vec1[:, :], bank[0][:, 0:96])
            dve.tensor_copy(vec2[:, :], bank[0][:, 96:176]).then_inc(vec_read, 1)
            dve.wait_ge(c_turned, 1)
            dve.tensor_copy(cT[:, :, :], bank[1][:, 0:9 * KC].rearrange("p (k n) -> p k n", k=KC)).then_inc(c_read, 1)
            dve.wait_ge(c_read, 1)
            link(dve.tensor_copy(c18[:, :, 0:9], cT[:, :, :]))
            dve.tensor_tensor(c18[:, :, 9:18], cT[:, :, :], c18[:, :, 0:9].bitcast(F32), ALU.subtract).then_inc(c_split, 1)
            split_to = [0]

            def lows_to(end):
                while split_to[0] < min(end, NSPLIT):
                    if owner(split_to[0]) == "vector":
                        remainder(dve, split_to[0], lo_done)
                    split_to[0] += 1

            for k in range(KC):
                dve.wait_ge(x_turned, k + 1)
                dve.tensor_copy(xT[:, k, :], bank[2 + k % 2][:, 0:NT]).then_inc(x_taken, 1)
            dve.wait_ge(x_taken, KC)
            dve.sem_inc(norm_in, 2)
            for k in range(KC):
                dve.wait_ge(st_turned, k + 1)
                dve.tensor_copy(sExt[:, k, :, 0:STATE], bank[4 + k % 2][:, 0:120].rearrange("p (b t) -> p b t", b=NB))\
                   .then_inc(st_taken, 1)
            link(dve.memset(ext[:, :, 0:STATE], 0.0))

            def across(a, n):
                return a.unsqueeze(2).to_broadcast(list(a.shape[:2]) + [n])

            def ada_take(s, kind, layer):
                a = ada[:, s]
                dve.wait_ge(ada_turned, 6 * (s + 1))
                dve.wait_ge(vec_read, 1)
                col = 48 * kind + 24 * layer
                sums = bank[6][:, 0:432].rearrange("p (m n) -> p m n", m=24)
                link(dve.tensor_tensor(a, sums[:, :, 0:9], across(vec1[:, col:col + 24], 9), ALU.add))
                link(dve.tensor_tensor(a, a, sums[:, :, 9:18], ALU.add))
                pre, post = 32 * kind + 8 * layer, 32 * kind + 16 + 8 * layer
                dve.scalar_tensor_tensor(a[:, 8:16, :], a[:, 8:16, :], 1.0, across(vec2[:, pre:pre + 8], 9), ALU.add, ALU.mult)
                link(dve.tensor_tensor(a[:, 16:24, :], a[:, 16:24, :], across(vec2[:, post:post + 8], 9), ALU.mult))
                dve.sem_inc(ada_taken, 1)

            def wide(a, n=KC // 2):
                return a.unsqueeze(1).to_broadcast([P, n, a.shape[-1]])

            def inverse(i):
                dve.wait_ge(std_ready, i + 1)
                link(dve.reciprocal(rstd[:, :], std[:, :]))

            def normalise(src, ks):
                link(dve.tensor_tensor(tT[:, ks, :], src[:, ks, :], wide(rstd[:, :]), ALU.mult))

            def vec(s, first, ks):
                return ada[:, s, 8 * first + ks.start:8 * first + ks.stop]

            def modulate(s, out, ks, done, src=None):
                src = tT if src is None else src
                for k in range(ks.start, ks.stop):
                    dve.tensor_scalar(out[:, k, 0:T], src[:, k, 0:T], ada[:, s, 8 + k, 0:1], ada[:, s, k, 0:1], ALU.mult, ALU.add)
                link(dve.tensor_tensor(small[:, ks, :], src[:, ks, T:NT], vec(s, 1, ks)[:, :, 1:9], ALU.mult))
                link(dve.tensor_tensor(out[:, ks, T:NT], small[:, ks, :], vec(s, 0, ks)[:, :, 1:9], ALU.add))
                if done is not None:
                    dve.sem_inc(done, 1)

            def residual(s, ks, done):
                for k in range(ks.start, ks.stop):
                    dve.scalar_tensor_tensor(xT[:, k, 0:T], tT[:, k, 0:T], ada[:, s, 16 + k, 0:1], xT[:, k, 0:T], ALU.mult, ALU.add)
                link(dve.tensor_tensor(small[:, ks, :], tT[:, ks, T:NT], vec(s, 2, ks)[:, :, 1:9], ALU.mult))
                link(dve.tensor_tensor(xT[:, ks, T:NT], xT[:, ks, T:NT], small[:, ks, :], ALU.add))
                if done is not None:
                    dve.sem_inc(done, 1)

            lows_to(firsts[("ada", 0)] + 2 + PAIRS)
            inverse(0)
            for ks in HALVES:
                normalise(xT, ks)
                lows_to(firsts[("ada", 0)] + 4 + PAIRS)
            lows_to(firsts[("ada", 1)])
            ada_take(0, 0, 0)
            for ks in HALVES:
                modulate(0, hT, ks, None)
            lows_to(firsts[("ada", 1)] + 3)
            link(dve.tensor_copy(ext[:, :, STATE:EXT], hT[:, :, 0:T]))
            link(dve.tensor_copy(sExt[:, :, :, STATE], hT[:, :, T:NT]))
            link(dve.tensor_tensor(sum_a[:, :, 1:EXT], ext[:, :, 1:EXT], ext[:, :, 0:EXT - 1], ALU.add))
            link(dve.tensor_tensor(sum_b[:, 2:KC, 3:EXT], sum_a[:, 2:KC, 3:EXT], sum_a[:, 2:KC, 1:EXT - 2], ALU.add))
            link(dve.tensor_tensor(sum_a[:, 4:KC, 7:EXT], sum_b[:, 4:KC, 7:EXT], sum_b[:, 4:KC, 3:EXT - 4], ALU.add))
            link(dve.tensor_tensor(sum_b[:, 6:KC, 15:EXT], sum_a[:, 6:KC, 15:EXT], sum_a[:, 6:KC, 7:EXT - 8], ALU.add))
            lows_to(firsts[("ada", 1)] + 6)
            for g, n in enumerate(WIN):
                s = (sum_a, sum_b)[g % 2]
                ks = slice(2 * g, 2 * g + 2)
                link(dve.scalar_tensor_tensor(tT[:, ks, 16:T], s[:, ks, STATE + 16:EXT], 1.0 / n, ext[:, ks, STATE + 16:EXT],
                                              ALU.mult, ALU.subtract))
                link(dve.tensor_tensor(tT[:, ks, 0:16], s[:, ks, STATE:STATE + 16],
                                       invcnt[:, g, :].unsqueeze(1).to_broadcast([P, 2, 16]), ALU.mult))
                link(dve.tensor_tensor(tT[:, ks, 0:16], tT[:, ks, 0:16], ext[:, ks, STATE:STATE + 16], ALU.subtract))
                for k in range(2 * g, 2 * g + 2):
                    link(dve.tensor_reduce(small[:, k, :], sExt[:, k, :, STATE + 1 - n:STATE + 1], X, ALU.add))
                    link(dve.scalar_tensor_tensor(tT[:, k, T:NT], small[:, k, :], 1.0 / n, sExt[:, k, :, STATE], ALU.mult, ALU.subtract))
            dve.sem_inc(pm_ready, 1)
            i0 = firsts[("ada", 1)]
            lows_to(i0 + 4 + PAIRS)
            for hf in range(2):
                dve.wait_ge(pool_taken, KC // 2 * (hf + 1))
                dve.sem_inc(norm_in, 1)
            inverse(1)
            for ks in HALVES:
                normalise(mT, ks)
                residual(0, ks, norm_in)
                lows_to(i0 + 7 + PAIRS)
            lows_to(i0 + 10 + PAIRS)
            inverse(2)
            dve.wait_ge(ps_turned, 1)
            for ks in HALVES:
                normalise(xT, ks)
                lows_to(firsts[("w1", 0)] + PAIRS)
            ada_take(1, 1, 0)
            for ks in HALVES:
                modulate(1, hT, ks, h_ready)
            def operand_low(n, out, src, hi):
                for hf, ks in enumerate(HALVES):
                    dve.wait_ge(act_hi, 2 * n - 1 + hf)
                    dve.tensor_tensor(out[:, ks, :], src[:, ks, :], hi[:, ks, :].bitcast(F32), ALU.subtract).then_inc(act_lo, 1)

            dve.wait_ge(out_done, 32)
            operand_low(1, mLo, hT, tHi)
            i0 = firsts[("w1", 0)]

            def g_low(c):
                for i in (2 * c, 2 * c + 1):
                    dve.wait_ge(g_hi, i + 1)
                    dve.tensor_tensor(gLo[:, i, :], g_new[:, i % 4, :], gHi[:, i, :].bitcast(F32), ALU.subtract).then_inc(g_lo, 1)

            for c in range(FB // 2):
                lows_to(i0 + 2 * c + PAIRS)
                lows_to(i0 + 2 * c + 1 + PAIRS)
                dve.wait_ge(pair_used, i0 + 2 * c + 2)
                for m in range(2):
                    i = 2 * c + m
                    dve.wait_ge(fup_silu, i + 1)
                    if i >= 4:
                        dve.wait_ge(g_lo, i - 3)
                    dve.tensor_tensor(g_new[:, i % 4, :], bank[4 * (c % 2) + 2 + m][:, 0:NT], silu_up[:, i % 2, :], ALU.mult).then_inc(fup_done, 1)
                if c >= 1:
                    g_low(c - 1)
            g_low(FB // 2 - 1)
            i0 = firsts[("w2", 0)]
            for c in range(4):
                lows_to(i0 + 3 * c + 3 + PAIRS)
                dve.wait_ge(pair_used, i0 + 3 * c + 3)
                for m in range(2):
                    dve.tensor_copy(mT[:, 2 * c + m, :], bank[((0, 1), (4, 5))[c % 2][m]][:, 0:NT]).then_inc(fdn_taken, 1)
            for hf in range(2):
                dve.wait_ge(fdn_taken, KC // 2 * (hf + 1))
                dve.sem_inc(norm_in, 1)
            i0 = firsts[("ada", 2)]
            lows_to(i0 + 2 + PAIRS)
            inverse(3)
            for hf, ks in enumerate(HALVES):
                normalise(mT, ks)
                residual(1, ks, norm_in)
                lows_to(i0 + (4, 8)[hf] + PAIRS)
            inverse(4)
            for ks in HALVES:
                normalise(xT, ks)
                for k in range(ks.start, ks.stop):
                    ins = dve.tensor_scalar(hT[:, k, :], tT[:, k, :], vec2[:, 64 + k:65 + k], None, ALU.mult)
                link(ins)
                dve.sem_inc(h_ready, 1)
                if ks is HALVES[0]:
                    lows_to(i0 + 10 + PAIRS)
            operand_low(2, mLo, hT, tHi)

            def rope(i, out):
                dve.wait_ge(rot_summed, i + 1)
                link(dve.tensor_tensor(rot_a, bank[4 + i % 2][:, 0:NT], sin, ALU.mult))
                link(dve.tensor_tensor(rot_b, rawT[:, i % 4, :], cos, ALU.mult))
                dve.tensor_tensor(out, rot_a, rot_b, ALU.add).then_inc(rot_done, 1)
                dve.wait_ge(rot_done, i + 1)

            def rows_out(q):
                dve.wait_ge(kv_turned, q + 1)
                cols = slice(512 * (q % 2), 512 * (q % 2) + 512)
                rows = (ktok[:, 0, cols], ktok[:, 1, cols], ktok[0:NB, 2, cols]) if q < 2 else \
                    (vtok[:, 0, cols], vtok[:, 1, cols], vntok[:, cols])
                dve.tensor_copy(rows[0], bank[4][:, :])
                dve.tensor_copy(rows[1], bank[5][:, :])
                dve.tensor_copy(rows[2], bank[7][0:NB, :]).then_inc(kv_taken, 1)

            i0 = firsts[("wkv", 0)]
            for c in range(8):
                lows_to(i0 + c + PAIRS)
                if 1 <= c <= 4:
                    rope(2 * c - 2, kT[:, 2 * c - 2, :])
                    rope(2 * c - 1, kT[:, 2 * c - 1, :])
                if c == 4:
                    ada_take(2, 0, 1)
                if c in (5, 6):
                    if c == 5:
                        dve.wait_ge(act_lo, 4)
                    ks = HALVES[c - 5]
                    link(dve.tensor_tensor(hT[:, ks, :], xT[:, ks, :], wide(rstd[:, :]), ALU.mult))
                    modulate(2, hT, ks, h_ready, hT)
                if c == 7:
                    rows_out(0)
            operand_low(3, mLo, hT, tHi)
            i0 = firsts[("wq", 0)]
            for c in range(13):
                if c < 12:
                    lows_to(min(i0 + c + PAIRS, firsts[("wo", 0)]))
                if c < 2:
                    rows_out(c + 1)
                if c == 1:
                    rows_out(3)
                    link(dve.tensor_copy(vnew[:, :, :], vraw[:, :, T:NT]))
                    dve.wait_ge(k_rows, 16 * 2)
                if c == 5:
                    dve.wait_ge(v_rows, 16 * 2)
                if c >= 1:
                    for i in (2 * c - 2, 2 * c - 1):
                        rope(KC + i, qT[:, i, :])
            dve.wait_ge(rot_summed, KC + NG * KC)
            link(dve.memset(hflat[:, 0:384], 0.0))
            link(dve.memset(hflat[:, 1156:1156 + 768], 0.0))
            for g in range(NG):
                for s in range(2):
                    q = slice(HD * s, HD * (s + 1))
                    ins = dve.tensor_tensor(kprod[q, g, :, :, s], qT[q, g * KC:(g + 1) * KC, T:NT].rearrange("p j b -> p b j"),
                                            kT[q, :, T:NT].rearrange("p j b -> p b j"), ALU.mult)
            link(ins)
            dve.sem_inc(pair_ready, 1)

            dve.wait_ge(qr_hi, 1)
            rows = slice(0, 32 * NG)
            for q in range(2):
                cols = slice(512 * q, 512 * (q + 1))
                ins = dve.tensor_tensor(q_lo[rows, cols], bank[6 + q][rows, :], q_hi[rows, cols].bitcast(F32), ALU.subtract)
            ins.then_inc(qr_taken, 1)

            def key_sums(t):
                b, g = t // NG, t % NG
                dve.wait_ge(k_halved, t + 1)
                dve.tensor_reduce(s_scores[:, g, H * b:H * (b + 1)], k_prod[t % 2].rearrange("p (h d) -> p h d", d=HD)[:, :, 0:HD // 2], X, ALU.add)\
                   .then_inc(k_summed, 1)

            for t in range(NB * NG):
                n = first[("ck", 0)] + t // 2
                dve.wait_ge(slab_in[n % RING], slab_total(n))
                dve.wait_ge(q_spread, t + 1)
                if t >= 2:
                    dve.wait_ge(k_summed, t - 1)
                for q in range(2):
                    cols = slice(512 * q, 512 * (q + 1))
                    ins = dve.tensor_tensor(k_prod[t % 2][:, cols], slab_view(n)[:, t % 2, cols], bank[2 * (t % 2) + q][:, :], ALU.mult)
                ins.then_inc(k_used, 1)
                if t >= 1:
                    key_sums(t - 1)
            key_sums(NB * NG - 1)
            dve.wait_ge(s_turned, 1)
            link(dve.tensor_scalar(s_soft[:, 0:384], bank[6][:, 0:384], SCALE, None, ALU.mult))
            link(dve.tensor_scalar(s_soft[:, 384:387], bank[5][:, 0:3], SCALE, None, ALU.mult))
            dve.tensor_reduce(s_stat[:, 0:1], s_soft, X, ALU.max, negate=True).then_inc(s_max, 1)
            dve.wait_ge(s_exp, 1)
            link(dve.reciprocal(s_stat[:, 2:3], s_stat[:, 1:2]))
            dve.tensor_scalar(s_soft, s_soft, s_stat[:, 2:3], None, ALU.mult).then_inc(s_prob, 1)
            dve.wait_ge(s_prob, 1)
            link(dve.tensor_reduce(s_stat[:, 3:4], s_soft[:, 384:387], X, ALU.add))
            dve.tensor_copy(pnewb, s_stat[:, 3:4].to_broadcast([P, P])).then_inc(pn_ready, 1)
            dve.wait_ge(sp_turned, 1)
            dve.tensor_copy(s_pT[:, :, :, 0:H], bank[7][:, 0:384].rearrange("p (g b n) -> p g b n", g=NG, b=NB)).then_inc(sp_taken, 1)
            dve.wait_ge(pn_spread, 1)
            for f in range(2):
                dve.wait_ge(cache_used, 6 * (f + 1))
                for q in range(2):
                    ins = dve.tensor_tensor(sv_own[f][:, 512 * q:512 * (q + 1)].rearrange("p (h d) -> p h d", d=HD),
                                            bank[2 * f + q][:, :].rearrange("p (h d) -> p h d", d=HD),
                                            cst("head")[:, 8 * q:8 * (q + 1)].unsqueeze(2).to_broadcast([P, 8, HD]), ALU.mult)
                ins.then_inc(sv_picked, 1)
            dve.wait_ge(sv_turned, 1)
            for s in range(2):
                q = slice(HD * s, HD * (s + 1))
                pn = bank[5][q, P:2 * P].rearrange("p (b j s) -> p j b s", b=NB, j=KC)[:, :, :, s]
                ins = dve.tensor_tensor(small[q, :, :], pn, vnew[q, :, :], ALU.mult)
            link(ins)
            link(dve.tensor_tensor(mT[:, :, T:NT], small[:, :, :], bank[4][:, 0:8 * KC].rearrange("p (k b) -> p k b", k=KC), ALU.add))
            dve.sem_inc(sv_done, 1)
            def mask_max(u):
                c = u % 2
                n = P * (c + 1)
                dve.wait_ge(a_scored, u + 1)
                if u >= 4:
                    dve.wait_ge(a_sum, u - 3)
                for q, (g0, g1) in enumerate(((0, 2), (2, 3))):
                    src = bank[2 * c + q][:, 0:256 * (g1 - g0)].rearrange("p (g k) -> p g k", k=256)[:, :, 0:n]
                    ins = dve.scalar_tensor_tensor(sm[u % 4][:, g0:g1, 0:n], src, SCALE, mask[:, g0:g1, 256 - n:256], ALU.mult, ALU.add)
                link(ins)
                dve.tensor_reduce(p_stat[:, u % 8, 0:1], sm[u % 4][:, :, 0:n], mybir.AxisListType.XY, ALU.max, negate=True).then_inc(a_max, 1)

            def head_out(u):
                h, c = u // 2, u % 2
                dve.wait_ge(a_exp, u + 1)
                link(dve.reciprocal(p_stat[:, u % 8, 2:3], p_stat[:, u % 8, 1:2]))
                dve.wait_ge(a_out, u + 1)
                dve.tensor_scalar(otok[:, c, HD * h:HD * (h + 1)], bank[6 + u % 2][:, 0:HD], p_stat[:, u % 8, 2:3], None, ALU.mult)\
                   .then_inc(a_taken, 1)

            for u in range(2 * H + 5):
                if u < 2 * H:
                    mask_max(u)
                if u >= 5:
                    head_out(u - 5)
                if u in (8, 14, 20):
                    lows_to(firsts[("wo", 0)] + (u - 2) // 6)
            for k in range(KC):
                dve.wait_ge(ot_turned, k + 1)
                dve.tensor_copy(mT[:, k, 0:T], bank[k % 2][:, 0:T]).then_inc(ot_taken, 1)
            dve.wait_ge(ot_taken, KC)
            operand_low(4, hLo, mT, tHi)
            i0 = firsts[("ada", 3)]
            lows_to(i0 + PAIRS)
            for hf in range(2):
                dve.wait_ge(wo_taken, KC // 2 * (hf + 1))
                dve.sem_inc(norm_in, 1)
            lows_to(i0 + 2 + PAIRS)
            inverse(5)
            for hf, ks in enumerate(HALVES):
                normalise(woT, ks)
                residual(2, ks, norm_in)
                lows_to(i0 + (4, 8)[hf] + PAIRS)
            inverse(6)
            for ks in HALVES:
                normalise(xT, ks)
                lows_to(NSPLIT)
            ada_take(3, 1, 1)
            for ks in HALVES:
                modulate(3, hT, ks, h_ready)
            dve.memset(mT[:, :, :], 0.0)
            dve.memset(lg, 0.0)
            dve.memset(ye, 0.0)
            link(dve.memset(comb, 0.0))
            dve.wait_ge(lg_summed, 1)
            rows = (P, P, NB)
            dve.tensor_copy(lg[:, 0:2, :], bank[0][:, 0:2 * NE].rearrange("p (q e) -> p q e", q=2))
            link(dve.tensor_copy(lg[0:NB, 2, :], bank[0][0:NB, 2 * NE:3 * NE]))
            dve.tensor_reduce(r_s[:, :, 0:1], lg[:, :, :], X, ALU.max, negate=True).then_inc(lg_max, 1)
            cube = [P, 3, NE, NE]
            mine, other = lg.unsqueeze(3).to_broadcast(cube), lg.unsqueeze(2).to_broadcast(cube)
            dve.tensor_tensor(r_a, other, mine, ALU.is_gt)
            link(dve.tensor_tensor(r_b, other, mine, ALU.is_equal))
            link(dve.tensor_tensor(r_b, r_b, tri.unsqueeze(1).to_broadcast(cube), ALU.mult))
            link(dve.tensor_tensor(r_a, r_a, r_b, ALU.add))
            link(dve.tensor_reduce(gate, r_a, X, ALU.add))
            link(dve.tensor_scalar(sel, gate, 1.5, None, ALU.is_lt))
            dve.sem_inc(sel_ready, 1)
            for k in range(KC):
                dve.wait_ge(ht_hi, k + 1)
                dve.tensor_tensor(htok_lo[:, 0:2, P * k:P * (k + 1)], bank[2 + k % 2][:, 0:256].rearrange("p (c n) -> p c n", c=2),
                                  htok_hi[:, 0:2, P * k:P * (k + 1)].bitcast(F32), ALU.subtract)
                dve.tensor_tensor(htok_lo[0:NB, 2, P * k:P * (k + 1)], bank[2 + k % 2][0:NB, 256:384],
                                  htok_hi[0:NB, 2, P * k:P * (k + 1)].bitcast(F32), ALU.subtract).then_inc(ht_taken, 1)
            dve.wait_ge(lg_exp, 1)
            link(dve.tensor_tensor(r_c, r_c, sel, ALU.mult))
            link(dve.tensor_reduce(r_s[:, :, 1:2], r_c, X, ALU.add))
            link(dve.reciprocal(r_s[:, :, 2:3], r_s[:, :, 1:2]))
            link(dve.tensor_tensor(gate, r_c, r_s[:, :, 2:3].to_broadcast([P, 3, NE]), ALU.mult))
            dve.wait_ge(pos_summed, 1)
            for q, n in enumerate(rows):
                link(dve.scalar_tensor_tensor(r_c[0:n, q, :], bank[1][0:n, NE * q:NE * (q + 1)], 1.0, sel[0:n, q, :], ALU.add, ALU.mult))
                link(dve.tensor_scalar(posm[0:n, q, :], r_c[0:n, q, :], -1.0, None, ALU.add))
            link(dve.tensor_reduce(r_s[:, 0, 3:4], bank[1][:, 3 * NE:4 * NE], X, ALU.max))
            dve.tensor_scalar(flag[:, :], r_s[:, 0, 3:4], SLOTS + 0.5, None, ALU.is_gt).then_inc(flag_ready, 1)
            dve.wait_ge(flag_ready, 1)
            dve.sem_inc(moe_ready, 1)
            dve.sem_inc(up_ready, 1)
            dve.sem_inc(y1_copied, 1)
            dve.sem_inc(comb_copied, 1)
            dve.sem_inc(upT_ready, 1)

            def route(e, c, ahead):
                if ahead or c:
                    dve.wait_ge(comb_turned, e + (c * NE + ahead))
                for q, n in enumerate(rows):
                    place = posm[0:n, q, :][:, bass.ds(e + ahead, 1)]
                    dve.tensor_scalar(disp[0:n, q, :], iota[0:n, c * SLOTS:(c + 1) * SLOTS], place, None, ALU.is_equal)
                    ins = dve.tensor_scalar(dispg[0:n, q, :], iota[0:n, c * SLOTS:(c + 1) * SLOTS], place,
                                            gate[0:n, q, :][:, bass.ds(e + ahead, 1)], ALU.is_equal, ALU.mult)
                ins.then_inc(route_built, 1)

            def low(e, c, k):
                i, slot = (NSPLIT + k) % PAIRS, (NPRE + k) % RING
                dve.wait_ge(hi_done, e * PER_E + (NSPLIT + c * NE * PER_E + k + 1))
                dve.tensor_tensor(w_lo[:, i, :], ring[:, slot, :], w_hi[:, i, :].bitcast(F32), ALU.subtract).then_inc(lo_done, 1)

            def gathered_low(e, c, ahead):
                dve.wait_ge(xe_hi_ready, e + (c * NE + ahead + 1))
                for q in range(2):
                    ins = dve.tensor_tensor(xe_lo[:, 4 * q:4 * q + 4, :], bank[q][:, :].rearrange("p (k n) -> p k n", k=4),
                                            xe_hi[:, 4 * q:4 * q + 4, :].bitcast(F32), ALU.subtract)
                ins.then_inc(xe_ready, 1)

            def add_last(e, c, blocks=range(KC)):
                for k in blocks:
                    dve.wait_ge(c_summed, e * KC + (KC * c * (NE + 1) + k + 1))
                    dve.tensor_tensor(mT[:, k, :], mT[:, k, :], bank[k % 2][:, 0:NT], ALU.add).then_inc(y_added, 1)

            def expert(e, c, last):
                def count(per, k):
                    return e * per + (c * NE * per + k)

                def turned_low(j):
                    dve.wait_ge(upT_hi_ready, count(FCH, j + 1))
                    dve.tensor_tensor(upT_lo[:, :, :], bank[5][:, :].rearrange("p (k n) -> p k n", k=4),
                                      upT_hi[:, :, :].bitcast(F32), ALU.subtract).then_inc(upT_ready, 1)

                for k, (m, j, half) in enumerate(eslabs):
                    if (m, half) in ((1, 1), (3, 1)) and j < 2:
                        q = 2 * j + (m == 3)
                        add_last(e, c, (2 * q, 2 * q + 1))
                    if k + PAIRS < PER_E or not last:
                        low(e, c, k + PAIRS)
                    if (m, j, half) == (3, 1, 1):
                        dve.wait_ge(comb_turned, count(1, 1))
                        dve.tensor_copy(comb[0:SLOTS, :], bank[2][0:SLOTS, 0:NT]).then_inc(comb_copied, 1)
                    if (m, half) == (1, 1) and j >= 1:
                        turned_low(j - 1)
                    if (m, half) == (3, 1):
                        dve.wait_ge(pair_used, used_by(e, c, 3, j))
                        dve.wait_ge(silu_done, count(FCH, j + 2))
                        dve.tensor_tensor(up[0:SLOTS, :], bank[4][0:SLOTS, :], up_s[0:SLOTS, :], ALU.mult).then_inc(up_ready, 1)
                        if j == 1 and not last:
                            route(e, c, 1)
                    if (m, j, half) == (2, FCH - 2, 1):
                        turned_low(FCH - 1)
                        if not last:
                            gathered_low(e, c, 1)
                dve.wait_ge(pair_used, used_by(e, c, 2, FCH - 1))
                dve.tensor_copy(ye[0:SLOTS, 512:1024], bank[7][0:SLOTS, :]).then_inc(y1_copied, 1)

            def experts(c):
                route(0, c, 0)
                for k in range(PAIRS):
                    low(0, c, k)
                gathered_low(0, c, 0)
                with dve.Fori(0, NE - 1) as e:
                    expert(e, c, False)
                expert(NE - 1, c, True)
                add_last(NE, c)
                dve.memset(comb, 0.0).then_inc(comb_copied, 1)

            experts(0)
            overflow = dve.value_load(flag[0:1, 0:1], min_val=0, max_val=1)
            with dve.If(overflow > 0):
                for c in range(1, PASSES):
                    experts(c)
            link(dve.tensor_copy(small[:, 0, 0:1], mT[:, 0, 0:1]))
            dve.sem_inc(norm_in, 2)
            inverse(7)
            for hf, ks in enumerate(HALVES):
                normalise(mT, ks)
                residual(3, ks, h_ready if hf else None)

        @block.gpsimd
        def _(pool):
            pool.dma_start(o["pool_sample"][:, 0, 0:STATE - 1, :], w["state_pool"][:, 0, 1:STATE, :]).then_inc(moved_up, 16)
            def remainders(k):
                for i in range(firsts[("ada", k)], firsts[("ada", k)] + 12):
                    if owner(i) == "pool":
                        remainder(pool, i, lo_done_pool)

            remainders(1)
            remainders(2)
            pool.wait_ge(kv_taken, 2)
            pool.dma_start(o["k_prompt"][0].rearrange("(c p) h d -> p c (h d)", p=P), ktok[:, 0:2, :]).then_inc(k_rows, 16)
            pool.dma_start(o["k_sample"][:, 0].rearrange("b h d -> b (h d)"), ktok[0:NB, 2, :]).then_inc(k_rows, 16)
            pool.wait_ge(kv_taken, 4)
            pool.dma_start(o["v_prompt"][0].rearrange("(c p) h d -> p c (h d)", p=P), vtok[:, 0:2, :]).then_inc(v_rows, 16)
            pool.dma_start(o["v_sample"][:, 0].rearrange("b h d -> b (h d)"), vntok).then_inc(v_rows, 16)
            pool.wait_ge(k_rows, 32)
            pool.wait_ge(v_rows, 32)
            pool.wait_ge(moved_up, 16)
            for t in range(NB * NG):
                pool.wait_ge(k_used, t + 1)
                s = k_prod[t % 2].rearrange("p (h d) -> p h d", d=HD)
                pool.tensor_tensor(s[:, :, 0:HD // 2], s[:, :, 0:HD // 2], s[:, :, HD // 2:HD], ALU.add).then_inc(k_halved, 1)
            for u in range(2 * H):
                n = P * (u % 2 + 1)
                pool.wait_ge(a_exp, u + 1)
                if u >= 2:
                    pool.wait_ge(a_turned, u - 1)
                s = sm[u % 4]
                pool.tensor_tensor(p_sum[:, u % 2, 0:n], s[:, 0, 0:n], s[:, 1, 0:n], ALU.add).then_inc(pool_step, 1)
                pool.wait_ge(pool_step, u + 1)
                pool.tensor_tensor(p_sum[:, u % 2, 0:n], p_sum[:, u % 2, 0:n], s[:, 2, 0:n], ALU.add).then_inc(a_sum, 1)
            remainders(3)


def shape_constants():
    import numpy as np
    t = np.zeros((P, NCONST), np.float32)

    def put(name, v):
        a, b = CONST[name]
        t[:, a:b] = np.asarray(v, np.float32).reshape(-1, b - a)

    p = np.arange(P)
    half = HD // 2
    inv = (10000.0 ** (-np.arange(half, dtype=np.float64) / half)).astype(np.float32)
    pos = np.concatenate([np.arange(T), np.full(NB, PAST)]).astype(np.float32)
    ang = (inv[p % half][:, None] * pos[None, :]).astype(np.float32)
    put("cos", np.cos(ang.astype(np.float64)))
    put("sin", np.sin(ang.astype(np.float64)))
    dist = (P + p)[:, None] - np.arange(T)[None, :]
    m = [np.where((dist >= 0) & (dist <= win) & (dist % dil == 0), 0.0, NEG) for win, dil in GROUPS]
    put("mask", np.stack(m, 1))
    put("cnt", np.tile(np.stack([1.0 / np.minimum(n, np.arange(16) + 1) for n in WIN])[None], (P, 1, 1)))
    put("ident", np.eye(P))
    r = np.zeros((P, P))
    for i in range(P):
        r[i + half if i % HD < half else i - half, i] = -1.0 if i % HD < half else 1.0
    put("rot", r)
    put("before", p[:, None] < p[None, :])
    put("ones", np.ones((P, P)))
    put("iota", np.tile(np.arange(SLOTS * PASSES), (P, 1)))
    e = np.arange(NE)
    put("tri", np.tile((e[None, :] < e[:, None]).reshape(1, -1), (P, 1)))
    put("eps", np.full((P, 1), EPS))
    put("slot", p[:, None] // 32 == np.arange(4)[None, :])
    put("head", p[:, None] % 32 == np.arange(H)[None, :])
    return t


_INS = ["x_prompt", "x_sample", "state_pool", "cache_k", "cache_v", "c_prompt", "c_sample", "ada_mix_w", "ada_mix_b",
        "g_pre_mix", "g_post_mix", "pool_w", "pool_scale", "g_kv", "w_kv", "w_q", "w_o", "ada_ffn_w", "ada_ffn_b",
        "g_pre_ffn", "g_post_ffn", "ffn_w1", "ffn_w3", "ffn_w2", "router_w", "router_b", "moe_w1", "moe_w3", "moe_w2"]
_OUTS = [("y_prompt", (1, T, D)), ("y_sample", (NB, 1, D)), ("pool_prompt", (1, 1, STATE, D)), ("pool_sample", (NB, 1, STATE, D)),
         ("k_prompt", (1, T, H, HD)), ("v_prompt", (1, T, H, HD)), ("k_sample", (NB, 1, H, HD)), ("v_sample", (NB, 1, H, HD))]


def kernel(**inputs):
    import numpy as np
    import concourse.bacc as bacc
    from concourse.bass_utils import run_bass_kernel_spmd

    nc = bacc.Bacc("TRN2", target_bir_lowering=False, num_devices=1)
    arrays, w, o = {}, {}, {}
    for name in _INS:
        arrays[f"in_{name}"] = np.ascontiguousarray(inputs[name])
    arrays["in_shape_constants"] = shape_constants()
    for name, a in arrays.items():
        w[name[3:]] = nc.dram_tensor(name, a.shape, F32, kind="ExternalInput").ap()
    for name, shape in _OUTS:
        o[name] = nc.dram_tensor(f"out_{name}", shape, F32, kind="ExternalOutput").ap()
    yoco_step(nc, w, o)
    r = run_bass_kernel_spmd(nc, [arrays], core_ids=[0])
    return tuple(r.results[0][f"out_{name}"] for name, _ in _OUTS)
```
